# Optimizing a Trainium2 kernel written in Bass

```python
import math
import jax, jax.numpy as jnp
from jax import lax
import numpy as np

D_MODEL = 1024
BATCH = 1
SEQ = 1024
DEPTH = 2

HEAD_DIM = 64
S5_WIDTH = D_MODEL // 2
S5_GROUP = 16
S5_GROUPS = S5_WIDTH // S5_GROUP
S5_STATE = 64
NSA_WIDTH = D_MODEL - S5_WIDTH
NSA_HEADS = NSA_WIDTH // HEAD_DIM
NSA_KV_HEADS = 2
NSA_GROUP = NSA_HEADS // NSA_KV_HEADS
NSA_KV_WIDTH = NSA_KV_HEADS * HEAD_DIM
N_BRANCH = 3
CMP_BLOCK = 32
CMP_STRIDE = 16
CMP_HIDDEN = 128
SEL_BLOCK = 64
SEL_TOPN = 8
WINDOW = 512
L0_IN = S5_WIDTH + NSA_WIDTH + 6 * NSA_KV_WIDTH + N_BRANCH * NSA_HEADS
FOX_HEADS = D_MODEL // HEAD_DIM
L1_IN = 3 * D_MODEL + FOX_HEADS
Q_BLOCK = 128
D_FF = -((-8 * D_MODEL) // (3 * 256)) * 256
ALPHA = (2 * DEPTH) ** 0.25
BETA = (8 * DEPTH) ** -0.25
LN_EPS = 1e-5
NEG = -1e30
FORCE = 1e30

kernel_name = "hybrid_s5_nsa_fox_deepnorm"

def layer_norm(x, g, b):
    xf = x.astype(jnp.float32)
    mu = jnp.mean(xf, -1, keepdims=True)
    var = jnp.mean(jnp.square(xf - mu), -1, keepdims=True)
    return ((xf - mu) * lax.rsqrt(var + LN_EPS) * g + b).astype(x.dtype)

def swiglu(x, w_gate, w_up, w_down):
    return (jax.nn.silu(x @ w_gate) * (x @ w_up)) @ w_down

def masked_softmax(logits, mask):
    p = jax.nn.softmax(jnp.where(mask, logits, NEG), axis=-1)
    return jnp.where(mask, p, 0.0)

def alibi_slopes(n_heads):
    return 2.0 ** (-8.0 * (jnp.arange(n_heads, dtype=jnp.float32) + 1.0) / n_heads)

def s5_mixer(u, lam_re, lam_im, log_step, b_re, b_im, c_re, c_im, d, w_glu):
    f32 = jnp.float32
    B, L, G, P = u.shape
    step = jnp.exp(log_step.astype(f32))[:, None]
    lr, li = lam_re.astype(f32), lam_im.astype(f32)
    mag = jnp.exp(lr * step)
    a_re, a_im = mag * jnp.cos(li * step), mag * jnp.sin(li * step)
    den = lr * lr + li * li
    nr, ni = a_re - 1.0, a_im
    z_re = (nr * lr + ni * li) / den
    z_im = (ni * lr - nr * li) / den
    br, bi = b_re.astype(f32), b_im.astype(f32)
    bb_re = z_re[..., None] * br - z_im[..., None] * bi
    bb_im = z_re[..., None] * bi + z_im[..., None] * br
    uf = u.astype(f32)
    bu_re = jnp.einsum("blgp,gnp->blgn", uf, bb_re)
    bu_im = jnp.einsum("blgp,gnp->blgn", uf, bb_im)
    ar = jnp.broadcast_to(a_re, bu_re.shape)
    ai = jnp.broadcast_to(a_im, bu_re.shape)

    def combine(e1, e2):
        a1r, a1i, b1r, b1i = e1
        a2r, a2i, b2r, b2i = e2
        return (a2r * a1r - a2i * a1i, a2r * a1i + a2i * a1r,
                a2r * b1r - a2i * b1i + b2r, a2r * b1i + a2i * b1r + b2i)

    _, _, h_re, h_im = lax.associative_scan(combine, (ar, ai, bu_re, bu_im), axis=1)
    y = (jnp.einsum("blgn,gpn->blgp", h_re, c_re.astype(f32))
         - jnp.einsum("blgn,gpn->blgp", h_im, c_im.astype(f32))
         + d.astype(f32) * uf)
    y = jax.nn.gelu(y.reshape(B, L, G * P))
    y = y * jax.nn.sigmoid(y @ w_glu.astype(f32))
    return y.astype(u.dtype)

def compress(k, pos, w1, w2):
    B, L, Hk, dh = k.shape
    nc = (L - CMP_BLOCK) // CMP_STRIDE + 1
    idx = (np.arange(nc) * CMP_STRIDE)[:, None] + np.arange(CMP_BLOCK)[None, :]
    blocks = k[:, idx] + pos[:, None, :]
    blocks = blocks.transpose(0, 1, 3, 2, 4).reshape(B, nc, Hk, CMP_BLOCK * dh)
    return jax.nn.gelu(blocks @ w1) @ w2

def cmp_sel_overlap(nc, ns):
    c0 = np.arange(nc)[:, None] * CMP_STRIDE
    s0 = np.arange(ns)[None, :] * SEL_BLOCK
    ov = np.clip(np.minimum(c0 + CMP_BLOCK, s0 + SEL_BLOCK) - np.maximum(c0, s0), 0, None)
    return (ov / CMP_BLOCK).astype(np.float32)

def nsa_attention(q, kc, vc, ks, vs, kw, vw, gates, pos_k, pos_v, phk1, phk2, phv1, phv2):
    f32 = jnp.float32
    B, L, H, dh = q.shape
    G, R = NSA_KV_HEADS, NSA_GROUP
    scale = dh ** -0.5
    slopes = alibi_slopes(H).reshape(G, R)
    kcmp = compress(kc, pos_k, phk1, phk2).astype(f32)
    vcmp = compress(vc, pos_v, phv1, phv2).astype(f32)
    nc = kcmp.shape[1]
    cmp_end = jnp.arange(nc) * CMP_STRIDE + CMP_BLOCK - 1
    ns = L // SEL_BLOCK
    n_top = min(SEL_TOPN, ns)
    overlap = jnp.asarray(cmp_sel_overlap(nc, ns))
    ks_blk = ks.reshape(B, ns, SEL_BLOCK, G, dh).transpose(0, 3, 1, 2, 4)
    vs_blk = vs.reshape(B, ns, SEL_BLOCK, G, dh).transpose(0, 3, 1, 2, 4)
    kw_pad = jnp.pad(kw, ((0, 0), (WINDOW, 0), (0, 0), (0, 0)))
    vw_pad = jnp.pad(vw, ((0, 0), (WINDOW, 0), (0, 0), (0, 0)))
    qg = q.reshape(B, L, G, R, dh)
    gate = jax.nn.sigmoid(gates.astype(f32)).reshape(B, L, G, R, N_BRANCH)
    b_ix = jnp.arange(B)[:, None, None, None]
    g_ix = jnp.arange(G)[None, :, None, None]
    blk_ids = jnp.arange(ns)
    win_off = jnp.arange(WINDOW + Q_BLOCK)

    def block(i):
        start = i * Q_BLOCK
        t = start + jnp.arange(Q_BLOCK)
        qi = lax.dynamic_slice_in_dim(qg, start, Q_BLOCK, axis=1).astype(f32) * scale
        dist_c = (t[:, None] - cmp_end[None, :]).astype(f32)
        s_c = jnp.einsum("bqgrd,bcgd->bgrqc", qi, kcmp) - slopes[:, :, None, None] * dist_c
        p_c = masked_softmax(s_c, dist_c >= 0)
        o_c = jnp.einsum("bgrqc,bcgd->bqgrd", p_c, vcmp)
        imp = jnp.einsum("bgrqc,cs->bgqs", p_c, overlap)
        cur = t // SEL_BLOCK
        forced = ((blk_ids[None, :] == 0) | (blk_ids[None, :] == cur[:, None])
                  | (blk_ids[None, :] == cur[:, None] - 1))
        valid = blk_ids[None, :] * SEL_BLOCK <= t[:, None]
        imp = jnp.where(forced, FORCE, jnp.where(valid, imp, NEG))
        _, sel = lax.top_k(imp, n_top)
        k_sel = ks_blk[b_ix, g_ix, sel].astype(f32)
        v_sel = vs_blk[b_ix, g_ix, sel].astype(f32)
        s_pos = sel[..., None] * SEL_BLOCK + jnp.arange(SEL_BLOCK)
        d_sel = (t[None, None, :, None, None] - s_pos).astype(f32)
        s_s = (jnp.einsum("bqgrd,bgqnkd->bgrqnk", qi, k_sel)
               - slopes[None, :, :, None, None, None] * d_sel[:, :, None])
        m_sel = n_top * SEL_BLOCK
        s_s = s_s.reshape(B, G, R, Q_BLOCK, m_sel)
        p_s = masked_softmax(s_s, (d_sel >= 0)[:, :, None].reshape(B, G, 1, Q_BLOCK, m_sel))
        o_s = jnp.einsum("bgrqm,bgqmd->bqgrd", p_s, v_sel.reshape(B, G, Q_BLOCK, m_sel, dh))
        kwi = lax.dynamic_slice_in_dim(kw_pad, start, WINDOW + Q_BLOCK, axis=1).astype(f32)
        vwi = lax.dynamic_slice_in_dim(vw_pad, start, WINDOW + Q_BLOCK, axis=1).astype(f32)
        spos = start - WINDOW + win_off
        d_w = t[:, None] - spos[None, :]
        m_w = (d_w >= 0) & (d_w < WINDOW) & (spos[None, :] >= 0)
        s_w = (jnp.einsum("bqgrd,bkgd->bgrqk", qi, kwi)
               - slopes[:, :, None, None] * d_w.astype(f32))
        o_w = jnp.einsum("bgrqk,bkgd->bqgrd", masked_softmax(s_w, m_w), vwi)
        gi = lax.dynamic_slice_in_dim(gate, start, Q_BLOCK, axis=1)
        o = gi[..., 0:1] * o_c + gi[..., 1:2] * o_s + gi[..., 2:3] * o_w
        return o.astype(q.dtype)

    out = lax.map(block, jnp.arange(L // Q_BLOCK))
    return out.transpose(1, 0, 2, 3, 4, 5).reshape(B, L, H * dh)

def ab_mixer(x, w_in, lam_re, lam_im, log_step, b_re, b_im, c_re, c_im, d, w_glu,
             pos_k, pos_v, phk1, phk2, phv1, phv2, w_out):
    B, L, _ = x.shape
    h = x @ w_in
    offs = np.cumsum([S5_WIDTH, NSA_WIDTH] + [NSA_KV_WIDTH] * 6).tolist()
    u, q, kc, vc, ks, vs, kw, vw, g = jnp.split(h, offs, axis=-1)
    kv = lambda a: a.reshape(B, L, NSA_KV_HEADS, HEAD_DIM)
    y_a = s5_mixer(u.reshape(B, L, S5_GROUPS, S5_GROUP), lam_re, lam_im, log_step,
                   b_re, b_im, c_re, c_im, d, w_glu)
    y_b = nsa_attention(q.reshape(B, L, NSA_HEADS, HEAD_DIM), kv(kc), kv(vc), kv(ks), kv(vs),
                        kv(kw), kv(vw), g, pos_k, pos_v, phk1, phk2, phv1, phv2)
    return jnp.concatenate([y_a, y_b.astype(y_a.dtype)], axis=-1) @ w_out

def fox_attention(q, k, v, log_f):
    f32 = jnp.float32
    B, L, H, dh = q.shape
    scale = dh ** -0.5
    c = lax.cumsum(log_f, axis=1).transpose(0, 2, 1)
    kf, vf = k.astype(f32), v.astype(f32)
    s_idx = jnp.arange(L)

    def block(i):
        start = i * Q_BLOCK
        t = start + jnp.arange(Q_BLOCK)
        qi = lax.dynamic_slice_in_dim(q, start, Q_BLOCK, axis=1).astype(f32) * scale
        ci = lax.dynamic_slice_in_dim(c, start, Q_BLOCK, axis=2)
        s = jnp.einsum("bqhd,bkhd->bhqk", qi, kf) + ci[..., None] - c[:, :, None, :]
        p = masked_softmax(s, s_idx[None, :] <= t[:, None])
        return jnp.einsum("bhqk,bkhd->bqhd", p, vf).astype(q.dtype)

    out = lax.map(block, jnp.arange(L // Q_BLOCK))
    return out.transpose(1, 0, 2, 3, 4).reshape(B, L, H * dh)

def fox_mixer(x, w_in, b_f, w_out):
    B, L, _ = x.shape
    h = x @ w_in
    q, k, v, f = jnp.split(h, [D_MODEL, 2 * D_MODEL, 3 * D_MODEL], axis=-1)
    log_f = jax.nn.log_sigmoid((f + b_f).astype(jnp.float32))
    hd = lambda a: a.reshape(B, L, FOX_HEADS, HEAD_DIM)
    o = fox_attention(hd(q), hd(k), hd(v), log_f)
    return o.astype(x.dtype) @ w_out

def setup_inputs(seed: int = 0) -> dict:
    key = jax.random.key(seed)
    keys = iter(jax.random.split(key, 40))
    f32 = jnp.float32
    nrm = lambda shape, s: jax.random.normal(next(keys), shape, f32) * s
    G, N, P = S5_GROUPS, S5_STATE, S5_GROUP
    p = {}
    p["x"] = nrm((BATCH, SEQ, D_MODEL), 1.0)
    p["l0_w_in"] = nrm((D_MODEL, L0_IN), D_MODEL ** -0.5)
    p["l0_s5_lambda_re"] = -0.5 + nrm((G, N), 0.01)
    p["l0_s5_lambda_im"] = math.pi * jnp.arange(N, dtype=f32)[None, :] + nrm((G, N), 0.01)
    p["l0_s5_log_step"] = jax.random.uniform(next(keys), (G,), f32, math.log(1e-3), math.log(1e-1))
    p["l0_s5_b_re"] = nrm((G, N, P), (2 * P) ** -0.5)
    p["l0_s5_b_im"] = nrm((G, N, P), (2 * P) ** -0.5)
    p["l0_s5_c_re"] = nrm((G, P, N), (2 * N) ** -0.5)
    p["l0_s5_c_im"] = nrm((G, P, N), (2 * N) ** -0.5)
    p["l0_s5_d"] = nrm((G, P), 1.0)
    p["l0_s5_w_glu"] = nrm((S5_WIDTH, S5_WIDTH), S5_WIDTH ** -0.5)
    p["l0_nsa_pos_k"] = nrm((CMP_BLOCK, HEAD_DIM), 0.5)
    p["l0_nsa_pos_v"] = nrm((CMP_BLOCK, HEAD_DIM), 0.5)
    p["l0_nsa_phi_k1"] = nrm((CMP_BLOCK * HEAD_DIM, CMP_HIDDEN), (CMP_BLOCK * HEAD_DIM) ** -0.5)
    p["l0_nsa_phi_k2"] = nrm((CMP_HIDDEN, HEAD_DIM), CMP_HIDDEN ** -0.5)
    p["l0_nsa_phi_v1"] = nrm((CMP_BLOCK * HEAD_DIM, CMP_HIDDEN), (CMP_BLOCK * HEAD_DIM) ** -0.5)
    p["l0_nsa_phi_v2"] = nrm((CMP_HIDDEN, HEAD_DIM), CMP_HIDDEN ** -0.5)
    p["l0_w_out"] = nrm((D_MODEL, D_MODEL), BETA * D_MODEL ** -0.5)
    p["l0_ln1_g"] = 1.0 + nrm((D_MODEL,), 0.02)
    p["l0_ln1_b"] = nrm((D_MODEL,), 0.02)
    p["l0_ffn_w_gate"] = nrm((D_MODEL, D_FF), D_MODEL ** -0.5)
    p["l0_ffn_w_up"] = nrm((D_MODEL, D_FF), D_MODEL ** -0.5)
    p["l0_ffn_w_down"] = nrm((D_FF, D_MODEL), BETA * D_FF ** -0.5)
    p["l0_ln2_g"] = 1.0 + nrm((D_MODEL,), 0.02)
    p["l0_ln2_b"] = nrm((D_MODEL,), 0.02)
    p["l1_w_in"] = nrm((D_MODEL, L1_IN), D_MODEL ** -0.5)
    p["l1_fox_b_f"] = 3.0 + nrm((FOX_HEADS,), 0.5)
    p["l1_w_out"] = nrm((D_MODEL, D_MODEL), BETA * D_MODEL ** -0.5)
    p["l1_ln1_g"] = 1.0 + nrm((D_MODEL,), 0.02)
    p["l1_ln1_b"] = nrm((D_MODEL,), 0.02)
    p["l1_ffn_w_gate"] = nrm((D_MODEL, D_FF), D_MODEL ** -0.5)
    p["l1_ffn_w_up"] = nrm((D_MODEL, D_FF), D_MODEL ** -0.5)
    p["l1_ffn_w_down"] = nrm((D_FF, D_MODEL), BETA * D_FF ** -0.5)
    p["l1_ln2_g"] = 1.0 + nrm((D_MODEL,), 0.02)
    p["l1_ln2_b"] = nrm((D_MODEL,), 0.02)
    return p

def reference(x, l0_w_in, l0_s5_lambda_re, l0_s5_lambda_im, l0_s5_log_step, l0_s5_b_re,
              l0_s5_b_im, l0_s5_c_re, l0_s5_c_im, l0_s5_d, l0_s5_w_glu, l0_nsa_pos_k,
              l0_nsa_pos_v, l0_nsa_phi_k1, l0_nsa_phi_k2, l0_nsa_phi_v1, l0_nsa_phi_v2,
              l0_w_out, l0_ln1_g, l0_ln1_b, l0_ffn_w_gate, l0_ffn_w_up, l0_ffn_w_down,
              l0_ln2_g, l0_ln2_b, l1_w_in, l1_fox_b_f, l1_w_out, l1_ln1_g, l1_ln1_b,
              l1_ffn_w_gate, l1_ffn_w_up, l1_ffn_w_down, l1_ln2_g, l1_ln2_b):
    mixer_params = (
        (l0_w_in, l0_s5_lambda_re, l0_s5_lambda_im, l0_s5_log_step, l0_s5_b_re, l0_s5_b_im,
         l0_s5_c_re, l0_s5_c_im, l0_s5_d, l0_s5_w_glu, l0_nsa_pos_k, l0_nsa_pos_v,
         l0_nsa_phi_k1, l0_nsa_phi_k2, l0_nsa_phi_v1, l0_nsa_phi_v2, l0_w_out),
        (l1_w_in, l1_fox_b_f, l1_w_out),
    )
    norm_ffn_params = (
        (l0_ln1_g, l0_ln1_b, l0_ffn_w_gate, l0_ffn_w_up, l0_ffn_w_down, l0_ln2_g, l0_ln2_b),
        (l1_ln1_g, l1_ln1_b, l1_ffn_w_gate, l1_ffn_w_up, l1_ffn_w_down, l1_ln2_g, l1_ln2_b),
    )
    for layer in range(DEPTH):
        mixer = ab_mixer if layer % 2 == 0 else fox_mixer
        ln1_g, ln1_b, w_gate, w_up, w_down, ln2_g, ln2_b = norm_ffn_params[layer]
        x = layer_norm(ALPHA * x + mixer(x, *mixer_params[layer]), ln1_g, ln1_b)
        x = layer_norm(ALPHA * x + swiglu(x, w_gate, w_up, w_down), ln2_g, ln2_b)
    return x


_drawn_inputs = setup_inputs


def setup_inputs(seed=0):
    import zlib

    import numpy as np

    out = dict(_drawn_inputs(seed))
    spreads = {}
    factors = {'l0_s5_lambda_re': 64.0,
     'l0_s5_lambda_im': 64.0,
     'l0_s5_log_step': 64.0,
     'l0_s5_b_re': 64.0,
     'l0_s5_b_im': 64.0,
     'l0_s5_c_re': 64.0,
     'l0_s5_c_im': 64.0,
     'l0_nsa_pos_k': 8.0,
     'l0_nsa_phi_k1': 4.28,
     'l0_nsa_phi_k2': 4.191,
     'l0_ln1_g': 2.764,
     'l0_ln2_g': 2.83,
     'l1_fox_b_f': 3.567,
     'l1_ln1_g': 2.687,
     'l1_ln1_b': 2.872,
     'l1_ln2_g': 8.083,
     'l1_ln2_b': 8.112,
     'l0_ln1_b': 4.395,
     'l0_ln2_b': 5.621}
    for name, (base, spread) in spreads.items():
        noise = np.random.default_rng([zlib.crc32(name.encode()), seed]).standard_normal(out[name].shape)
        drawn = base * np.exp(spread * noise) if base else spread * noise
        out[name] = __import__('jax').numpy.asarray(drawn.astype(out[name].dtype))
    for name, factor in factors.items():
        out[name] = (out[name] * factor).astype(out[name].dtype)
    return out
```

```python
from contextlib import ExitStack

import concourse.bass as bass
from concourse import mybir

F32 = mybir.dt.float32
F32R = mybir.dt.float32r
BF16 = mybir.dt.bfloat16
ALU = mybir.AluOpType
ACT = mybir.ActivationFunctionType
AX = mybir.AxisListType

P = 128
T = 1024
D = 1024
KT = D // P
NT = T // P
HALF = 512
DFF = 2816
FT = DFF // P
DEPTH = 2
ALPHA = (2 * DEPTH) ** 0.25
LN_EPS = 1e-5
KB = 1024
BASE = 17 * KB


class Mem:

    def __init__(self, nc, ctx):
        self.nc, self.sems = nc, []
        self.psum = ctx.enter_context(nc.psum_tensor("psum", [P, 8, HALF], F32))

    def at(self, name, shape, offset, dtype=F32):
        return self.nc.alloc_sbuf_tensor_at(name, shape, dtype, offset=BASE + offset)

    def sem(self, name):
        self.sems.append(self.nc.alloc_semaphore(name))
        return self.sems[-1]

    def recycle_semaphores(self):
        self.nc.all_engine_barrier()
        self.nc.clear_and_free_semaphores(self.sems)
        self.nc.all_engine_barrier()
        self.sems = []


class Chain:

    def __init__(self, eng, sem, base=0):
        self.eng, self.sem, self.base, self.n = eng, sem, base, 0

    def link(self, instruction):
        instruction.then_inc(self.sem, 1)
        self.n += 1
        self.eng.wait_ge(self.sem, self.base + self.n)


def split_passes(pe, out, w_hi, w_lo, x_hi, x_lo, first, last):
    pe.matmul(out, w_hi, x_hi, start=first, stop=False)
    pe.matmul(out, w_hi, x_lo, start=False, stop=False)
    return pe.matmul(out, w_lo, x_hi, start=False, stop=last)


def load_x(nc, mem, tag, xt_dram, x_hi, x_lo):
    raw = mem.at(f"{tag}_raw", [P, KT, T], 64 * KB)
    s_raw = [mem.sem(f"{tag}_raw_loaded{k}") for k in range(KT)]
    s_hi = mem.sem(f"{tag}_hi_ready")
    s_lo = mem.sem(f"{tag}_lo_ready")
    with nc.Block() as block:
        @block.sync
        def _(sp):
            for k in range(KT):
                sp.dma_start(raw[:, k, :], xt_dram[:, k, :]).then_inc(s_raw[k], 16)

        @block.scalar
        def _(act):
            for k in range(KT):
                act.wait_ge(s_raw[k], 16)
                nc.scalar.activation(x_hi[:, k, :], raw[:, k, :], ACT.Copy).then_inc(s_hi, 1)

        @block.vector
        def _(dve):
            for k in range(KT):
                dve.wait_ge(s_hi, k + 1)
                nc.vector.tensor_tensor(x_lo[:, k, :], raw[:, k, :], x_hi[:, k, :].bitcast(F32),
                                        ALU.subtract).then_inc(s_lo, 1)
            dve.wait_ge(s_lo, KT)


def project(nc, mem, tag, x_hi, x_lo, w_dram, n_tiles, dst, ring):
    raw = mem.at(f"{tag}_wraw", [P, 2, KT, P], ring)
    w_hi = mem.at(f"{tag}_whi", [P, 2, KT, P], ring + 8 * KB, F32R)
    w_lo = mem.at(f"{tag}_wlo", [P, 2, KT, P], ring + 16 * KB, F32R)
    ps = mem.psum
    s_raw = [mem.sem(f"{tag}_w_loaded{u}") for u in range(2)]
    s_hi = mem.sem(f"{tag}_w_hi_ready")
    s_lo = mem.sem(f"{tag}_w_lo_ready")
    s_mm = mem.sem(f"{tag}_half_done")
    s_ev = [mem.sem(f"{tag}_half{h}_out") for h in range(2)]
    n_pairs, odd = divmod(n_tiles, 2)

    with nc.Block() as block:
        @block.sync
        def _(sp):
            def load(j, u):
                sp.dma_start(raw[:, u], w_dram[2 * j + u]).then_inc(s_raw[u], 16)

            load(0, 0)
            load(0, 1)

            def next_load(j, u):
                sp.wait_ge(s_lo, 2 * j + u - 1)
                load(j, u)

            with sp.Fori(1, n_pairs, 1) as j:
                next_load(j, 0)
                next_load(j, 1)
            if odd:
                next_load(n_pairs, 0)

        @block.scalar
        def _(act):
            act.sem_inc(s_ev[0], 2)

            def split(j, u):
                act.wait_ge(s_raw[u], 16 * j + 16)
                act.wait_ge(s_mm, 4 * j + 2 * u + 2)
                nc.scalar.activation(w_hi[:, u], raw[:, u], ACT.Copy).then_inc(s_hi, 1)

            def evacuate(j, u):
                act.wait_ge(s_mm, 4 + 4 * j + 2 * u + 1)
                nc.scalar.activation(dst[:, 2 * j + u, 0:HALF], ps[:, 2 * u, :], ACT.Copy)\
                    .then_inc(s_ev[0], 1)

            split(0, 0)
            split(0, 1)
            evacuate(0, 0)
            with act.Fori(1, n_pairs, 1) as j:
                split(j, 0)
                evacuate(j - 1, 1)
                split(j, 1)
                evacuate(j, 0)
            if odd:
                split(n_pairs, 0)
            evacuate(n_pairs - 1, 1)
            if odd:
                evacuate(n_pairs, 0)

        @block.vector
        def _(dve):
            dve.sem_inc(s_ev[1], 2)

            def split(j, u):
                dve.wait_ge(s_hi, 2 * j + u + 1)
                nc.vector.tensor_tensor(w_lo[:, u], raw[:, u], w_hi[:, u].bitcast(F32),
                                        ALU.subtract).then_inc(s_lo, 1)

            def evacuate(j, u):
                dve.wait_ge(s_mm, 4 + 4 * j + 2 * u + 2)
                nc.vector.tensor_copy(dst[:, 2 * j + u, HALF:T], ps[:, 2 * u + 1, :])\
                    .then_inc(s_ev[1], 1)

            split(0, 0)
            split(0, 1)
            evacuate(0, 0)
            with dve.Fori(1, n_pairs, 1) as j:
                split(j, 0)
                evacuate(j - 1, 1)
                split(j, 1)
                evacuate(j, 0)
            if odd:
                split(n_pairs, 0)
            evacuate(n_pairs - 1, 1)
            if odd:
                evacuate(n_pairs, 0)

        @block.tensor
        def _(pe):
            pe.sem_inc(s_mm, 4)

            def tile(j, u):
                pe.wait_ge(s_lo, 2 * j + u + 1)
                for h in range(2):
                    pe.wait_ge(s_ev[h], 2 * j + u + 1)
                    cols = slice(h * HALF, (h + 1) * HALF)
                    for k in range(KT):
                        mm = split_passes(nc.tensor, ps[:, 2 * u + h, :], w_hi[:, u, k], w_lo[:, u, k],
                                          x_hi[:, k, cols], x_lo[:, k, cols], k == 0, k == KT - 1)
                    mm.then_inc(s_mm, 1)

            with pe.Fori(0, n_pairs, 1) as j:
                tile(j, 0)
                tile(j, 1)
            if odd:
                tile(n_pairs, 0)


def gate_up(nc, mem, tag, x_hi, x_lo, w_dram, hidden, ring):
    raw = mem.at(f"{tag}_wraw", [P, 2, KT, P], ring)
    w_hi = mem.at(f"{tag}_whi", [P, 2, KT, P], ring + 8 * KB, F32R)
    w_lo = mem.at(f"{tag}_wlo", [P, 2, KT, P], ring + 16 * KB, F32R)
    sg = mem.at(f"{tag}_sg", [P, 2, HALF], ring + 24 * KB)
    ps = mem.psum
    s_raw = [mem.sem(f"{tag}_w_loaded{u}") for u in range(2)]
    s_hi = mem.sem(f"{tag}_w_hi_ready")
    s_lo = mem.sem(f"{tag}_w_lo_ready")
    s_mm = mem.sem(f"{tag}_half_done")
    s_sig = mem.sem(f"{tag}_sigmoid_ready")
    s_gs = mem.sem(f"{tag}_gate_silu")
    s_h = mem.sem(f"{tag}_hidden_done")
    n_pairs = FT // 2

    with nc.Block() as block:
        @block.sync
        def _(sp):
            for gu in range(2):
                sp.dma_start(raw[:, gu], w_dram[0, gu]).then_inc(s_raw[gu], 16)
            with sp.Fori(1, FT, 1) as f:
                for gu in range(2):
                    sp.wait_ge(s_lo, 2 * f + gu - 1)
                    sp.dma_start(raw[:, gu], w_dram[f, gu]).then_inc(s_raw[gu], 16)

        @block.scalar
        def _(act):
            def split(j, fu):
                for gu in range(2):
                    act.wait_ge(s_raw[gu], 32 * j + 16 * fu + 16)
                    act.wait_ge(s_mm, 8 * j + 4 * fu + 2 * gu + 2)
                    nc.scalar.activation(w_hi[:, gu], raw[:, gu], ACT.Copy).then_inc(s_hi, 1)

            def sigmoid(j, fu):
                for h in range(2):
                    act.wait_ge(s_mm, 4 + 8 * j + 4 * fu + h + 1)
                    act.wait_ge(s_h, 4 * j + 2 * fu + h + 1)
                    nc.scalar.activation(sg[:, h, :], ps[:, 4 * fu + h, :], ACT.Sigmoid)\
                        .then_inc(s_sig, 1)

            split(0, 0)
            split(0, 1)
            sigmoid(0, 0)
            with act.Fori(1, n_pairs, 1) as j:
                split(j, 0)
                sigmoid(j - 1, 1)
                split(j, 1)
                sigmoid(j, 0)
            sigmoid(n_pairs - 1, 1)

        @block.vector
        def _(dve):
            dve.sem_inc(s_h, 2)

            def split(j, fu):
                for gu in range(2):
                    dve.wait_ge(s_hi, 4 * j + 2 * fu + gu + 1)
                    nc.vector.tensor_tensor(w_lo[:, gu], raw[:, gu], w_hi[:, gu].bitcast(F32),
                                            ALU.subtract).then_inc(s_lo, 1)

            def multiply(j, fu):
                for h in range(2):
                    dve.wait_ge(s_sig, 4 * j + 2 * fu + h + 1)
                    nc.vector.tensor_tensor(sg[:, h, :], ps[:, 4 * fu + h, :], sg[:, h, :],
                                            ALU.mult).then_inc(s_gs, 1)
                    dve.wait_ge(s_mm, 4 + 8 * j + 4 * fu + 2 + h + 1)
                    dve.wait_ge(s_gs, 4 * j + 2 * fu + h + 1)
                    nc.vector.tensor_tensor(hidden[:, 2 * j + fu, h * HALF:(h + 1) * HALF], sg[:, h, :],
                                            ps[:, 4 * fu + 2 + h, :], ALU.mult).then_inc(s_h, 1)

            split(0, 0)
            split(0, 1)
            multiply(0, 0)
            with dve.Fori(1, n_pairs, 1) as j:
                split(j, 0)
                multiply(j - 1, 1)
                split(j, 1)
                multiply(j, 0)
            multiply(n_pairs - 1, 1)

        @block.tensor
        def _(pe):
            pe.sem_inc(s_mm, 4)

            def tiles(j, fu, first):
                for gu in range(2):
                    pe.wait_ge(s_lo, 4 * j + 2 * fu + gu + 1)
                    for h in range(2):
                        if not first:
                            pe.wait_ge(s_h, 4 * j + 2 * fu + h - 1)
                        cols = slice(h * HALF, (h + 1) * HALF)
                        for k in range(KT):
                            mm = split_passes(nc.tensor, ps[:, 4 * fu + 2 * gu + h, :], w_hi[:, gu, k],
                                              w_lo[:, gu, k], x_hi[:, k, cols], x_lo[:, k, cols],
                                              k == 0, k == KT - 1)
                        mm.then_inc(s_mm, 1)

            tiles(0, 0, True)
            tiles(0, 1, True)
            with pe.Fori(1, n_pairs, 1) as j:
                tiles(j, 0, False)
                tiles(j, 1, False)


def project_norm(nc, mem, tag, src, n_k, w_dram, res_dram, gb_dram, ident, x_dram, x_hi, x_lo, ring, last):
    MT = NT // 2
    raw = mem.at(f"{tag}_wraw", [P, 2, D], ring)
    w_hi = mem.at(f"{tag}_whi", [P, 2, D], ring + 8 * KB, F32R)
    w_lo = mem.at(f"{tag}_wlo", [P, 2, D], ring + 16 * KB, F32R)
    a_hi = mem.at(f"{tag}_ahi", [P, 2, HALF], ring + 24 * KB, F32R)
    a_lo = mem.at(f"{tag}_alo", [P, 2, HALF], ring + 28 * KB, F32R)
    res = mem.at(f"{tag}_res", [P, 2, D], ring + 32 * KB)
    gb = mem.at(f"{tag}_gb", [P, 2, D], ring + 40 * KB)
    stats = mem.at(f"{tag}_stats", [P, MT, 2, 6], ring + 48 * KB)
    mv = mem.at(f"{tag}_mv", [P, MT, 2], ring + 48 * KB + 256)
    vare = mem.at(f"{tag}_vare", [P, MT], ring + 48 * KB + 320)
    std = mem.at(f"{tag}_std", [P, MT], ring + 48 * KB + 352)
    rstd = mem.at(f"{tag}_rstd", [P, MT], ring + 48 * KB + 384)
    newt = mem.at(f"{tag}_newt", [P, MT], ring + 48 * KB + 416)
    shift = mem.at(f"{tag}_shift", [P, MT], ring + 48 * KB + 448)
    ps = mem.psum
    s_raw = [mem.sem(f"{tag}_w_loaded{u}") for u in range(2)]
    s_gb = mem.sem(f"{tag}_gb_loaded")
    s_res = [mem.sem(f"{tag}_res_loaded{u}") for u in range(2)]
    s_hi = mem.sem(f"{tag}_hi_ready")
    s_lo = mem.sem(f"{tag}_lo_ready")
    s_k = mem.sem(f"{tag}_k_done")
    s_acc = mem.sem(f"{tag}_tile_summed")
    s_y = mem.sem(f"{tag}_y_ready")
    s_dve = mem.sem(f"{tag}_dve_chain")
    s_var = mem.sem(f"{tag}_var_ready")
    s_std = mem.sem(f"{tag}_std_ready")
    s_coef = mem.sem(f"{tag}_coef_ready")
    s_xn = mem.sem(f"{tag}_normed")
    s_xg = mem.sem(f"{tag}_scaled")
    s_out = mem.sem(f"{tag}_x_ready")
    s_st = mem.sem(f"{tag}_x_stored")
    s_tr = mem.sem(f"{tag}_transposed")
    s_xh = mem.sem(f"{tag}_x_hi_ready")
    s_xl = mem.sem(f"{tag}_x_lo_ready")

    def parked(m, p):
        return src[:, 2 * m:2 * m + 2, p * HALF:(p + 1) * HALF]

    def banks(m):
        return ps[:, 2 * m:2 * m + 2, :]

    with nc.Block() as block:
        @block.sync
        def _(sp):
            sp.dma_start(raw[:, 0], w_dram[0]).then_inc(s_raw[0], 16)
            sp.dma_start(raw[:, 1], w_dram[1]).then_inc(s_raw[1], 16)
            sp.dma_start(gb[:, :, :], gb_dram.partition_broadcast(P)).then_inc(s_gb, 16)
            with sp.Fori(1, n_k // 2, 1) as j:
                for u in range(2):
                    sp.wait_ge(s_lo, 2 * j + u - 1)
                    sp.dma_start(raw[:, u], w_dram[2 * j + u]).then_inc(s_raw[u], 16)
            with sp.Fori(0, n_k // 2, 1) as j:
                for u in range(2):
                    sp.wait_ge(s_lo, n_k + 2 * j + u - 1)
                    sp.dma_start(raw[:, u], w_dram[2 * j + u]).then_inc(s_raw[u], 16)

        @block.gpsimd
        def _(pool):
            def load_residual(t):
                if t >= 2:
                    pool.wait_ge(s_y, t - 1)
                pool.dma_start(res[:, t % 2], res_dram[t * P:(t + 1) * P, :]).then_inc(s_res[t % 2], 16)

            for p in range(2):
                for m in range(MT):
                    load_residual(MT * p + m)
                if p == 0:
                    pool.wait_ge(s_gb, 16)
                for m in range(MT):
                    pool.wait_ge(s_xn, MT * p + m + 1)
                    nc.gpsimd.tensor_tensor(parked(m, p), parked(m, p),
                                            gb[:, 0, :].rearrange("p (a n) -> p a n", a=2),
                                            ALU.mult).then_inc(s_xg, 1)
                for m in range(MT):
                    t = MT * p + m
                    pool.wait_ge(s_out, t + 1)
                    pool.dma_start(x_dram[t * P:(t + 1) * P, :].rearrange("t (a n) -> t a n", a=2),
                                   parked(m, p)).then_inc(s_st, 16)
            pool.wait_ge(s_st, 16 * NT)

        @block.scalar
        def _(act):
            def split(p, j, u):
                act.wait_ge(s_raw[u], 8 * n_k * p + 16 * j + 16)
                act.wait_ge(s_k, n_k * p + 2 * j + u + 1)
                nc.scalar.activation(w_hi[:, u], raw[:, u], ACT.Copy)
                nc.scalar.activation(a_hi[:, u], src[:, 2 * j + u, p * HALF:(p + 1) * HALF],
                                     ACT.Copy).then_inc(s_hi, 1)

            def normalize(p):
                act.wait_ge(s_var, p + 1)
                nc.scalar.activation(std[:, :], vare[:, :], ACT.Sqrt).then_inc(s_std, 1)
                act.wait_ge(s_coef, p + 1)
                for m in range(MT):
                    nc.scalar.activation(parked(m, p), parked(m, p), ACT.Identity,
                                         bias=shift[:, m:m + 1], scale=rstd[:, m:m + 1]).then_inc(s_xn, 1)

            with act.Fori(0, n_k // 2, 1) as j:
                split(0, j, 0)
                split(0, j, 1)
            split(1, 0, 0)
            split(1, 0, 1)
            normalize(0)
            with act.Fori(1, n_k // 2, 1) as j:
                split(1, j, 0)
                split(1, j, 1)
            normalize(1)
            if not last:
                for t in range(NT):
                    act.wait_ge(s_tr, t + 1)
                    nc.scalar.activation(x_hi[:, :, t * P:(t + 1) * P],
                                         banks(t % MT).rearrange("p a (b n) -> p (a b) n", n=P),
                                         ACT.Copy).then_inc(s_xh, 1)

        @block.vector
        def _(dve):
            chain = Chain(dve, s_dve)

            def split(p, j, u):
                dve.wait_ge(s_hi, n_k * p + 2 * j + u + 1)
                nc.vector.tensor_tensor(w_lo[:, u], raw[:, u], w_hi[:, u].bitcast(F32), ALU.subtract)
                nc.vector.tensor_tensor(a_lo[:, u], src[:, 2 * j + u, p * HALF:(p + 1) * HALF],
                                        a_hi[:, u].bitcast(F32), ALU.subtract).then_inc(s_lo, 1)

            def residual(p):
                for m in range(MT):
                    t = MT * p + m
                    dve.wait_ge(s_res[t % 2], 16 * (t // 2) + 16)
                    dve.wait_ge(s_acc, t + 1)
                    if m == 0:
                        dve.wait_ge(s_lo, n_k * (p + 1))
                    nc.vector.scalar_tensor_tensor(
                        out=parked(m, p), in0=res[:, t % 2].rearrange("p (a n) -> p a n", a=2),
                        scalar=ALPHA, in1=banks(m), op0=ALU.mult, op1=ALU.add).then_inc(s_y, 1)

            def statistics(p):
                dve.wait_ge(s_y, MT * (p + 1))
                for m in range(MT):
                    for a in range(2):
                        nc.vector.bn_stats(stats[:, m, a, :], src[:, 2 * m + a, p * HALF:(p + 1) * HALF])\
                            .then_inc(s_dve, 1)
                        chain.n += 1
                dve.wait_ge(s_dve, chain.n)
                for m in range(MT):
                    nc.vector.bn_aggr(mv[:, m, :], stats[:, m].rearrange("p a b -> p (a b)")).then_inc(s_dve, 1)
                    chain.n += 1
                dve.wait_ge(s_dve, chain.n)
                nc.vector.tensor_scalar(vare[:, :], mv[:, :, 1], LN_EPS, None, ALU.add).then_inc(s_var, 1)
                dve.wait_ge(s_std, p + 1)
                chain.link(nc.vector.reciprocal(std[:, :], std[:, :]))
                chain.link(nc.vector.tensor_tensor(newt[:, :], std[:, :], std[:, :], ALU.mult))
                chain.link(nc.vector.tensor_tensor(newt[:, :], newt[:, :], vare[:, :], ALU.mult))
                chain.link(nc.vector.tensor_scalar(newt[:, :], newt[:, :], -0.5, 1.5, ALU.mult, ALU.add))
                chain.link(nc.vector.tensor_tensor(rstd[:, :], newt[:, :], std[:, :], ALU.mult))
                nc.vector.scalar_tensor_tensor(out=shift[:, :], in0=mv[:, :, 0], scalar=-1.0,
                                               in1=rstd[:, :], op0=ALU.mult, op1=ALU.mult).then_inc(s_coef, 1)
                for m in range(MT):
                    dve.wait_ge(s_xg, MT * p + m + 1)
                    nc.vector.tensor_tensor(parked(m, p), parked(m, p),
                                            gb[:, 1, :].rearrange("p (a n) -> p a n", a=2),
                                            ALU.add).then_inc(s_out, 1)

            with dve.Fori(0, n_k // 2, 1) as j:
                split(0, j, 0)
                split(0, j, 1)
            residual(0)
            split(1, 0, 0)
            split(1, 0, 1)
            statistics(0)
            with dve.Fori(1, n_k // 2, 1) as j:
                split(1, j, 0)
                split(1, j, 1)
            residual(1)
            statistics(1)
            if not last:
                for t in range(NT):
                    dve.wait_ge(s_xh, t + 1)
                    cols = slice(t * P, (t + 1) * P)
                    nc.vector.tensor_tensor(x_lo[:, :, cols], banks(t % MT).rearrange("p a (b n) -> p (a b) n", n=P),
                                            x_hi[:, :, cols].bitcast(F32), ALU.subtract).then_inc(s_xl, 1)
                dve.wait_ge(s_xl, NT)

        @block.tensor
        def _(pe):
            pe.sem_inc(s_k, 2)

            def products(p, j, u, first, final):
                pe.wait_ge(s_lo, n_k * p + 2 * j + u + 1)
                for m in range(MT):
                    if first and p:
                        pe.wait_ge(s_y, m + 1)
                    for h in range(2):
                        mm = split_passes(nc.tensor, ps[:, 2 * m + h, :], a_hi[:, u, m * P:(m + 1) * P],
                                          a_lo[:, u, m * P:(m + 1) * P], w_hi[:, u, h * HALF:(h + 1) * HALF],
                                          w_lo[:, u, h * HALF:(h + 1) * HALF], first, final)
                    if final:
                        mm.then_inc(s_acc, 1)
                if not final:
                    mm.then_inc(s_k, 1)

            for p in range(2):
                products(p, 0, 0, True, False)
                products(p, 0, 1, False, False)
                with pe.Fori(1, n_k // 2 - 1, 1) as j:
                    products(p, j, 0, False, False)
                    products(p, j, 1, False, False)
                products(p, n_k // 2 - 1, 0, False, False)
                products(p, n_k // 2 - 1, 1, False, True)
                pe.wait_ge(s_acc, MT * (p + 1))
                pe.sem_inc(s_k, 1)
            if not last:
                for t in range(NT):
                    p, m = divmod(t, MT)
                    pe.wait_ge(s_out, t + 1)
                    if p == 0:
                        pe.wait_ge(s_y, MT + m + 1)
                    else:
                        pe.wait_ge(s_xl, m + 1)
                    for k in range(KT):
                        tr = nc.tensor.transpose(ps[:, 2 * m + k // 4, (k % 4) * P:(k % 4 + 1) * P],
                                                 src[:, 2 * m + k // 4, p * HALF + (k % 4) * P:
                                                     p * HALF + (k % 4 + 1) * P], ident[:, :])
                    tr.then_inc(s_tr, 1)


HD = 64
NEG = -1e30


def load_constants(nc, mem, ident_dram, mask_dram):
    ident = mem.at("ident", [P, P], 204 * KB)
    ident_b = mem.at("ident_bf16", [P, P], 204 * KB + 512, BF16)
    masks = mem.at("masks", [P, 2, P], 204 * KB + 768, BF16)
    wide = mem.at("mask_wide", [P, 2, P], 0)
    s_in = mem.sem("constants_loaded")
    s_cast = mem.sem("constants_cast")
    with nc.Block() as block:
        @block.sync
        def _(sp):
            sp.dma_start(ident[:, :], ident_dram).then_inc(s_in, 16)
            sp.dma_start(wide[:, :, :], mask_dram).then_inc(s_in, 16)

        @block.vector
        def _(dve):
            dve.wait_ge(s_in, 32)
            nc.vector.tensor_copy(ident_b[:, :], ident[:, :]).then_inc(s_cast, 1)
            nc.vector.tensor_copy(masks[:, :, :], wide[:, :, :]).then_inc(s_cast, 1)
            dve.wait_ge(s_cast, 2)
    return ident, ident_b, masks


def attention(nc, mem, tag, n_iter, units, stage, q_rows, keys, values, weigh, ident, ident_b, masks,
              q_st, att_dst):
    pr = mem.at(f"{tag}_p", [P, 2, T], 8 * KB)
    pt = mem.at(f"{tag}_pt", [P, 2, 2, HALF], 16 * KB)
    acc = mem.at(f"{tag}_acc", [P, NT, 2 * HD], 24 * KB)
    negmax = mem.at(f"{tag}_negmax", [P, 2], 28 * KB)
    rowmax = mem.at(f"{tag}_rowmax", [P, 2], 28 * KB + 32)
    rowsum = mem.at(f"{tag}_rowsum", [P, 2], 28 * KB + 64)
    weight = mem.at(f"{tag}_weight", [P, 2], 28 * KB + 96)
    ps = mem.psum
    s_stage = {e: mem.sem(f"{tag}_staged_{e}") for e in ("dma", "dve", "act", "pool", "values")}
    s_vt = mem.sem(f"{tag}_values_transposed")
    s_sc = mem.sem(f"{tag}_scores_ready")
    s_m1 = mem.sem(f"{tag}_rowmax_ready")
    s_mx = mem.sem(f"{tag}_negmax_ready")
    s_p = mem.sem(f"{tag}_probs_ready")
    s_t = mem.sem(f"{tag}_chunk_transposed")
    s_pt = mem.sem(f"{tag}_chunk_out")
    s_o = mem.sem(f"{tag}_product_ready")
    s_w = mem.sem(f"{tag}_weight_steps")
    s_acc = mem.sem(f"{tag}_unit_done")
    s_at = mem.sem(f"{tag}_pair_transposed")
    s_att = mem.sem(f"{tag}_pair_done")
    nu = len(units)
    chunks, n_chunks = [], 0
    for _, _, _, _, n, _ in units:
        own = []
        for first in range(0, n, 4):
            own.append((n_chunks, first, min(4, n - first)))
            n_chunks += 1
        chunks.append(own)
    assert nu % 2 == 0 and n_chunks % 2 == 0

    def scores_bank(x, c):
        return ps[:, 2 * (x % 2) + c, :]

    def scores_row(x, n):
        return ps[:, 2 * (x % 2):2 * (x % 2) + 2, :].rearrange("p a n -> p (a n)")[:, 0:n * P]

    def t_bank(cc):
        return ps[:, 4 + cc % 2, :]

    def o_bank(x):
        return ps[:, 6 + x % 2, 0:HD]

    with nc.Block() as block:
        @block.sync
        def _(sp):
            stage["once"](sp, s_stage["dma"])
            with sp.Fori(0, n_iter, 1) as j:
                sp.wait_ge(s_att, j + 1)
                stage["dma"](sp, j, s_stage["dma"])

        @block.gpsimd
        def _(pool):
            if "pool" in stage:
                with pool.Fori(0, n_iter, 1) as j:
                    pool.wait_ge(s_att, j + 1)
                    stage["pool"](pool, j, s_stage["pool"])

        @block.scalar
        def _(act):
            with act.Fori(0, n_iter, 1) as j:
                act.wait_ge(s_att, j + 1)
                stage["act"](act, j, s_stage["act"])
                if "values" in stage:
                    act.wait_ge(s_vt, j + 1)
                    stage["values"](act, s_stage["values"])

                for x in range(nu + 1):
                    if x < nu:
                        n = units[x][4]
                        act.wait_ge(s_mx, j * nu + x + 1)
                        if x >= 2:
                            act.wait_ge(s_t, j * n_chunks + chunks[x - 2][-1][0] + 1)
                            act.wait_ge(s_acc, j * nu + x - 1)
                        nc.scalar.activation(pr[:, x % 2, 0:n * P], scores_row(x, n), ACT.Exp,
                                             bias=negmax[:, x % 2:x % 2 + 1],
                                             accum_out=rowsum[:, x % 2:x % 2 + 1]).then_inc(s_p, 1)
                    if x >= 1:
                        for c, (cc, _, m) in enumerate(chunks[x - 1]):
                            act.wait_ge(s_t, j * n_chunks + cc + 1)
                            if x - 1 >= 2:
                                act.wait_ge(s_o, j * nu + x - 2)
                            nc.scalar.activation(pt[:, (x - 1) % 2, c, 0:m * P], t_bank(cc)[:, 0:m * P],
                                                 ACT.Copy).then_inc(s_pt, 1)

        @block.vector
        def _(dve):
            dve.sem_inc(s_att, 1)
            with dve.Fori(0, n_iter, 1) as j:
                dve.wait_ge(s_att, j + 1)
                stage["dve"](dve, j, s_stage["dve"])
                for x in range(nu + 2):
                    if x < nu:
                        s = slice(x % 2, x % 2 + 1)
                        dve.wait_ge(s_sc, j * nu + x + 1)
                        nc.vector.tensor_reduce(rowmax[:, s], scores_row(x, units[x][4]), AX.X, ALU.max)\
                            .then_inc(s_m1, 1)
                        dve.wait_ge(s_m1, j * nu + x + 1)
                        nc.vector.tensor_scalar(negmax[:, s], rowmax[:, s], -1.0, None, ALU.mult)\
                            .then_inc(s_mx, 1)
                    if x >= 2:
                        y = x - 2
                        s = slice(y % 2, y % 2 + 1)
                        dve.wait_ge(s_p, j * nu + y + 1)
                        weigh(dve, j, units[y], weight[:, s], rowsum[:, s], acc, o_bank(y), s_w, s_o, s_acc,
                              y, nu)
                dve.wait_ge(s_at, j + 1)
                nc.vector.tensor_copy(att_dst(j), ps[:, 0:2, :].rearrange("p a n -> p (a n)"))\
                    .then_inc(s_att, 1)

        @block.tensor
        def _(pe):
            with pe.Fori(0, n_iter, 1) as j:
                if "values" in stage:
                    pe.wait_ge(s_stage["pool"], j + 1)
                    for k in range(NT):
                        tr = nc.tensor.transpose(ps[:, 2 + k // 4, (k % 4) * P:(k % 4 + 1) * P],
                                                 stage["values_in"][:, k * P:(k + 1) * P], ident[:, :])
                    tr.then_inc(s_vt, 1)
                    pe.wait_ge(s_stage["values"], j + 1)
                pe.wait_ge(s_stage["dma"], j * stage["dma_step"] + stage["dma_first"])
                pe.wait_ge(s_stage["dve"], j * stage["dve_step"] + stage["dve_step"])
                pe.wait_ge(s_stage["act"], j * stage["act_step"] + stage["act_step"])

                for x in range(nu + 2):
                    if x < nu:
                        hh, qb, branch, kt0, n, mask = units[x]
                        if x >= 2:
                            pe.wait_ge(s_p, j * nu + x - 1)
                        lhs = q_st[0:q_rows, hh, qb * P:(qb + 1) * P]
                        for c, (_, first, m) in enumerate(chunks[x]):
                            here = {t: v for t, v in mask.items() if first <= t < first + m}
                            mm = nc.tensor.matmul(scores_bank(x, c)[:, 0:m * P], lhs,
                                                  keys(j, hh, branch, kt0 + first, m), start=True,
                                                  stop=not here)
                            for i, (t, which) in enumerate(here.items()):
                                col = (t - first) * P
                                mm = nc.tensor.matmul(scores_bank(x, c)[:, col:col + P], ident_b[:, :],
                                                      masks[:, which, :], start=False,
                                                      stop=i == len(here) - 1)
                        mm.then_inc(s_sc, 1)
                    if 1 <= x <= nu:
                        y = x - 1
                        pe.wait_ge(s_p, j * nu + y + 1)
                        for c, (cc, first, m) in enumerate(chunks[y]):
                            if cc >= 2:
                                pe.wait_ge(s_pt, j * n_chunks + cc - 1)
                            for i in range(m):
                                tr = nc.tensor.transpose(
                                    t_bank(cc)[:, i * P:(i + 1) * P],
                                    pr[:, y % 2, (first + i) * P:(first + i + 1) * P], ident[:, :])
                            tr.then_inc(s_t, 1)
                    if x >= 2:
                        y = x - 2
                        hh, qb, branch, kt0, n, mask = units[y]
                        if y >= 2:
                            pe.wait_ge(s_acc, j * nu + y - 1)
                        for c, (cc, first, m) in enumerate(chunks[y]):
                            pe.wait_ge(s_pt, j * n_chunks + cc + 1)
                            for i in range(m):
                                mm = nc.tensor.matmul(o_bank(y), pt[:, y % 2, c, i * P:(i + 1) * P],
                                                      values(j, hh, branch, kt0 + first + i),
                                                      start=first + i == 0, stop=first + i == n - 1)
                        mm.then_inc(s_o, 1)
                pe.wait_ge(s_acc, j * nu + nu)
                for k in range(NT):
                    tr = nc.tensor.transpose(ps[:, k // 4, (k % 4) * P:(k % 4 + 1) * P], acc[:, k, :],
                                             ident[:, :])
                tr.then_inc(s_at, 1)


def fox_decay(nc, mem, tag, proj, tile, bias_dram, c_dram):
    H = 16
    buf = [mem.at(f"{tag}_b{i}", [H, T], 4 * KB * i) for i in range(6)]
    z, e, u, lf, c, nc_ = buf
    ones = mem.at(f"{tag}_ones", [H, T], 24 * KB)
    b_f = mem.at(f"{tag}_bf", [H, 1], 28 * KB)
    s_in = mem.sem(f"{tag}_bias_loaded")
    s_dve = mem.sem(f"{tag}_dve_chain")
    s_act = mem.sem(f"{tag}_act_steps")
    s_out = mem.sem(f"{tag}_stored")
    with nc.Block() as block:
        @block.sync
        def _(sp):
            sp.dma_start(b_f[:, :], bias_dram).then_inc(s_in, 16)
            sp.wait_ge(s_dve, 9)
            sp.dma_start(c_dram[0], c[:, :]).then_inc(s_out, 16)
            sp.dma_start(c_dram[1], nc_[:, :]).then_inc(s_out, 16)
            sp.wait_ge(s_out, 32)

        @block.vector
        def _(dve):
            chain = Chain(dve, s_dve)
            V = nc.vector
            chain.link(V.memset(ones[:, :], 1.0))
            dve.wait_ge(s_in, 16)
            chain.link(V.tensor_scalar(z[:, :], proj[0:H, tile, :], b_f[:, 0:1], None, ALU.add))
            dve.wait_ge(s_act, 2)
            chain.link(V.tensor_scalar(u[:, :], e[:, :], 1.0, None, ALU.add))
            chain.link(V.scalar_tensor_tensor(out=e[:, :], in0=u[:, :], scalar=-1.0, in1=e[:, :],
                                              op0=ALU.add, op1=ALU.subtract))
            dve.wait_ge(s_act, 3)
            chain.link(V.tensor_tensor(lf[:, :], lf[:, :], e[:, :], ALU.subtract))
            chain.link(V.tensor_scalar(z[:, :], z[:, :], 0.0, None, ALU.min))
            chain.link(V.tensor_tensor(lf[:, :], z[:, :], lf[:, :], ALU.subtract))
            chain.link(V.tensor_tensor_scan(c[:, :], ones[:, :], lf[:, :], 0.0, ALU.mult, ALU.add))
            chain.link(V.tensor_scalar(nc_[:, :], c[:, :], -1.0, None, ALU.mult))

        @block.scalar
        def _(act):
            act.wait_ge(s_dve, 2)
            nc.scalar.activation(e[:, :], z[:, :], ACT.Abs).then_inc(s_act, 1)
            act.wait_ge(s_act, 1)
            nc.scalar.activation(e[:, :], e[:, :], ACT.Exp, scale=-1.0).then_inc(s_act, 1)
            act.wait_ge(s_dve, 3)
            nc.scalar.activation(lf[:, :], u[:, :], ACT.Ln).then_inc(s_act, 1)


def fox_attention(nc, mem, tag, proj, c_dram, one_dram, consts, att):
    ident, ident_b, masks = consts
    q_st = mem.at(f"{tag}_q", [HD + 2, 2, T], 0)
    k_st = mem.at(f"{tag}_k", [HD + 2, 2, T], 32 * KB)
    v_in = mem.at(f"{tag}_vin", [P, T], 40 * KB)
    v_st = mem.at(f"{tag}_v", [P, NT, 2 * HD], 44 * KB)
    units = [(hh, qb, 0, 0, qb + 1, {qb: 0}) for hh in range(2) for qb in range(NT)]
    ps = mem.psum

    def once(sp, s):
        sp.dma_start(q_st[HD + 1:HD + 2, :, :], one_dram).then_inc(s, 16)
        sp.dma_start(k_st[HD:HD + 1, :, :], one_dram).then_inc(s, 16)

    def dma(sp, j, s):
        pair = slice(None), bass.ds(2 * j, 2)
        sp.dma_start(q_st[HD:HD + 1, :, :], c_dram[0:1, bass.ds(2 * j, 2), :]).then_inc(s, 16)
        sp.dma_start(k_st[HD + 1:HD + 2, :, :], c_dram[1:2, bass.ds(2 * j, 2), :]).then_inc(s, 16)

    def stage_dve(dve, j, s):
        for hh in range(2):
            nc.vector.tensor_scalar(q_st[0:HD, hh, :], proj[hh * HD:(hh + 1) * HD, j, :], HD ** -0.5, None,
                                    ALU.mult).then_inc(s, 1)

    def stage_act(act, j, s):
        for hh in range(2):
            nc.scalar.activation(k_st[0:HD, hh, :], proj[hh * HD:(hh + 1) * HD, 8 + j, :], ACT.Copy)\
                .then_inc(s, 1)

    def stage_pool(pool, j, s):
        nc.gpsimd.tensor_copy(v_in[:, :], proj[:, 16 + j, :]).then_inc(s, 1)

    def values_out(act, s):
        nc.scalar.activation(v_st[:, :, :], ps[:, 2:4, :].rearrange("p a (b n) -> p (a b) n", n=P),
                             ACT.Copy).then_inc(s, 1)

    def keys(j, hh, branch, kt, m):
        return k_st[:, hh, kt * P:(kt + m) * P]

    def values(j, hh, branch, kt):
        return v_st[:, kt, hh * HD:(hh + 1) * HD]

    def weigh(dve, j, unit, w, rowsum, acc, o, s_w, s_o, s_acc, y, nu):
        hh, qb = unit[0], unit[1]
        nc.vector.reciprocal(w, rowsum).then_inc(s_w, 1)
        dve.wait_ge(s_w, j * nu + y + 1)
        dve.wait_ge(s_o, j * nu + y + 1)
        nc.vector.tensor_scalar(acc[:, qb, hh * HD:(hh + 1) * HD], o, w, None, ALU.mult).then_inc(s_acc, 1)

    stage = dict(once=once, dma=dma, dve=stage_dve, act=stage_act, pool=stage_pool, values=values_out,
                 values_in=v_in, dma_step=32, dma_first=64, dve_step=2, act_step=2)
    attention(nc, mem, tag, D // P, units, stage, HD + 2, keys, values, weigh, ident, ident_b, masks,
              q_st, lambda j: att[:, j, :])


NB = 63
NH = 8
SB = 16
TOPN = 8
FORCE = 1e30
GELU_C = 0.044715
GELU_S = 0.7978845608028654


def gelu_steps(nc, chain, act_step, x, t):
    V = nc.vector
    chain.link(V.tensor_tensor(t, x, x, ALU.mult))
    chain.link(V.tensor_scalar(t, t, GELU_C, 1.0, ALU.mult, ALU.add))
    chain.link(V.tensor_tensor(t, t, x, ALU.mult))
    act_step()
    chain.link(V.scalar_tensor_tensor(out=t, in0=t, scalar=1.0, in1=x, op0=ALU.add, op1=ALU.mult))
    chain.link(V.tensor_scalar(x, t, 0.5, None, ALU.mult))


class NsaBuffers:

    def __init__(self, mem):
        self.keys = [mem.at(f"nsa_keys{b}", [HD + 18, 2, T], (124 + 8 * b) * KB) for b in range(2)]
        self.values = mem.at("nsa_values", [P, 2, NT, 2 * HD], 140 * KB)
        self.o_cmp = mem.at("nsa_o_cmp", [P, NT, NH, HD], 148 * KB)
        self.sel_t = mem.at("nsa_sel_t", [HD + SB, 2, T], 164 * KB)
        self.gates = mem.at("nsa_gates", [P, NT, 3 * NH], 205 * KB + 512)
        self.q_cmp = mem.at("nsa_q_cmp", [HD + 2, NH, T], 30 * KB)
        self.k_cmp = mem.at("nsa_k_cmp", [HD + 2, 2, HD], 62 * KB)
        self.v_cmp = mem.at("nsa_v_cmp", [P, 2, P], 62 * KB + 512)


def nsa_prepare(nc, mem, tag, proj, d, consts, nb):
    ident, ident_b, _ = consts
    w1 = [mem.at(f"{tag}_w1k", [P, 32, P], 0), mem.at(f"{tag}_w1v", [P, 32, P], 188 * KB)]
    w2 = mem.at(f"{tag}_w2", [P, 2, HD], 16 * KB)
    pos = mem.at(f"{tag}_pos", [HD, 2, 32], 17 * KB)
    bias = mem.at(f"{tag}_bias", [P, 2], 18 * KB)
    hid = mem.at(f"{tag}_hid", [P, 2, 2, HD], 19 * KB)
    tmp = mem.at(f"{tag}_tmp", [P, 2, 2, HD], 20 * KB)
    ps = mem.psum
    s_w1 = mem.sem(f"{tag}_w1_loaded")
    s_w2 = mem.sem(f"{tag}_small_loaded")
    s_aug = mem.sem(f"{tag}_rows_loaded")
    s_gt = mem.sem(f"{tag}_gates_transposed")
    s_vt = mem.sem(f"{tag}_values_transposed")
    s_hid = mem.sem(f"{tag}_hidden_summed")
    s_bias = mem.sem(f"{tag}_bias_summed")
    s_dve = mem.sem(f"{tag}_dve_chain")
    s_pre = mem.sem(f"{tag}_tanh_arg")
    s_tanh = mem.sem(f"{tag}_tanh_ready")
    s_hr = mem.sem(f"{tag}_hidden_ready")
    s_kv = mem.sem(f"{tag}_compressed")
    s_z = mem.sem(f"{tag}_zeroed")
    s_a = mem.sem(f"{tag}_act_steps")
    s_g = mem.sem(f"{tag}_pool_steps")

    with nc.Block() as block:
        @block.sync
        def _(sp):
            for kv in range(2):
                sp.dma_start(w1[kv][:, :, :], d["nsa_w1"][kv]).then_inc(s_w1, 16)
            sp.dma_start(w2[:, :, :], d["nsa_w2"]).then_inc(s_w2, 16)
            sp.dma_start(pos[:, :, :], d["nsa_pos"]).then_inc(s_w2, 16)
            for b in range(2):
                sp.dma_start(nb.keys[b][HD:HD + 18, :, :], d["nsa_key_rows"][b]).then_inc(s_aug, 16)
            sp.dma_start(nb.k_cmp[HD:HD + 2, :, :], d["nsa_cmp_rows"]).then_inc(s_aug, 16)
            sp.dma_start(nb.q_cmp[HD:HD + 2, :, :], d["nsa_query_rows"]).then_inc(s_aug, 16)
            sp.wait_ge(s_aug, 64)

        @block.gpsimd
        def _(pool):
            nc.gpsimd.memset(nb.k_cmp[0:HD, :, :], 0.0).then_inc(s_z, 1)
            nc.gpsimd.memset(nb.v_cmp[:, :, :], 0.0).then_inc(s_z, 1)
            for b in range(2):
                nc.gpsimd.tensor_copy(nb.keys[b][0:HD, 0, :], proj[0:HD, 10 + 2 * b, :]).then_inc(s_g, 1)
            pool.wait_ge(s_g, 2)

        @block.scalar
        def _(act):
            act.wait_ge(s_gt, 1)
            nc.scalar.activation(nb.gates[:, :, :], ps[:, 0, 0:3 * NH * NT].rearrange("p (a b) -> p a b", a=NT),
                                 ACT.Sigmoid).then_inc(s_a, 1)
            for b in range(2):
                act.wait_ge(s_vt, b + 1)
                nc.scalar.activation(nb.values[:, b], ps[:, 1 + 2 * b:3 + 2 * b, :].rearrange(
                    "p a (b n) -> p (a b) n", n=P), ACT.Copy).then_inc(s_a, 1)
            for h in range(NH):
                row = (h % 2) * HD
                nc.scalar.activation(nb.q_cmp[0:HD, h, :], proj[row:row + HD, 4 + h // 2, :], ACT.Copy,
                                     scale=HD ** -0.5).then_inc(s_a, 1)
            act.wait_ge(s_pre, 1)
            nc.scalar.activation(tmp[:, :, :, 0:NB], tmp[:, :, :, 0:NB], ACT.Tanh, scale=GELU_S)\
                .then_inc(s_tanh, 1)
            act.wait_ge(s_a, 3 + NH)

        @block.vector
        def _(dve):
            V = nc.vector
            chain = Chain(dve, s_dve)
            for b in range(2):
                V.tensor_copy(nb.keys[b][0:HD, 1, :], proj[HD:P, 10 + 2 * b, :]).then_inc(s_dve, 1)
                chain.n += 1
            dve.wait_ge(s_bias, 1)
            chain.link(V.tensor_copy(bias[:, :], ps[:, 6, 0:2]))
            dve.wait_ge(s_hid, 1)
            for kv in range(2):
                for g in range(2):
                    chain.link(V.tensor_scalar(hid[:, kv, g, 0:NB], ps[:, 5 + 2 * g, kv * P:kv * P + NB],
                                               bias[:, kv:kv + 1], None, ALU.add))

            def tanh():
                dve.sem_inc(s_pre, 1)
                dve.wait_ge(s_tanh, 1)

            gelu_steps(nc, chain, tanh, hid[:, :, :, 0:NB], tmp[:, :, :, 0:NB])
            dve.sem_inc(s_hr, 1)
            dve.wait_ge(s_kv, 1)
            dve.wait_ge(s_z, 2)
            chain.link(V.tensor_copy(nb.k_cmp[0:HD, :, 0:NB], ps[0:HD, 6, P:2 * P].rearrange(
                "p (a n) -> p a n", a=2)[:, :, 0:NB]))
            for hh in range(2):
                chain.link(V.tensor_copy(nb.v_cmp[hh * HD:hh * HD + NB, :, hh * HD:(hh + 1) * HD],
                                         ps[0:NB, 0, 256:256 + 2 * HD].rearrange("p (a n) -> p a n", a=2)))

        @block.tensor
        def _(pe):
            for t in range(NT):
                tr = nc.tensor.transpose(ps[:, 0, t * 3 * NH:(t + 1) * 3 * NH],
                                         proj[0:3 * NH, 14, t * P:(t + 1) * P], ident[0:3 * NH, 0:3 * NH])
            tr.then_inc(s_gt, 1)
            for b in range(2):
                for t in range(NT):
                    tr = nc.tensor.transpose(ps[:, 1 + 2 * b + t // 4, (t % 4) * P:(t % 4 + 1) * P],
                                             proj[:, 11 + 2 * b, t * P:(t + 1) * P], ident[:, :])
                tr.then_inc(s_vt, 1)
            pe.wait_ge(s_w1, 32)
            pe.wait_ge(s_w2, 32)
            for kv in range(2):
                for r in range(32):
                    mm = nc.tensor.matmul(ps[:, 6, kv:kv + 1], w1[kv][0:HD, r, :], pos[:, kv, r:r + 1],
                                          start=r == 0, stop=r == 31)
            mm.then_inc(s_bias, 1)
            for kv in range(2):
                for g in range(2):
                    rows = slice(g * HD, (g + 1) * HD)
                    for r in range(32):
                        mm = nc.tensor.matmul(ps[:, 5 + 2 * g, kv * P:kv * P + NB],
                                              w1[kv][rows, r, :],
                                              proj[rows, 8 + kv, r:r + 16 * (NB - 1) + 1:16],
                                              start=r == 0, stop=r == 31)
            mm.then_inc(s_hid, 1)
            pe.wait_ge(s_hr, 1)
            pe.wait_ge(s_a, 1)
            for g in range(2):
                nc.tensor.matmul(ps[0:HD, 6, P + g * HD:P + g * HD + NB], w2[:, 0, :], hid[:, 0, g, 0:NB],
                                 start=True, stop=True)
            for g in range(2):
                mm = nc.tensor.matmul(ps[0:NB, 0, 256 + g * HD:256 + (g + 1) * HD], hid[:, 1, g, 0:NB],
                                      w2[:, 1, :], start=True, stop=True)
            mm.then_inc(s_kv, 1)


def nsa_compressed(nc, mem, tag, d, consts, nb):
    ident, ident_b, _ = consts
    maskw = mem.at(f"{tag}_maskw", [P, NT, HD], 0)
    keep = mem.at(f"{tag}_keep", [P, NT, HD], 2 * KB)
    maskb = mem.at(f"{tag}_maskb", [P, NT, HD], 4 * KB, BF16)
    selm = mem.at(f"{tag}_selm", [P, 2, NT, SB], 5 * KB)
    lower = mem.at(f"{tag}_lower", [P, SB, SB], 6 * KB)
    over = mem.at(f"{tag}_overlap", [P, SB], 7 * KB)
    e = mem.at(f"{tag}_e", [P, 2, NH, HD], 8 * KB)
    p_t = mem.at(f"{tag}_pt", [P, 2, 4, P], 12 * KB)
    gt = mem.at(f"{tag}_gt", [P, 2, SB, SB], 16 * KB)
    eq = mem.at(f"{tag}_eq", [P, 2, SB, SB], 18 * KB)
    imp = mem.at(f"{tag}_imp", [P, 2, SB], 20 * KB)
    rank = mem.at(f"{tag}_rank", [P, 2, SB], 20 * KB + 128)
    selb = mem.at(f"{tag}_selb", [P, 2, SB], 20 * KB + 256)
    mx = mem.at(f"{tag}_mx", [P, NH], 20 * KB + 384)
    sm = mem.at(f"{tag}_sm", [P, NH], 20 * KB + 416)
    ps = mem.psum
    s_in = mem.sem(f"{tag}_constants_loaded")
    s_dve = mem.sem(f"{tag}_dve_chain")
    s_mask = mem.sem(f"{tag}_mask_ready")
    s_sc = mem.sem(f"{tag}_scores_ready")
    s_sub = mem.sem(f"{tag}_shifted")
    s_exp = mem.sem(f"{tag}_exp_ready")
    s_pr = mem.sem(f"{tag}_probs_ready")
    s_tr = mem.sem(f"{tag}_transposed")
    s_pt = mem.sem(f"{tag}_transposes_out")
    s_o = mem.sem(f"{tag}_products_ready")
    s_sb = mem.sem(f"{tag}_choice_ready")
    s_st = mem.sem(f"{tag}_choice_transposed")
    s_end = mem.sem(f"{tag}_block_done")

    with nc.Block() as block:
        @block.sync
        def _(sp):
            for dst, name in ((maskw, "cmp_mask"), (keep, "cmp_keep"), (selm, "sel_mul_add"),
                              (lower, "lower"), (over, "overlap")):
                src = d[name]
                sp.dma_start(dst[:], src).then_inc(s_in, 16)

        @block.scalar
        def _(act):
            for q in range(NT):
                b = q % 2
                act.wait_ge(s_sub, q + 1)
                nc.scalar.activation(e[:, b], e[:, b], ACT.Exp).then_inc(s_exp, 1)
                act.wait_ge(s_tr, q + 1)
                nc.scalar.activation(p_t[:, b], ps[:, 2 + b, :].rearrange("p (a n) -> p a n", a=4),
                                     ACT.Copy).then_inc(s_pt, 1)

        @block.vector
        def _(dve):
            V = nc.vector
            chain = Chain(dve, s_dve)
            dve.wait_ge(s_in, 80)
            V.tensor_copy(maskb[:, :, :], maskw[:, :, :]).then_inc(s_mask, 1)
            for q in range(NT):
                b = q % 2
                scores = ps[:, b, :].rearrange("p (h n) -> p h n", h=NH)
                dve.wait_ge(s_sc, q + 1)
                chain.link(V.tensor_reduce(mx[:, :], scores, AX.X, ALU.max))
                V.tensor_tensor(e[:, b], scores, mx[:, :].unsqueeze(2).broadcast_to([P, NH, HD]),
                                ALU.subtract).then_inc(s_sub, 1)
                dve.wait_ge(s_exp, q + 1)
                chain.link(V.tensor_reduce(sm[:, :], e[:, b], AX.X, ALU.add))
                chain.link(V.reciprocal(sm[:, :], sm[:, :]))
                chain.link(V.tensor_tensor(e[:, b], e[:, b], sm[:, :].unsqueeze(2).broadcast_to([P, NH, HD]),
                                           ALU.mult))
                V.tensor_tensor(e[:, b], e[:, b], keep[:, q, :].unsqueeze(1).broadcast_to([P, NH, HD]),
                                ALU.mult).then_inc(s_pr, 1)
                dve.wait_ge(s_o, q + 1)
                chain.link(V.tensor_tensor(
                    imp[:, :, :], ps[:, 6 + b, 0:2 * SB].rearrange("p (g s) -> p g s", g=2),
                    selm[:, 0, q, :].unsqueeze(1).broadcast_to([P, 2, SB]), ALU.mult))
                chain.link(V.tensor_tensor(imp[:, :, :], imp[:, :, :],
                                           selm[:, 1, q, :].unsqueeze(1).broadcast_to([P, 2, SB]), ALU.add))
                for g in range(2):
                    other = imp[:, g, :].unsqueeze(1).broadcast_to([P, SB, SB])
                    own = imp[:, g, :].unsqueeze(2).broadcast_to([P, SB, SB])
                    V.tensor_tensor(gt[:, g], other, own, ALU.is_gt).then_inc(s_dve, 1)
                    V.tensor_tensor(eq[:, g], other, own, ALU.is_equal).then_inc(s_dve, 1)
                    chain.n += 2
                dve.wait_ge(s_dve, chain.n)
                chain.link(V.tensor_tensor(eq[:, :, :, :], eq[:, :, :, :],
                                           lower[:, :, :].unsqueeze(1).broadcast_to([P, 2, SB, SB]), ALU.mult))
                chain.link(V.tensor_tensor(gt[:, :, :, :], gt[:, :, :, :], eq[:, :, :, :], ALU.add))
                chain.link(V.tensor_reduce(rank[:, :, :], gt[:, :, :, :], AX.X, ALU.add))
                V.tensor_scalar(selb[:, :, :], rank[:, :, :], float(TOPN), NEG, ALU.is_ge, ALU.mult)\
                    .then_inc(s_sb, 1)
                V.tensor_tensor(nb.o_cmp[:, q], ps[:, 4 + b, :].rearrange("p (h n) -> p h n", h=NH),
                                nb.gates[:, q, 0:3 * NH:3].unsqueeze(2).broadcast_to([P, NH, HD]),
                                ALU.mult).then_inc(s_dve, 1)
                chain.n += 1
                dve.wait_ge(s_st, q + 1)
                V.tensor_copy(nb.sel_t[HD:HD + SB, :, q * P:(q + 1) * P],
                              ps[0:SB, 6 + b, P:3 * P].rearrange("p (g n) -> p g n", g=2)).then_inc(s_end, 1)

        @block.tensor
        def _(pe):
            def scores(q):
                b = q % 2
                bank = ps[:, b, :].rearrange("p (h n) -> p h n", h=NH)
                if q >= 2:
                    pe.wait_ge(s_sub, q - 1)
                nc.tensor.matmul(bank, ident_b[:, :], maskb[:, q, :].unsqueeze(1).broadcast_to([P, NH, HD]),
                                 start=True, stop=True)
                for h in range(NH):
                    mm = nc.tensor.matmul(bank[:, h, :], nb.q_cmp[:, h, q * P:(q + 1) * P],
                                          nb.k_cmp[:, h // 4, :], start=False, stop=True,
                                          skip_group_check=True)
                mm.then_inc(s_sc, 1)

            pe.wait_ge(s_mask, 1)
            scores(0)
            for q in range(NT):
                b = q % 2
                if q + 1 < NT:
                    scores(q + 1)
                pe.wait_ge(s_pr, q + 1)
                if q >= 2:
                    pe.wait_ge(s_pt, q - 1)
                for k in range(4):
                    tr = nc.tensor.transpose(ps[:, 2 + b, k * P:(k + 1) * P],
                                             e[:, b, 2 * k:2 * k + 2, :].rearrange("p h n -> p (h n)"),
                                             ident[:, :])
                tr.then_inc(s_tr, 1)
                pe.wait_ge(s_pt, q + 1)
                if q >= 2:
                    pe.wait_ge(s_end, q - 1)
                for k in range(4):
                    nc.tensor.matmul(ps[:, 4 + b, k * P:(k + 1) * P], p_t[:, b, k, :], nb.v_cmp[:, k // 2, :],
                                     start=True, stop=True)
                for k in range(4):
                    mm = nc.tensor.matmul(ps[:, 6 + b, (k // 2) * SB:(k // 2 + 1) * SB], p_t[:, b, k, :],
                                          over[:, :], start=k % 2 == 0, stop=k % 2 == 1)
                mm.then_inc(s_o, 1)
                pe.wait_ge(s_sb, q + 1)
                for g in range(2):
                    tr = nc.tensor.transpose(ps[0:SB, 6 + b, (1 + g) * P:(2 + g) * P], selb[:, g, :],
                                             ident[:, :])
                tr.then_inc(s_st, 1)


def nsa_attention(nc, mem, tag, proj, d, consts, nb, att):
    ident, ident_b, masks = consts
    q_st = mem.at(f"{tag}_q", [HD + 18, 2, T], 0)
    WT = 512 // P
    units = []
    for hh in range(2):
        for qb in range(NT):
            units.append((hh, qb, 0, 0, qb + 1, {qb: 0}))
            kt0 = max(0, qb - WT)
            far = {0: 1} if qb >= WT else {}
            units.append((hh, qb, 1, kt0, qb + 1 - kt0, {**far, qb - kt0: 0}))

    def once(sp, s):
        pass

    def dma(sp, j, s):
        sp.dma_start(q_st[HD + SB:HD + 18, :, :], d["nsa_query_rows"][:, bass.ds(2 * j, 2), :]).then_inc(s, 16)

    def stage_dve(dve, j, s):
        nc.vector.tensor_scalar(q_st[0:HD, 0, :], proj[0:HD, 4 + j, :], HD ** -0.5, None, ALU.mult)\
            .then_inc(s, 1)
        nc.vector.tensor_copy(q_st[HD:HD + SB, 0, :], nb.sel_t[HD:HD + SB, j // 2, :]).then_inc(s, 1)

    def stage_act(act, j, s):
        nc.scalar.activation(q_st[0:HD, 1, :], proj[HD:P, 4 + j, :], ACT.Copy, scale=HD ** -0.5)\
            .then_inc(s, 1)
        nc.scalar.activation(q_st[HD:HD + SB, 1, :], nb.sel_t[HD:HD + SB, j // 2, :], ACT.Copy).then_inc(s, 1)

    def keys(j, hh, branch, kt, m):
        return nb.keys[branch][:, j // 2, kt * P:(kt + m) * P]

    def values(j, hh, branch, kt):
        return nb.values[:, branch, kt, bass.ds((j // 2) * HD, HD)]

    def weigh(dve, j, unit, w, rowsum, acc, o, s_w, s_o, s_acc, y, nu):
        hh, qb, branch = unit[0], unit[1], unit[2]
        step = 2 * (j * nu + y)
        nc.vector.reciprocal(w, rowsum).then_inc(s_w, 1)
        dve.wait_ge(s_w, step + 1)
        nc.vector.tensor_tensor(w, w, nb.gates[:, qb, bass.ds(6 * j + 3 * hh + 1 + branch, 1)], ALU.mult)\
            .then_inc(s_w, 1)
        dve.wait_ge(s_w, step + 2)
        dve.wait_ge(s_o, j * nu + y + 1)
        own = acc[:, qb, hh * HD:(hh + 1) * HD]
        if branch == 0:
            before = nb.o_cmp[:, qb, bass.ds(2 * j + hh, 1), :].rearrange("p a n -> p (a n)")
        else:
            before = own
            dve.wait_ge(s_acc, j * nu + y)
        nc.vector.scalar_tensor_tensor(out=own, in0=o, scalar=w, in1=before, op0=ALU.mult, op1=ALU.add)\
            .then_inc(s_acc, 1)

    stage = dict(once=once, dma=dma, dve=stage_dve, act=stage_act, dma_step=16, dma_first=16, dve_step=2,
                 act_step=2)
    attention(nc, mem, tag, NH // 2, units, stage, HD + 18, keys, values, weigh, ident, ident_b, masks,
              q_st, lambda j: att[:, 4 + j, :])


def shape_constants(np):
    q = np.arange(P)
    t = np.arange(T, dtype=np.float32)
    masks = np.stack([np.where(q[None] <= q[:, None], 0, NEG), np.where(q[None] > q[:, None], 0, NEG)], 1)
    slopes = np.float32(2.0) ** (-8.0 * np.arange(1, NH + 1, dtype=np.float32) / NH)
    query_rows = np.stack([-slopes[:, None] * t[None], np.repeat(slopes[:, None], T, 1)])
    one = np.ones((1, 2, T))
    block = (np.arange(T)[None] // HD == np.arange(SB)[:, None])
    key_rows = np.zeros((2, 18, 2, T))
    key_rows[0, 0:SB] = block[:, None]
    key_rows[:, SB] = 1
    key_rows[:, SB + 1] = t
    end = np.arange(NB) * 16 + 31
    cmp_rows = np.zeros((2, 2, HD))
    cmp_rows[0, :, 0:NB] = 1
    cmp_rows[1, :, 0:NB] = end
    tok = (np.arange(NT)[None, :] * P + q[:, None])[:, :, None]
    keep = np.zeros((P, NT, HD))
    keep[:, :, 0:NB] = end[None, None] <= tok
    blk = np.arange(SB)[None, None]
    cur = tok // HD
    forced = (blk == 0) | (blk == cur) | (blk == cur - 1)
    valid = blk * HD <= tok
    sel_mul = (~forced & valid)
    sel_add = np.where(forced, FORCE, np.where(valid, 0, NEG))
    lower = np.broadcast_to(q[None, None, 0:SB] < q[None, 0:SB, None], (P, SB, SB))
    c0, s0 = (np.arange(NB) * 16)[:, None], (np.arange(SB) * HD)[None]
    ov = np.zeros((2, HD, SB))
    ov[:, 0:NB] = np.clip(np.minimum(c0 + 32, s0 + HD) - np.maximum(c0, s0), 0, None) / 32
    out = dict(ident=np.eye(P), masks=masks, nsa_query_rows=query_rows, one=one, nsa_key_rows=key_rows,
               nsa_cmp_rows=cmp_rows, cmp_mask=np.where(keep > 0, 0, NEG), cmp_keep=keep,
               sel_mul_add=np.stack([sel_mul, sel_add], 1), lower=lower, overlap=ov.reshape(P, SB))
    return {k: np.ascontiguousarray(v, dtype=np.float32) for k, v in out.items()}


CL = 4
NCH = T // CL
NP = 16
CH = 32
INV_2PI = 0.15915494309189535
PI2_HI, PI2_MID, PI2_LO = 6.28125, 1.93500518798828125e-3, 3.0199159819567e-7
ROUND = 12582912.0
PI_F = 3.1415925
HALF_PI = 1.5707963267948966


class S5Buffers:
    def __init__(self, mem):
        self.rot = mem.at("s5_rot", [P, 2, NP, NCH], 0)
        self.ca = mem.at("s5_ca", [P, 2, NP, CL + 1, CH], 32 * KB)
        self.m4 = mem.at("s5_m4", [P, NP], 52 * KB)
        self.wb = mem.at("s5_wb", [P, 2, NP, P], 124 * KB)
        self.wt = mem.at("s5_wt", [P, NP, P], 140 * KB)
        self.u = mem.at("s5_u", [P, NP, NCH], 164 * KB + 256)


def s5_weights(nc, mem, tag, proj, d, consts, sb):
    ident = consts[0]
    small = mem.at(f"{tag}_small", [P, 30, NP], 52 * KB + 64)
    names = iter(range(30))

    def reg():
        i = next(names)
        return small[:, i, :]

    lr, li, step, mag, th, r0, r1, cos, sin, a_re, a_im, den, nr, z_re, z_im, t0, t1, t2 = (
        reg() for _ in range(18))
    w_re, w_im = [reg(), reg()], [reg(), reg()]
    braw = mem.at(f"{tag}_braw", [P, 2, NP, CH], 56 * KB)
    tmp = mem.at(f"{tag}_tmp", [P, 2, NP, CH], 60 * KB)
    ba = mem.at(f"{tag}_ba", [P, 2, NP, CL, CH], 148 * KB)
    u_sh = mem.at(f"{tag}_ush", [P, 4, CL, NCH], 181 * KB)
    ptmp = mem.at(f"{tag}_ptmp", [P, NP, NCH // 2], 197 * KB - 512)
    ptmp = [mem.at(f"{tag}_ptmp0", [P, 8, NCH // 2], 197 * KB)]
    ps = mem.psum
    s_par = mem.sem(f"{tag}_parameters_loaded")
    s_b = mem.sem(f"{tag}_bc_loaded")
    s_v = mem.sem(f"{tag}_dve_chain")
    s_a = mem.sem(f"{tag}_act_steps")
    s_ph = mem.sem(f"{tag}_angles_ready")
    s_w = mem.sem(f"{tag}_rotation_ready")
    s_g = mem.sem(f"{tag}_pool_chain")
    s_sh = mem.sem(f"{tag}_u_reordered")
    s_u = mem.sem(f"{tag}_u_laid_out")
    s_ba = mem.sem(f"{tag}_ba_ready")
    s_ca = mem.sem(f"{tag}_ca_ready")
    s_tb = mem.sem(f"{tag}_b_transposed")
    s_wb = mem.sem(f"{tag}_wb_out")
    s_tt = mem.sem(f"{tag}_toeplitz_summed")
    s_wt = mem.sem(f"{tag}_wt_out")
    s_z = mem.sem(f"{tag}_wt_cleared")

    with nc.Block() as block:
        @block.sync
        def _(sp):
            sp.dma_start(lr, d["s5_lr"]).then_inc(s_par, 16)
            sp.dma_start(li, d["s5_li"]).then_inc(s_par, 16)
            for g in range(2):
                sp.dma_start(step[g * HD:(g + 1) * HD, :], d["s5_ls"][g].partition_broadcast(HD))\
                    .then_inc(s_par, 16)
            sp.dma_start(braw[:, 0], d["s5_b"][0]).then_inc(s_b, 16)
            sp.dma_start(braw[:, 1], d["s5_b"][1]).then_inc(s_b, 16)
            for ri in range(2):
                sp.dma_start(sb.ca[:, ri, :, 0, :], d["s5_c"][ri]).then_inc(s_b, 16)
            sp.wait_ge(s_sh, 4)
            for i in range(CL):
                for q in range(4):
                    sp.dma_start(sb.u[i * CH:(i + 1) * CH, q:NP:4, :],
                                 u_sh[q * CH:(q + 1) * CH, :, i, :]).then_inc(s_u, 16)
            sp.wait_ge(s_u, 16 * CL * 4)

        @block.scalar
        def _(act):
            act.wait_ge(s_par, 64)
            A = nc.scalar.activation

            def one(out, in_, func, **kw):
                A(out, in_, func, **kw).then_inc(s_a, 1)

            one(step, step, ACT.Exp)
            act.wait_ge(s_v, 1)
            one(mag, t0, ACT.Exp)
            act.wait_ge(s_ph, 1)
            one(sin, r0, ACT.Sin)
            one(cos, r1, ACT.Sin)
            for o in range(4):
                nc.scalar.activation(u_sh[:, o], proj[:, o, :].rearrange("p (c i) -> p i c", i=CL), ACT.Copy)\
                    .then_inc(s_sh, 1)
            for n in range(8):
                act.wait_ge(s_tb, n + 1)
                nc.scalar.activation(sb.wb[:, n // 4, 4 * (n % 4):4 * (n % 4) + 4, :],
                                     ps[:, n % 4, :].rearrange("p (a n) -> p a n", a=4), ACT.Copy)\
                    .then_inc(s_wb, 1)
            act.wait_ge(s_z, 1)
            for b in range(4):
                act.wait_ge(s_tt, b + 1)
                for i in range(CL):
                    rows = slice(i * CH, (i + 1) * CH)
                    nc.scalar.activation(sb.wt[rows, 4 * b:4 * b + 4, i * CH:P],
                                         ps[rows, 4 + b, :].rearrange("p (a n) -> p a n", a=4)[:, :, i * CH:P],
                                         ACT.Copy).then_inc(s_wt, 1)
            act.wait_ge(s_wt, 16)

        @block.gpsimd
        def _(pool):
            G = nc.gpsimd
            chain = Chain(pool, s_g)
            G.memset(sb.wt[:, :, :], 0.0).then_inc(s_z, 1)
            rr, ri = sb.rot[:, 0], sb.rot[:, 1]
            chain.link(G.memset(rr[:, :, 0:1], 1.0))
            chain.link(G.memset(ri[:, :, 0:1], 0.0))
            pool.wait_ge(s_w, 1)
            n, cur = 1, 0
            while n < NCH:
                for h in range(2):
                    pr = slice(8 * h, 8 * h + 8)
                    wr = w_re[cur][:, pr].unsqueeze(2).broadcast_to([P, 8, n])
                    wi = w_im[cur][:, pr].unsqueeze(2).broadcast_to([P, 8, n])
                    old_r, old_i = rr[:, pr, 0:n], ri[:, pr, 0:n]
                    new_r, new_i = rr[:, pr, n:2 * n], ri[:, pr, n:2 * n]
                    t = ptmp[0][:, :, 0:n]
                    chain.link(G.tensor_tensor(new_r, old_r, wr, ALU.mult))
                    chain.link(G.tensor_tensor(t, old_i, wi, ALU.mult))
                    chain.link(G.tensor_tensor(new_r, new_r, t, ALU.subtract))
                    chain.link(G.tensor_tensor(new_i, old_r, wi, ALU.mult))
                    chain.link(G.tensor_tensor(t, old_i, wr, ALU.mult))
                    chain.link(G.tensor_tensor(new_i, new_i, t, ALU.add))
                n *= 2
                nxt = 1 - cur
                t = ptmp[0][:, 0, 0:NP]
                chain.link(G.tensor_tensor(w_re[nxt], w_re[cur], w_re[cur], ALU.mult))
                chain.link(G.tensor_tensor(t, w_im[cur], w_im[cur], ALU.mult))
                chain.link(G.tensor_tensor(w_re[nxt], w_re[nxt], t, ALU.subtract))
                chain.link(G.tensor_tensor(w_im[nxt], w_re[cur], w_im[cur], ALU.mult))
                chain.link(G.tensor_tensor(w_im[nxt], w_im[nxt], w_im[nxt], ALU.add))
                cur = nxt

        @block.vector
        def _(dve):
            V = nc.vector
            chain = Chain(dve, s_v)
            TT, TS = V.tensor_tensor, V.tensor_scalar
            dve.wait_ge(s_par, 64)
            dve.wait_ge(s_a, 1)
            chain.link(TT(t0, lr, step, ALU.mult))
            chain.link(TT(th, li, step, ALU.mult))
            chain.link(TS(t1, th, INV_2PI, ROUND, ALU.mult, ALU.add))
            chain.link(TS(t1, t1, -ROUND, None, ALU.add))
            chain.link(V.scalar_tensor_tensor(out=r0, in0=t1, scalar=-PI2_HI, in1=th, op0=ALU.mult, op1=ALU.add))
            chain.link(V.scalar_tensor_tensor(out=r0, in0=t1, scalar=-PI2_MID, in1=r0, op0=ALU.mult, op1=ALU.add))
            chain.link(V.scalar_tensor_tensor(out=r0, in0=t1, scalar=-PI2_LO, in1=r0, op0=ALU.mult, op1=ALU.add))
            chain.link(TS(r0, r0, PI_F, -PI_F, ALU.min, ALU.max))
            chain.link(TS(r1, r0, -1.0, None, ALU.mult))
            chain.link(TT(r1, r1, r0, ALU.max))
            TS(r1, r1, -1.0, HALF_PI, ALU.mult, ALU.add).then_inc(s_ph, 1)
            dve.wait_ge(s_a, 4)
            chain.link(TT(a_re, mag, cos, ALU.mult))
            chain.link(TT(a_im, mag, sin, ALU.mult))
            chain.link(TT(t0, cos, cos, ALU.mult))
            chain.link(TT(t1, sin, sin, ALU.mult))
            chain.link(TT(t2, cos, sin, ALU.mult))
            chain.link(TT(t0, t0, t1, ALU.subtract))
            chain.link(TT(t2, t2, t2, ALU.add))
            chain.link(TT(t1, t2, t2, ALU.mult))
            chain.link(TT(w_re[0], t0, t0, ALU.mult))
            chain.link(TT(w_re[0], w_re[0], t1, ALU.subtract))
            chain.link(TT(w_im[0], t0, t2, ALU.mult))
            TT(w_im[0], w_im[0], w_im[0], ALU.add).then_inc(s_w, 1)
            chain.link(TT(t0, mag, mag, ALU.mult))
            chain.link(TT(sb.m4[:, :], t0, t0, ALU.mult))
            chain.link(TT(den, lr, lr, ALU.mult))
            chain.link(TT(t0, li, li, ALU.mult))
            chain.link(TT(den, den, t0, ALU.add))
            chain.link(V.reciprocal(den, den))
            chain.link(TS(nr, a_re, -1.0, None, ALU.add))
            chain.link(TT(t0, nr, lr, ALU.mult))
            chain.link(TT(t1, a_im, li, ALU.mult))
            chain.link(TT(t0, t0, t1, ALU.add))
            chain.link(TT(z_re, t0, den, ALU.mult))
            chain.link(TT(t0, a_im, lr, ALU.mult))
            chain.link(TT(t1, nr, li, ALU.mult))
            chain.link(TT(t0, t0, t1, ALU.subtract))
            chain.link(TT(z_im, t0, den, ALU.mult))

            def wide(x):
                return x.unsqueeze(2).broadcast_to([P, NP, CH])

            def times(out_r, out_i, in_r, in_i, m_r, m_i, sign):
                chain.link(TT(tmp[:, 0], in_i, wide(m_i), ALU.mult))
                chain.link(TT(tmp[:, 1], in_r, wide(m_i), ALU.mult))
                chain.link(TT(out_r, in_r, wide(m_r), ALU.mult))
                chain.link(TT(out_i, in_i, wide(m_r), ALU.mult))
                chain.link(TT(out_r, out_r, tmp[:, 0], ALU.subtract if sign > 0 else ALU.add))
                chain.link(TT(out_i, out_i, tmp[:, 1], ALU.add if sign > 0 else ALU.subtract))

            dve.wait_ge(s_b, 64)
            times(ba[:, 0, :, CL - 1], ba[:, 1, :, CL - 1], braw[:, 0], braw[:, 1], z_re, z_im, 1)
            for i in range(CL - 2, -1, -1):
                times(ba[:, 0, :, i], ba[:, 1, :, i], ba[:, 0, :, i + 1], ba[:, 1, :, i + 1], a_re, a_im, 1)
            dve.sem_inc(s_ba, 1)
            chain.link(TS(sb.ca[:, 1, :, 0, :], sb.ca[:, 1, :, 0, :], -1.0, None, ALU.mult))
            for j in range(1, CL + 1):
                times(sb.ca[:, 0, :, j], sb.ca[:, 1, :, j], sb.ca[:, 0, :, j - 1], sb.ca[:, 1, :, j - 1],
                      a_re, a_im, -1)
            dve.sem_inc(s_ca, 1)

        @block.tensor
        def _(pe):
            pe.wait_ge(s_ba, 1)
            for n in range(8):
                if n >= 4:
                    pe.wait_ge(s_wb, n - 3)
                for k in range(4):
                    tr = nc.tensor.transpose(ps[:, n % 4, k * P:(k + 1) * P],
                                             ba[:, n // 4, 4 * (n % 4) + k].rearrange("p i c -> p (i c)"),
                                             ident[:, :])
                tr.then_inc(s_tb, 1)
            pe.wait_ge(s_ca, 1)
            for b in range(4):
                for k in range(4):
                    pair = 4 * b + k
                    for i in range(CL):
                        for ri in range(2):
                            mm = nc.tensor.matmul(
                                ps[i * CH:(i + 1) * CH, 4 + b, k * P + i * CH:(k + 1) * P],
                                ba[:, ri, pair, CL - 1, :],
                                sb.ca[:, ri, pair, 0:CL - i, :].rearrange("p j c -> p (j c)"),
                                start=ri == 0, stop=ri == 1)
                mm.then_inc(s_tt, 1)


def s5_run(nc, mem, tag, proj, d, consts, sb, att):
    v = mem.at(f"{tag}_v", [P, 2, 4, NCH + 1], 181 * KB)
    tmp = mem.at(f"{tag}_tmp", [P, 2, 4, NCH], 56 * KB)
    mb = mem.at(f"{tag}_mb", [P, 4, NCH + 1], 190 * KB)
    ysb = mem.at(f"{tag}_ysb", [P, 2, 4, NCH], 195 * KB)
    yt = mem.at(f"{tag}_yt", [P, 4, CL, NCH], 148 * KB)
    gl = mem.at(f"{tag}_gelu_tmp", [P, 4, T], 0)
    wg = mem.at(f"{tag}_wg", [P, 4, 512], 16 * KB)
    sg = mem.at(f"{tag}_sg", [P, 4, T], 24 * KB)
    dd = mem.at(f"{tag}_d", [P, 4], 52 * KB + 2560)
    ps = mem.psum
    s_in = mem.sem(f"{tag}_weights_loaded")
    s_v = mem.sem(f"{tag}_dve_chain")
    s_s = mem.sem(f"{tag}_inputs_summed")
    s_rd = mem.sem(f"{tag}_inputs_read")
    s_h = mem.sem(f"{tag}_states_ready")
    s_y = mem.sem(f"{tag}_outputs_summed")
    s_ys = mem.sem(f"{tag}_outputs_out")
    s_yt = [mem.sem(f"{tag}_outputs_laid_out{b}") for b in range(4)]
    s_pre = mem.sem(f"{tag}_tanh_arg")
    s_th = mem.sem(f"{tag}_tanh_ready")
    s_ge = mem.sem(f"{tag}_gelu_ready")
    s_z = mem.sem(f"{tag}_gate_summed")
    s_sg = mem.sem(f"{tag}_gate_ready")

    with nc.Block() as block:
        @block.sync
        def _(sp):
            sp.dma_start(dd[:, :], d["s5_d"]).then_inc(s_in, 16)
            for b in range(4):
                sp.wait_ge(s_ys, b + 1)
                for i in range(CL):
                    for q in range(4):
                        sp.dma_start(yt[q * CH:(q + 1) * CH, b, i, :],
                                     ysb[i * CH:(i + 1) * CH, b % 2, q, :]).then_inc(s_yt[b], 16)
            sp.wait_ge(s_h, 4)
            sp.dma_start(wg[:, :, :], d["s5_wg"]).then_inc(s_in, 16)

        @block.scalar
        def _(act):
            for b in range(4):
                act.wait_ge(s_y, b + 1)
                if b >= 2:
                    act.wait_ge(s_yt[b - 2], 16 * 16)
                nc.scalar.activation(ysb[:, b % 2], ps[:, 4 + 2 * (b % 2):6 + 2 * (b % 2), :].rearrange(
                    "p a (b n) -> p (a b) n", b=2), ACT.Copy).then_inc(s_ys, 1)
            act.wait_ge(s_pre, 1)
            nc.scalar.activation(gl[:, :, :], gl[:, :, :], ACT.Tanh, scale=GELU_S).then_inc(s_th, 1)
            for f in range(4):
                act.wait_ge(s_z, f + 1)
                nc.scalar.activation(sg[:, f, :], ps[:, 2 * f:2 * f + 2, :].rearrange("p a n -> p (a n)"),
                                     ACT.Sigmoid).then_inc(s_sg, 1)

        @block.vector
        def _(dve):
            V = nc.vector
            chain = Chain(dve, s_v)
            TT = V.tensor_tensor
            chain.link(V.memset(v[:, :, :, 0:1], 0.0))
            for b in range(4):
                prs = slice(4 * b, 4 * b + 4)
                rr, ri = sb.rot[:, 0, prs, :], sb.rot[:, 1, prs, :]
                s_re = ps[:, 0:2, :].rearrange("p a (b n) -> p (a b) n", b=2)
                s_im = ps[:, 2:4, :].rearrange("p a (b n) -> p (a b) n", b=2)
                v_re, v_im = v[:, 0, :, 1:NCH + 1], v[:, 1, :, 1:NCH + 1]
                chain.link(V.tensor_copy(mb[:, :, :], sb.m4[:, prs].unsqueeze(2).broadcast_to([P, 4, NCH + 1])))
                chain.link(V.memset(mb[:, :, 0:1], 0.0))
                dve.wait_ge(s_s, b + 1)
                if b:
                    dve.wait_ge(s_y, b)
                chain.link(TT(tmp[:, 0], s_im, ri, ALU.mult))
                chain.link(TT(tmp[:, 1], s_re, ri, ALU.mult))
                chain.link(TT(v_re, s_re, rr, ALU.mult))
                TT(v_im, s_im, rr, ALU.mult).then_inc(s_rd, 1)
                dve.wait_ge(s_rd, b + 1)
                chain.link(TT(v_re, v_re, tmp[:, 0], ALU.add))
                chain.link(TT(v_im, v_im, tmp[:, 1], ALU.subtract))
                for part in range(2):
                    flat = v[:, part].rearrange("p a n -> p (a n)")
                    chain.link(V.tensor_tensor_scan(flat, mb[:, :, :].rearrange("p a n -> p (a n)"), flat,
                                                    0.0, ALU.mult, ALU.add))
                chain.link(TT(tmp[:, 0], v_im, ri, ALU.mult))
                chain.link(TT(tmp[:, 1], v_re, ri, ALU.mult))
                chain.link(TT(v_re, v_re, rr, ALU.mult))
                chain.link(TT(v_im, v_im, rr, ALU.mult))
                chain.link(TT(v_re, v_re, tmp[:, 0], ALU.subtract))
                TT(v_im, v_im, tmp[:, 1], ALU.add).then_inc(s_h, 1)
            dve.wait_ge(s_in, 16)
            for b in range(4):
                dve.wait_ge(s_yt[b], 16 * 16)
                V.scalar_tensor_tensor(out=yt[:, b], in0=proj[:, b, :].rearrange("p (c i) -> p i c", i=CL),
                                       scalar=dd[:, b:b + 1], in1=yt[:, b], op0=ALU.mult, op1=ALU.add)\
                    .then_inc(s_v, 1)
                chain.n += 1
            dve.wait_ge(s_v, chain.n)

            def tanh():
                dve.sem_inc(s_pre, 1)
                dve.wait_ge(s_th, 1)

            dve.wait_ge(s_h, 4)
            gelu_steps(nc, chain, tanh, yt[:, :, :, :].rearrange("p a i c -> p a (i c)"), gl[:, :, :])
            dve.sem_inc(s_ge, 1)
            for f in range(4):
                dve.wait_ge(s_sg, f + 1)
                TT(att[:, f, :].rearrange("p (c i) -> p i c", i=CL), yt[:, f],
                   sg[:, f, :].rearrange("p (i c) -> p i c", i=CL), ALU.mult).then_inc(s_v, 1)
                chain.n += 1
            dve.wait_ge(s_v, chain.n)

        @block.tensor
        def _(pe):
            def inputs(b):
                if b:
                    pe.wait_ge(s_rd, b)
                for part in range(2):
                    for k in range(4):
                        mm = nc.tensor.matmul(ps[:, 2 * part + k // 2, (k % 2) * NCH:(k % 2 + 1) * NCH],
                                              sb.wb[:, part, 4 * b + k, :], sb.u[:, 4 * b + k, :],
                                              start=True, stop=True)
                mm.then_inc(s_s, 1)

            inputs(0)
            for b in range(4):
                if b + 1 < 4:
                    inputs(b + 1)
                pe.wait_ge(s_h, b + 1)
                if b >= 2:
                    pe.wait_ge(s_ys, b - 1)
                for k in range(4):
                    out = ps[:, 4 + 2 * (b % 2) + k // 2, (k % 2) * NCH:(k % 2 + 1) * NCH]
                    pair = 4 * b + k
                    nc.tensor.matmul(out, sb.wt[:, pair, :], sb.u[:, pair, :], start=True, stop=False)
                    for part in range(2):
                        mm = nc.tensor.matmul(out, sb.ca[:, part, pair, 1:CL + 1, :].rearrange(
                            "p j c -> p (j c)"), v[:, part, k, 0:NCH], start=False, stop=part == 1)
                mm.then_inc(s_y, 1)
            pe.wait_ge(s_in, 32)
            pe.wait_ge(s_ge, 1)
            pe.wait_ge(s_ys, 4)
            for f in range(4):
                for h in range(2):
                    for k in range(4):
                        mm = nc.tensor.matmul(ps[:, 2 * f + h, :], wg[:, k, f * P:(f + 1) * P],
                                              yt[:, k, 2 * h:2 * h + 2, :].rearrange("p i c -> p (i c)"),
                                              start=k == 0, stop=k == 3)
                mm.then_inc(s_z, 1)


def trunk(nc, d, out):
    with ExitStack() as ctx:
        mem = Mem(nc, ctx)
        consts = load_constants(nc, mem, d["ident"], d["masks"])
        ident = consts[0]
        x_hi = mem.at("x_hi", [P, KT, T], 0, F32R)
        x_lo = mem.at("x_lo", [P, KT, T], 32 * KB, F32R)
        att = mem.at("att", [P, KT, T], 172 * KB)
        hidden = mem.at("hidden", [P, FT, T], 64 * KB)
        kept = [nc.dram_tensor(f"x_kept{i}", (T, D), F32, kind="Internal").ap() for i in range(3)]
        c_kept = nc.dram_tensor("fox_c", (2, 16, T), F32, kind="Internal").ap()
        load_x(nc, mem, "load", d["x_t"], x_hi, x_lo)

        proj = mem.at("proj0", [P, 15, T], 64 * KB)
        project(nc, mem, "in0", x_hi, x_lo, d["l0_w_in"], 15, proj, 164 * KB)
        sb = S5Buffers(mem)
        s5_weights(nc, mem, "s5w", proj, d, consts, sb)
        s5_run(nc, mem, "s5r", proj, d, consts, sb, att)
        nb = NsaBuffers(mem)
        nsa_prepare(nc, mem, "nsap", proj, d, consts, nb)
        nsa_compressed(nc, mem, "nsac", d, consts, nb)
        nsa_attention(nc, mem, "nsaa", proj, d, consts, nb, att)
        project_norm(nc, mem, "out0", att, KT, d["l0_w_out"], d["x"], d["l0_ln1"], ident, kept[0], x_hi, x_lo,
                     64 * KB, False)
        gate_up(nc, mem, "gu0", x_hi, x_lo, d["l0_gate_up"], hidden, 152 * KB)
        project_norm(nc, mem, "dn0", hidden, FT, d["l0_w_down"], kept[0], d["l0_ln2"], ident, kept[1], x_hi,
                     x_lo, 152 * KB, False)

        mem.recycle_semaphores()
        proj = mem.at("proj1", [P, 25, T], 64 * KB)
        project(nc, mem, "in1", x_hi, x_lo, d["l1_w_in"], 25, proj, 164 * KB)
        fox_decay(nc, mem, "foxd", proj, 24, d["l1_b_f"], c_kept)
        fox_attention(nc, mem, "foxa", proj, c_kept, d["one"], consts, att)
        project_norm(nc, mem, "out1", att, KT, d["l1_w_out"], kept[1], d["l1_ln1"], ident, kept[2], x_hi, x_lo,
                     64 * KB, False)
        gate_up(nc, mem, "gu1", x_hi, x_lo, d["l1_gate_up"], hidden, 152 * KB)
        project_norm(nc, mem, "dn1", hidden, FT, d["l1_w_down"], kept[2], d["l1_ln2"], ident, out, x_hi, x_lo,
                     152 * KB, True)


def layouts(np, i):
    def tiles(w):
        return np.ascontiguousarray(w.reshape(KT, P, w.shape[1] // P, P).transpose(2, 1, 0, 3))

    def to_full_tile(w):
        n = w.shape[1] % P
        return np.concatenate([w, w[:, 0:P - n]], 1)

    def pairs(a):
        return np.ascontiguousarray(a.reshape(NP, 2, HD).transpose(1, 2, 0).reshape(P, NP))

    def block(a):
        o = np.zeros((2, HD, NP, 2, CH // 2), np.float32)
        a = a.reshape(NP, 2, HD, CH // 2)
        for g in range(2):
            o[g, :, :, g, :] = a[:, g].transpose(1, 0, 2)
        return o.reshape(P, NP, CH)

    x = i["x"][0]
    w1 = np.stack([i["l0_nsa_phi_k1"], i["l0_nsa_phi_v1"]]).reshape(2, 32, HD, P).transpose(0, 2, 1, 3)
    out = dict(
        x=x, x_t=x.T.reshape(KT, P, T).transpose(1, 0, 2),
        l0_w_in=tiles(to_full_tile(i["l0_w_in"])), l1_w_in=tiles(to_full_tile(i["l1_w_in"])),
        l1_b_f=i["l1_fox_b_f"].reshape(16, 1),
        nsa_w1=np.concatenate([w1, w1], 1), nsa_w2=np.stack([i["l0_nsa_phi_k2"], i["l0_nsa_phi_v2"]], 1),
        nsa_pos=np.stack([i["l0_nsa_pos_k"].T, i["l0_nsa_pos_v"].T], 1),
        s5_lr=pairs(i["l0_s5_lambda_re"]), s5_li=pairs(i["l0_s5_lambda_im"]),
        s5_ls=i["l0_s5_log_step"].reshape(NP, 2).T,
        s5_b=np.stack([block(i["l0_s5_b_re"]), block(i["l0_s5_b_im"])]),
        s5_c=np.stack([block(i["l0_s5_c_re"].transpose(0, 2, 1)), block(i["l0_s5_c_im"].transpose(0, 2, 1))]),
        s5_d=i["l0_s5_d"].reshape(4, P).T, s5_wg=i["l0_s5_w_glu"].reshape(4, P, 512).transpose(1, 0, 2))
    for n in range(DEPTH):
        out[f"l{n}_w_out"] = i[f"l{n}_w_out"].reshape(KT, P, D)
        out[f"l{n}_gate_up"] = np.stack([tiles(i[f"l{n}_ffn_w_gate"]), tiles(i[f"l{n}_ffn_w_up"])], 1)
        out[f"l{n}_w_down"] = i[f"l{n}_ffn_w_down"].reshape(FT, P, D)
        for k in (1, 2):
            out[f"l{n}_ln{k}"] = np.stack([i[f"l{n}_ln{k}_g"], i[f"l{n}_ln{k}_b"]])
    return {k: np.ascontiguousarray(v) for k, v in {**shape_constants(np), **out}.items()}


def kernel(**inputs):
    import numpy as np
    import concourse.bacc as bacc
    from concourse.bass_utils import run_bass_kernel_spmd as run

    arrays = layouts(np, {k: np.asarray(v) for k, v in inputs.items()})
    nc = bacc.Bacc("TRN2", target_bir_lowering=False, num_devices=1)
    d = {k: nc.dram_tensor(f"in_{k}", v.shape, F32, kind="ExternalInput").ap() for k, v in arrays.items()}
    out = nc.dram_tensor("out_x", (T, D), F32, kind="ExternalOutput").ap()
    trunk(nc, d, out)
    r = run(nc, [{f"in_{k}": v for k, v in arrays.items()}], core_ids=[0])
    return r.results[0]["out_x"].reshape(1, T, D)
```

```python
from contextlib import ExitStack

import concourse.bass as bass
from concourse import mybir

F32 = mybir.dt.float32
F32R = mybir.dt.float32r
BF16 = mybir.dt.bfloat16
ALU = mybir.AluOpType
ACT = mybir.ActivationFunctionType
AX = mybir.AxisListType

P = 128
T = 1024
D = 1024
KT = D // P
NT = T // P
HALF = 512
DFF = 2816
FT = DFF // P
DEPTH = 2
ALPHA = (2 * DEPTH) ** 0.25
LN_EPS = 1e-5
KB = 1024
BASE = 17 * KB


class Mem:

    def __init__(self, nc, ctx):
        self.nc, self.sems = nc, []
        self.psum = ctx.enter_context(nc.psum_tensor("psum", [P, 8, HALF], F32))

    def at(self, name, shape, offset, dtype=F32):
        return self.nc.alloc_sbuf_tensor_at(name, shape, dtype, offset=BASE + offset)

    def sem(self, name):
        self.sems.append(self.nc.alloc_semaphore(name))
        return self.sems[-1]

    def recycle_semaphores(self):
        self.nc.all_engine_barrier()
        self.nc.clear_and_free_semaphores(self.sems)
        self.nc.all_engine_barrier()
        self.sems = []


class Chain:

    def __init__(self, eng, sem, base=0):
        self.eng, self.sem, self.base, self.n = eng, sem, base, 0

    def link(self, instruction):
        instruction.then_inc(self.sem, 1)
        self.n += 1
        self.eng.wait_ge(self.sem, self.base + self.n)


def split_passes(pe, out, w_hi, w_lo, x_hi, x_lo, first, last):
    pe.matmul(out, w_hi, x_hi, start=first, stop=False)
    pe.matmul(out, w_hi, x_lo, start=False, stop=False)
    return pe.matmul(out, w_lo, x_hi, start=False, stop=last)


def load_x(nc, mem, tag, xt_dram, x_hi, x_lo):
    raw = mem.at(f"{tag}_raw", [P, KT, T], 64 * KB)
    s_raw = [mem.sem(f"{tag}_raw_loaded{k}") for k in range(KT)]
    s_hi = mem.sem(f"{tag}_hi_ready")
    s_lo = mem.sem(f"{tag}_lo_ready")
    with nc.Block() as block:
        @block.sync
        def _(sp):
            for k in range(KT):
                sp.dma_start(raw[:, k, :], xt_dram[:, k, :]).then_inc(s_raw[k], 16)

        @block.scalar
        def _(act):
            for k in range(KT):
                act.wait_ge(s_raw[k], 16)
                nc.scalar.activation(x_hi[:, k, :], raw[:, k, :], ACT.Copy).then_inc(s_hi, 1)

        @block.vector
        def _(dve):
            for k in range(KT):
                dve.wait_ge(s_hi, k + 1)
                nc.vector.tensor_tensor(x_lo[:, k, :], raw[:, k, :], x_hi[:, k, :].bitcast(F32),
                                        ALU.subtract).then_inc(s_lo, 1)
            dve.wait_ge(s_lo, KT)


def project(nc, mem, tag, x_hi, x_lo, w_dram, n_tiles, dst, ring):
    raw = mem.at(f"{tag}_wraw", [P, 2, KT, P], ring)
    w_hi = mem.at(f"{tag}_whi", [P, 2, KT, P], ring + 8 * KB, F32R)
    w_lo = mem.at(f"{tag}_wlo", [P, 2, KT, P], ring + 16 * KB, F32R)
    ps = mem.psum
    s_raw = [mem.sem(f"{tag}_w_loaded{u}") for u in range(2)]
    s_hi = mem.sem(f"{tag}_w_hi_ready")
    s_lo = mem.sem(f"{tag}_w_lo_ready")
    s_mm = mem.sem(f"{tag}_half_done")
    s_ev = [mem.sem(f"{tag}_half{h}_out") for h in range(2)]
    n_pairs, odd = divmod(n_tiles, 2)

    with nc.Block() as block:
        @block.sync
        def _(sp):
            def load(j, u):
                sp.dma_start(raw[:, u], w_dram[2 * j + u]).then_inc(s_raw[u], 16)

            load(0, 0)
            load(0, 1)

            def next_load(j, u):
                sp.wait_ge(s_lo, 2 * j + u - 1)
                load(j, u)

            with sp.Fori(1, n_pairs, 1) as j:
                next_load(j, 0)
                next_load(j, 1)
            if odd:
                next_load(n_pairs, 0)

        @block.scalar
        def _(act):
            act.sem_inc(s_ev[0], 2)

            def split(j, u):
                act.wait_ge(s_raw[u], 16 * j + 16)
                act.wait_ge(s_mm, 4 * j + 2 * u + 2)
                nc.scalar.activation(w_hi[:, u], raw[:, u], ACT.Copy).then_inc(s_hi, 1)

            def evacuate(j, u):
                act.wait_ge(s_mm, 4 + 4 * j + 2 * u + 1)
                nc.scalar.activation(dst[:, 2 * j + u, 0:HALF], ps[:, 2 * u, :], ACT.Copy)\
                    .then_inc(s_ev[0], 1)

            split(0, 0)
            split(0, 1)
            evacuate(0, 0)
            with act.Fori(1, n_pairs, 1) as j:
                split(j, 0)
                evacuate(j - 1, 1)
                split(j, 1)
                evacuate(j, 0)
            if odd:
                split(n_pairs, 0)
            evacuate(n_pairs - 1, 1)
            if odd:
                evacuate(n_pairs, 0)

        @block.vector
        def _(dve):
            dve.sem_inc(s_ev[1], 2)

            def split(j, u):
                dve.wait_ge(s_hi, 2 * j + u + 1)
                nc.vector.tensor_tensor(w_lo[:, u], raw[:, u], w_hi[:, u].bitcast(F32),
                                        ALU.subtract).then_inc(s_lo, 1)

            def evacuate(j, u):
                dve.wait_ge(s_mm, 4 + 4 * j + 2 * u + 2)
                nc.vector.tensor_copy(dst[:, 2 * j + u, HALF:T], ps[:, 2 * u + 1, :])\
                    .then_inc(s_ev[1], 1)

            split(0, 0)
            split(0, 1)
            evacuate(0, 0)
            with dve.Fori(1, n_pairs, 1) as j:
                split(j, 0)
                evacuate(j - 1, 1)
                split(j, 1)
                evacuate(j, 0)
            if odd:
                split(n_pairs, 0)
            evacuate(n_pairs - 1, 1)
            if odd:
                evacuate(n_pairs, 0)

        @block.tensor
        def _(pe):
            pe.sem_inc(s_mm, 4)

            def tile(j, u):
                pe.wait_ge(s_lo, 2 * j + u + 1)
                for h in range(2):
                    pe.wait_ge(s_ev[h], 2 * j + u + 1)
                    cols = slice(h * HALF, (h + 1) * HALF)
                    for k in range(KT):
                        mm = split_passes(nc.tensor, ps[:, 2 * u + h, :], w_hi[:, u, k], w_lo[:, u, k],
                                          x_hi[:, k, cols], x_lo[:, k, cols], k == 0, k == KT - 1)
                    mm.then_inc(s_mm, 1)

            with pe.Fori(0, n_pairs, 1) as j:
                tile(j, 0)
                tile(j, 1)
            if odd:
                tile(n_pairs, 0)


def gate_up(nc, mem, tag, x_hi, x_lo, w_dram, hidden, ring):
    raw = mem.at(f"{tag}_wraw", [P, 2, KT, P], ring)
    w_hi = mem.at(f"{tag}_whi", [P, 2, KT, P], ring + 8 * KB, F32R)
    w_lo = mem.at(f"{tag}_wlo", [P, 2, KT, P], ring + 16 * KB, F32R)
    sg = mem.at(f"{tag}_sg", [P, 2, HALF], ring + 24 * KB)
    ps = mem.psum
    s_raw = [mem.sem(f"{tag}_w_loaded{u}") for u in range(2)]
    s_hi = mem.sem(f"{tag}_w_hi_ready")
    s_lo = mem.sem(f"{tag}_w_lo_ready")
    s_mm = mem.sem(f"{tag}_half_done")
    s_sig = mem.sem(f"{tag}_sigmoid_ready")
    s_gs = mem.sem(f"{tag}_gate_silu")
    s_h = mem.sem(f"{tag}_hidden_done")
    n_pairs = FT // 2

    with nc.Block() as block:
        @block.sync
        def _(sp):
            for gu in range(2):
                sp.dma_start(raw[:, gu], w_dram[0, gu]).then_inc(s_raw[gu], 16)
            with sp.Fori(1, FT, 1) as f:
                for gu in range(2):
                    sp.wait_ge(s_lo, 2 * f + gu - 1)
                    sp.dma_start(raw[:, gu], w_dram[f, gu]).then_inc(s_raw[gu], 16)

        @block.scalar
        def _(act):
            def split(j, fu):
                for gu in range(2):
                    act.wait_ge(s_raw[gu], 32 * j + 16 * fu + 16)
                    act.wait_ge(s_mm, 8 * j + 4 * fu + 2 * gu + 2)
                    nc.scalar.activation(w_hi[:, gu], raw[:, gu], ACT.Copy).then_inc(s_hi, 1)

            def sigmoid(j, fu):
                for h in range(2):
                    act.wait_ge(s_mm, 4 + 8 * j + 4 * fu + h + 1)
                    act.wait_ge(s_h, 4 * j + 2 * fu + h + 1)
                    nc.scalar.activation(sg[:, h, :], ps[:, 4 * fu + h, :], ACT.Sigmoid)\
                        .then_inc(s_sig, 1)

            split(0, 0)
            split(0, 1)
            sigmoid(0, 0)
            with act.Fori(1, n_pairs, 1) as j:
                split(j, 0)
                sigmoid(j - 1, 1)
                split(j, 1)
                sigmoid(j, 0)
            sigmoid(n_pairs - 1, 1)

        @block.vector
        def _(dve):
            dve.sem_inc(s_h, 2)

            def split(j, fu):
                for gu in range(2):
                    dve.wait_ge(s_hi, 4 * j + 2 * fu + gu + 1)
                    nc.vector.tensor_tensor(w_lo[:, gu], raw[:, gu], w_hi[:, gu].bitcast(F32),
                                            ALU.subtract).then_inc(s_lo, 1)

            def multiply(j, fu):
                for h in range(2):
                    dve.wait_ge(s_sig, 4 * j + 2 * fu + h + 1)
                    nc.vector.tensor_tensor(sg[:, h, :], ps[:, 4 * fu + h, :], sg[:, h, :],
                                            ALU.mult).then_inc(s_gs, 1)
                    dve.wait_ge(s_mm, 4 + 8 * j + 4 * fu + 2 + h + 1)
                    dve.wait_ge(s_gs, 4 * j + 2 * fu + h + 1)
                    nc.vector.tensor_tensor(hidden[:, 2 * j + fu, h * HALF:(h + 1) * HALF], sg[:, h, :],
                                            ps[:, 4 * fu + 2 + h, :], ALU.mult).then_inc(s_h, 1)

            split(0, 0)
            split(0, 1)
            multiply(0, 0)
            with dve.Fori(1, n_pairs, 1) as j:
                split(j, 0)
                multiply(j - 1, 1)
                split(j, 1)
                multiply(j, 0)
            multiply(n_pairs - 1, 1)

        @block.tensor
        def _(pe):
            pe.sem_inc(s_mm, 4)

            def tiles(j, fu, first):
                for gu in range(2):
                    pe.wait_ge(s_lo, 4 * j + 2 * fu + gu + 1)
                    for h in range(2):
                        if not first:
                            pe.wait_ge(s_h, 4 * j + 2 * fu + h - 1)
                        cols = slice(h * HALF, (h + 1) * HALF)
                        for k in range(KT):
                            mm = split_passes(nc.tensor, ps[:, 4 * fu + 2 * gu + h, :], w_hi[:, gu, k],
                                              w_lo[:, gu, k], x_hi[:, k, cols], x_lo[:, k, cols],
                                              k == 0, k == KT - 1)
                        mm.then_inc(s_mm, 1)

            tiles(0, 0, True)
            tiles(0, 1, True)
            with pe.Fori(1, n_pairs, 1) as j:
                tiles(j, 0, False)
                tiles(j, 1, False)


def project_norm(nc, mem, tag, src, n_k, w_dram, res_dram, gb_dram, ident, x_dram, x_hi, x_lo, ring, last):
    MT = NT // 2
    raw = mem.at(f"{tag}_wraw", [P, 2, D], ring)
    w_hi = mem.at(f"{tag}_whi", [P, 2, D], ring + 8 * KB, F32R)
    w_lo = mem.at(f"{tag}_wlo", [P, 2, D], ring + 16 * KB, F32R)
    a_hi = mem.at(f"{tag}_ahi", [P, 2, HALF], ring + 24 * KB, F32R)
    a_lo = mem.at(f"{tag}_alo", [P, 2, HALF], ring + 28 * KB, F32R)
    res = mem.at(f"{tag}_res", [P, 2, D], ring + 32 * KB)
    gb = mem.at(f"{tag}_gb", [P, 2, D], ring + 40 * KB)
    stats = mem.at(f"{tag}_stats", [P, MT, 2, 6], ring + 48 * KB)
    mv = mem.at(f"{tag}_mv", [P, MT, 2], ring + 48 * KB + 256)
    vare = mem.at(f"{tag}_vare", [P, MT], ring + 48 * KB + 320)
    std = mem.at(f"{tag}_std", [P, MT], ring + 48 * KB + 352)
    rstd = mem.at(f"{tag}_rstd", [P, MT], ring + 48 * KB + 384)
    newt = mem.at(f"{tag}_newt", [P, MT], ring + 48 * KB + 416)
    shift = mem.at(f"{tag}_shift", [P, MT], ring + 48 * KB + 448)
    ps = mem.psum
    s_raw = [mem.sem(f"{tag}_w_loaded{u}") for u in range(2)]
    s_gb = mem.sem(f"{tag}_gb_loaded")
    s_res = [mem.sem(f"{tag}_res_loaded{u}") for u in range(2)]
    s_hi = mem.sem(f"{tag}_hi_ready")
    s_lo = mem.sem(f"{tag}_lo_ready")
    s_k = mem.sem(f"{tag}_k_done")
    s_acc = mem.sem(f"{tag}_tile_summed")
    s_y = mem.sem(f"{tag}_y_ready")
    s_dve = mem.sem(f"{tag}_dve_chain")
    s_var = mem.sem(f"{tag}_var_ready")
    s_std = mem.sem(f"{tag}_std_ready")
    s_coef = mem.sem(f"{tag}_coef_ready")
    s_xn = mem.sem(f"{tag}_normed")
    s_xg = mem.sem(f"{tag}_scaled")
    s_out = mem.sem(f"{tag}_x_ready")
    s_st = mem.sem(f"{tag}_x_stored")
    s_tr = mem.sem(f"{tag}_transposed")
    s_xh = mem.sem(f"{tag}_x_hi_ready")
    s_xl = mem.sem(f"{tag}_x_lo_ready")

    def parked(m, p):
        return src[:, 2 * m:2 * m + 2, p * HALF:(p + 1) * HALF]

    def banks(m):
        return ps[:, 2 * m:2 * m + 2, :]

    with nc.Block() as block:
        @block.sync
        def _(sp):
            sp.dma_start(raw[:, 0], w_dram[0]).then_inc(s_raw[0], 16)
            sp.dma_start(raw[:, 1], w_dram[1]).then_inc(s_raw[1], 16)
            sp.dma_start(gb[:, :, :], gb_dram.partition_broadcast(P)).then_inc(s_gb, 16)
            with sp.Fori(1, n_k // 2, 1) as j:
                for u in range(2):
                    sp.wait_ge(s_lo, 2 * j + u - 1)
                    sp.dma_start(raw[:, u], w_dram[2 * j + u]).then_inc(s_raw[u], 16)
            with sp.Fori(0, n_k // 2, 1) as j:
                for u in range(2):
                    sp.wait_ge(s_lo, n_k + 2 * j + u - 1)
                    sp.dma_start(raw[:, u], w_dram[2 * j + u]).then_inc(s_raw[u], 16)

        @block.gpsimd
        def _(pool):
            def load_residual(t):
                if t >= 2:
                    pool.wait_ge(s_y, t - 1)
                pool.dma_start(res[:, t % 2], res_dram[t * P:(t + 1) * P, :]).then_inc(s_res[t % 2], 16)

            for p in range(2):
                for m in range(MT):
                    load_residual(MT * p + m)
                if p == 0:
                    pool.wait_ge(s_gb, 16)
                for m in range(MT):
                    pool.wait_ge(s_xn, MT * p + m + 1)
                    nc.gpsimd.tensor_tensor(parked(m, p), parked(m, p),
                                            gb[:, 0, :].rearrange("p (a n) -> p a n", a=2),
                                            ALU.mult).then_inc(s_xg, 1)
                for m in range(MT):
                    t = MT * p + m
                    pool.wait_ge(s_out, t + 1)
                    pool.dma_start(x_dram[t * P:(t + 1) * P, :].rearrange("t (a n) -> t a n", a=2),
                                   parked(m, p)).then_inc(s_st, 16)
            pool.wait_ge(s_st, 16 * NT)

        @block.scalar
        def _(act):
            def split(p, j, u):
                act.wait_ge(s_raw[u], 8 * n_k * p + 16 * j + 16)
                act.wait_ge(s_k, n_k * p + 2 * j + u + 1)
                nc.scalar.activation(w_hi[:, u], raw[:, u], ACT.Copy)
                nc.scalar.activation(a_hi[:, u], src[:, 2 * j + u, p * HALF:(p + 1) * HALF],
                                     ACT.Copy).then_inc(s_hi, 1)

            def normalize(p):
                act.wait_ge(s_var, p + 1)
                nc.scalar.activation(std[:, :], vare[:, :], ACT.Sqrt).then_inc(s_std, 1)
                act.wait_ge(s_coef, p + 1)
                for m in range(MT):
                    nc.scalar.activation(parked(m, p), parked(m, p), ACT.Identity,
                                         bias=shift[:, m:m + 1], scale=rstd[:, m:m + 1]).then_inc(s_xn, 1)

            with act.Fori(0, n_k // 2, 1) as j:
                split(0, j, 0)
                split(0, j, 1)
            split(1, 0, 0)
            split(1, 0, 1)
            normalize(0)
            with act.Fori(1, n_k // 2, 1) as j:
                split(1, j, 0)
                split(1, j, 1)
            normalize(1)
            if not last:
                for t in range(NT):
                    act.wait_ge(s_tr, t + 1)
                    nc.scalar.activation(x_hi[:, :, t * P:(t + 1) * P],
                                         banks(t % MT).rearrange("p a (b n) -> p (a b) n", n=P),
                                         ACT.Copy).then_inc(s_xh, 1)

        @block.vector
        def _(dve):
            chain = Chain(dve, s_dve)

            def split(p, j, u):
                dve.wait_ge(s_hi, n_k * p + 2 * j + u + 1)
                nc.vector.tensor_tensor(w_lo[:, u], raw[:, u], w_hi[:, u].bitcast(F32), ALU.subtract)
                nc.vector.tensor_tensor(a_lo[:, u], src[:, 2 * j + u, p * HALF:(p + 1) * HALF],
                                        a_hi[:, u].bitcast(F32), ALU.subtract).then_inc(s_lo, 1)

            def residual(p):
                for m in range(MT):
                    t = MT * p + m
                    dve.wait_ge(s_res[t % 2], 16 * (t // 2) + 16)
                    dve.wait_ge(s_acc, t + 1)
                    if m == 0:
                        dve.wait_ge(s_lo, n_k * (p + 1))
                    nc.vector.scalar_tensor_tensor(
                        out=parked(m, p), in0=res[:, t % 2].rearrange("p (a n) -> p a n", a=2),
                        scalar=ALPHA, in1=banks(m), op0=ALU.mult, op1=ALU.add).then_inc(s_y, 1)

            def statistics(p):
                dve.wait_ge(s_y, MT * (p + 1))
                for m in range(MT):
                    for a in range(2):
                        nc.vector.bn_stats(stats[:, m, a, :], src[:, 2 * m + a, p * HALF:(p + 1) * HALF])\
                            .then_inc(s_dve, 1)
                        chain.n += 1
                dve.wait_ge(s_dve, chain.n)
                for m in range(MT):
                    nc.vector.bn_aggr(mv[:, m, :], stats[:, m].rearrange("p a b -> p (a b)")).then_inc(s_dve, 1)
                    chain.n += 1
                dve.wait_ge(s_dve, chain.n)
                nc.vector.tensor_scalar(vare[:, :], mv[:, :, 1], LN_EPS, None, ALU.add).then_inc(s_var, 1)
                dve.wait_ge(s_std, p + 1)
                chain.link(nc.vector.reciprocal(std[:, :], std[:, :]))
                chain.link(nc.vector.tensor_tensor(newt[:, :], std[:, :], std[:, :], ALU.mult))
                chain.link(nc.vector.tensor_tensor(newt[:, :], newt[:, :], vare[:, :], ALU.mult))
                chain.link(nc.vector.tensor_scalar(newt[:, :], newt[:, :], -0.5, 1.5, ALU.mult, ALU.add))
                chain.link(nc.vector.tensor_tensor(rstd[:, :], newt[:, :], std[:, :], ALU.mult))
                nc.vector.scalar_tensor_tensor(out=shift[:, :], in0=mv[:, :, 0], scalar=-1.0,
                                               in1=rstd[:, :], op0=ALU.mult, op1=ALU.mult).then_inc(s_coef, 1)
                for m in range(MT):
                    dve.wait_ge(s_xg, MT * p + m + 1)
                    nc.vector.tensor_tensor(parked(m, p), parked(m, p),
                                            gb[:, 1, :].rearrange("p (a n) -> p a n", a=2),
                                            ALU.add).then_inc(s_out, 1)

            with dve.Fori(0, n_k // 2, 1) as j:
                split(0, j, 0)
                split(0, j, 1)
            residual(0)
            split(1, 0, 0)
            split(1, 0, 1)
            statistics(0)
            with dve.Fori(1, n_k // 2, 1) as j:
                split(1, j, 0)
                split(1, j, 1)
            residual(1)
            statistics(1)
            if not last:
                for t in range(NT):
                    dve.wait_ge(s_xh, t + 1)
                    cols = slice(t * P, (t + 1) * P)
                    nc.vector.tensor_tensor(x_lo[:, :, cols], banks(t % MT).rearrange("p a (b n) -> p (a b) n", n=P),
                                            x_hi[:, :, cols].bitcast(F32), ALU.subtract).then_inc(s_xl, 1)
                dve.wait_ge(s_xl, NT)

        @block.tensor
        def _(pe):
            pe.sem_inc(s_k, 2)

            def products(p, j, u, first, final):
                pe.wait_ge(s_lo, n_k * p + 2 * j + u + 1)
                for m in range(MT):
                    if first and p:
                        pe.wait_ge(s_y, m + 1)
                    for h in range(2):
                        mm = split_passes(nc.tensor, ps[:, 2 * m + h, :], a_hi[:, u, m * P:(m + 1) * P],
                                          a_lo[:, u, m * P:(m + 1) * P], w_hi[:, u, h * HALF:(h + 1) * HALF],
                                          w_lo[:, u, h * HALF:(h + 1) * HALF], first, final)
                    if final:
                        mm.then_inc(s_acc, 1)
                if not final:
                    mm.then_inc(s_k, 1)

            for p in range(2):
                products(p, 0, 0, True, False)
                products(p, 0, 1, False, False)
                with pe.Fori(1, n_k // 2 - 1, 1) as j:
                    products(p, j, 0, False, False)
                    products(p, j, 1, False, False)
                products(p, n_k // 2 - 1, 0, False, False)
                products(p, n_k // 2 - 1, 1, False, True)
                pe.wait_ge(s_acc, MT * (p + 1))
                pe.sem_inc(s_k, 1)
            if not last:
                for t in range(NT):
                    p, m = divmod(t, MT)
                    pe.wait_ge(s_out, t + 1)
                    if p == 0:
                        pe.wait_ge(s_y, MT + m + 1)
                    else:
                        pe.wait_ge(s_xl, m + 1)
                    for k in range(KT):
                        tr = nc.tensor.transpose(ps[:, 2 * m + k // 4, (k % 4) * P:(k % 4 + 1) * P],
                                                 src[:, 2 * m + k // 4, p * HALF + (k % 4) * P:
                                                     p * HALF + (k % 4 + 1) * P], ident[:, :])
                    tr.then_inc(s_tr, 1)


HD = 64
NEG = -1e30


def load_constants(nc, mem, ident_dram, mask_dram):
    ident = mem.at("ident", [P, P], 204 * KB)
    ident_b = mem.at("ident_bf16", [P, P], 204 * KB + 512, BF16)
    masks = mem.at("masks", [P, 2, P], 204 * KB + 768, BF16)
    wide = mem.at("mask_wide", [P, 2, P], 0)
    s_in = mem.sem("constants_loaded")
    s_cast = mem.sem("constants_cast")
    with nc.Block() as block:
        @block.sync
        def _(sp):
            sp.dma_start(ident[:, :], ident_dram).then_inc(s_in, 16)
            sp.dma_start(wide[:, :, :], mask_dram).then_inc(s_in, 16)

        @block.vector
        def _(dve):
            dve.wait_ge(s_in, 32)
            nc.vector.tensor_copy(ident_b[:, :], ident[:, :]).then_inc(s_cast, 1)
            nc.vector.tensor_copy(masks[:, :, :], wide[:, :, :]).then_inc(s_cast, 1)
            dve.wait_ge(s_cast, 2)
    return ident, ident_b, masks


NU = 12
FIRST = 8
CHUNKS_AT = {5: (0, 1), 7: (2, 3), 8: (4, 5), 10: (6, 7), 11: (8, 9), 12: (10,), 13: (11,)}


def score_units(window):
    out = []
    for part, order in ((0, (3, 0, 1, 2, 4, 5, 6, 7)), (1, (0, 1, 2, 3))):
        q_first = 4 - 4 * part
        for n, kt in enumerate(order):
            q0, q1 = max(q_first, kt), min(q_first + 3, kt + 4 if window else NT)
            masks = {}
            if q0 == kt:
                masks[0] = 0
            if window and q1 == kt + 4:
                masks[q1 - q0] = 1
            out.append((part, kt, q0 - q_first, q1 - q0 + 1, masks, n == 0, n == len(order) - 1))
    return out


def row_chunks(window):
    out = []
    for qb in range(NT - 1, -1, -1):
        kt0 = max(0, qb - 4) if window else 0
        n = qb + 1 - kt0
        masks = {n - 1: 0}
        if window and qb >= 4:
            masks[0] = 1
        for c in range(1 if qb < 4 else 2):
            m = min(4, n - 4 * c)
            here = {t - 4 * c: w for t, w in masks.items() if 4 * c <= t < 4 * c + m}
            out.append((qb, kt0 + 4 * c, m, here, len(out) % 2, 4 * c + m == n))
    return out


class AttentionBuffers:

    def __init__(self, nc, mem, tag, base):
        at = mem.at
        self.q1 = [at(f"{tag}_q1_{s}", [P, T], base + 4 * s * KB, F32R) for s in range(2)]
        self.q2 = [at(f"{tag}_q2_{s}", [P, T], base + (8 + 4 * s) * KB, F32R) for s in range(2)]
        self.k1 = [at(f"{tag}_k1_{s}", [P, T], base + (16 + 4 * s) * KB, F32R) for s in range(2)]
        self.k2 = [at(f"{tag}_k2_{s}", [P, T], base + (24 + 4 * s) * KB, F32R) for s in range(2)]
        self.pt = at(f"{tag}_pt", [P, 3, HALF], base + 32 * KB)
        self.o_sb = at(f"{tag}_o_sb", [HD + 1, 2, HALF], base + 38 * KB)
        self.diag = at(f"{tag}_diag", [P, 2, 4, P], base + 42 * KB)
        self.v = at(f"{tag}_v", [P, 2, NT, HD + 1], base + 46 * KB)
        self.one = at(f"{tag}_ones", [P, HD], base + 50 * KB + 512)
        self.v_in = at(f"{tag}_v_in", [P, T], base + 51 * KB)
        self.zero = at(f"{tag}_zero", [P, T], base + 55 * KB)
        self.mx = at(f"{tag}_max", [P, NT], base + 59 * KB)
        self.weight = at(f"{tag}_weight", [P, 2, 4], base + 59 * KB + 32)


def attention_setup(nc, mem, tag, ab, rows):
    s_zero = mem.sem(f"{tag}_zero_ready")
    s_clear = mem.sem(f"{tag}_cleared")
    s_rows = mem.sem(f"{tag}_fixed_rows_loaded")
    with nc.Block() as block:
        @block.gpsimd
        def _(pool):
            nc.gpsimd.memset(ab.one[:, :], 1.0)
            nc.gpsimd.memset(ab.v[:, :, :, :], 1.0)
            pool.wait_ge(s_clear, 4)
            for dst, src in rows:
                pool.dma_start(dst, src).then_inc(s_rows, 16)
            pool.wait_ge(s_rows, 16 * len(rows))

        @block.vector
        def _(dve):
            nc.vector.memset(ab.zero[:, :], 0.0).then_inc(s_zero, 1)
            dve.wait_ge(s_zero, 1)
            nc.vector.tensor_copy(ab.q2[0][:, :], ab.zero[:, :]).then_inc(s_clear, 1)
            nc.vector.tensor_copy(ab.k2[0][:, :], ab.zero[:, :]).then_inc(s_clear, 1)

        @block.scalar
        def _(act):
            act.wait_ge(s_zero, 1)
            nc.scalar.activation(ab.q2[1][:, :], ab.zero[:, :], ACT.Copy).then_inc(s_clear, 1)
            nc.scalar.activation(ab.k2[1][:, :], ab.zero[:, :], ACT.Copy).then_inc(s_clear, 1)


def attention(nc, mem, tag, n_iter, n_seg, ab, units, chunks, own_row, hooks, consts):
    ident, ident_b, masks = consts
    ps = mem.psum
    s_rows = [mem.sem(f"{tag}_rows_loaded{s}") for s in range(2)]
    s_hi = mem.sem(f"{tag}_high_parts")
    s_lo = mem.sem(f"{tag}_low_parts")
    s_pool = mem.sem(f"{tag}_pool_staged")
    s_vt = mem.sem(f"{tag}_values_transposed")
    s_v = mem.sem(f"{tag}_values_out")
    s_sc = mem.sem(f"{tag}_row_scores")
    s_mx = mem.sem(f"{tag}_maxima")
    s_mt = mem.sem(f"{tag}_maxima_transposed")
    s_row = mem.sem(f"{tag}_max_row")
    s_st = mem.sem(f"{tag}_scores")
    s_exp = mem.sem(f"{tag}_exponentials")
    s_pv = mem.sem(f"{tag}_products")
    s_osb = mem.sem(f"{tag}_part_out")
    s_rec = mem.sem(f"{tag}_reciprocals")
    s_sum = mem.sem(f"{tag}_sums_turned")
    s_w = mem.sem(f"{tag}_diagonal_ready")
    s_bc = mem.sem(f"{tag}_weights_spread")
    s_mul = mem.sem(f"{tag}_part_scaled")
    s_fin = mem.sem(f"{tag}_dve_chain")
    s_apart = mem.sem(f"{tag}_apart")
    spare = ps[:, 7, :]

    def st_bank(u):
        return ps[:, 2 + u % 3, :]

    def o_bank(part):
        return ps[:, 5 + part, :]

    def aux_row(i):
        return HD - own_row[i]

    def own(i):
        return slice(own_row[i], own_row[i] + HD)

    def other(i):
        return slice(HD - own_row[i], 2 * HD - own_row[i])

    def loop(eng, step):
        step(0, 0, (0, 1), None)
        with eng.Fori(0, n_iter - 1, 1) as j:
            for i in range(1, n_seg):
                step(j, i, (j, i + 1) if i + 1 < n_seg else (j + 1, 0), (j, i - 1))
            step(j + 1, 0, (j + 1, 1), (j, n_seg - 1))
        for i in range(1, n_seg):
            j = n_iter - 1
            step(j, i, (j, i + 1) if i + 1 < n_seg else None, (j, i - 1))

    with nc.Block() as block:
        @block.gpsimd
        def _(pool):
            G = nc.gpsimd

            def stage(j, i):
                n, s = j * n_seg + i, i % 2
                a = aux_row(i)
                pool.wait_ge(s_pv, n * NU + NU)
                pool.wait_ge(s_st, n * NU + NU)
                pool.sem_inc(s_apart, 1)
                hooks["rows"](pool, j, i, s_rows[s])
                G.tensor_copy(ab.q2[s][a:a + 1, :], ab.zero[a:a + 1, :]).then_inc(s_pool, 1)
                pool.wait_ge(s_pool, hooks["pool_step"] * n + 1)
                pool.sem_inc(s_apart, 1)
                hooks["pool"](pool, j, i, s_pool)
                pool.wait_ge(s_pool, hooks["pool_step"] * (n + 1))
                pool.sem_inc(s_apart, 1)

            stage(0, 0)
            loop(pool, lambda j, i, nxt, prev: stage(*nxt) if nxt else None)

        @block.scalar
        def _(act):
            A = nc.scalar.activation

            def stage(j, i, part):
                n, s = j * n_seg + i, i % 2
                if part == 0:
                    act.wait_ge(s_st, n * NU + NU)
                    act.sem_inc(s_apart, 1)
                    A(ab.q2[s][own(i), :], hooks["q"](j, i), ACT.Copy, scale=hooks["scale"]).then_inc(s_hi, 1)
                    A(ab.k1[s][own(i), :], hooks["k"](j, i), ACT.Copy).then_inc(s_hi, 1)
                else:
                    act.wait_ge(s_hi, hooks["act_step"] * n + 2)
                    A(ab.k1[s][other(i), :], ab.k1[s][own(i), :].bitcast(F32), ACT.Copy).then_inc(s_hi, 1)
                    act.wait_ge(s_vt, n + 1)
                    act.sem_inc(s_apart, 1)
                    hooks["act"](act, j, i, s_hi)

            def exp(j, i, u):
                e = (j * n_seg + i) * NU + u
                act.wait_ge(s_st, e + 2 * NU + 1)
                act.wait_ge(s_pv, e + 2 * NU - 2)
                cols = slice(0, units[i][u][3] * P)
                A(ab.pt[:, u % 3, cols], st_bank(u)[:, cols], ACT.Exp).then_inc(s_exp, 1)

            def values_out(j, i):
                n = j * n_seg + i
                act.wait_ge(s_vt, n + 2)
                act.wait_ge(s_pv, n * NU + NU)
                act.wait_ge(s_mul, 2 * n + 2)
                hooks["values_out"](j, i, spare).then_inc(s_v, 1)

            def part_out(j, i, part):
                n = j * n_seg + i
                act.wait_ge(s_pv, n * NU + 2 * NU + (FIRST, NU)[part])
                act.wait_ge(s_mul, 2 * n + part + 3)
                A(ab.o_sb[:, part, :], o_bank(part)[0:HD + 1, :], ACT.Copy).then_inc(s_osb, 1)

            def step(j, i, nxt, prev):
                for x in range(NU):
                    exp(j, i, x)
                    if nxt and x in (0, 2):
                        stage(*nxt, x // 2)
                    if x == 8 and nxt:
                        values_out(*nxt)
                    if x == 10:
                        part_out(j, i, 0)
                part_out(j, i, 1)

            stage(0, 0, 0)
            stage(0, 0, 1)
            values_out(0, 0)
            loop(act, step)

        @block.vector
        def _(dve):
            V = nc.vector
            dve.sem_inc(s_mul, 4)
            dve.sem_inc(s_mx, 1)
            dve.sem_inc(s_row, 1)
            dve.sem_inc(s_rec, 2)

            def low_parts(j, i, what):
                n, s = j * n_seg + i, i % 2
                dve.wait_ge(s_hi, hooks["act_step"] * n + 1 + what)
                if what == 0:
                    V.scalar_tensor_tensor(out=ab.q1[s][other(i), :], in0=hooks["q"](j, i),
                                           scalar=hooks["scale"], in1=ab.q2[s][own(i), :].bitcast(F32),
                                           op0=ALU.mult, op1=ALU.subtract).then_inc(s_lo, 1)
                    V.tensor_copy(ab.q1[s][own(i), :], ab.q2[s][own(i), :].bitcast(F32)).then_inc(s_lo, 1)
                else:
                    V.tensor_tensor(ab.k2[s][own(i), :], hooks["k"](j, i), ab.k1[s][own(i), :].bitcast(F32),
                                    ALU.subtract).then_inc(s_lo, 1)

            def maxima(j, i, a):
                qb, _, m, _, bank, final = chunks[i][a]
                if not final:
                    return
                dve.wait_ge(s_sc, (j * n_seg + i) * NU + a + 1)
                if a >= 8:
                    src = ps[:, bank, 0:m * P]
                else:
                    src = ps[:, 0:2, :].rearrange("p a n -> p (a n)")[:, 0:HALF + m * P]
                V.tensor_reduce(ab.mx[:, qb:qb + 1], src, AX.X, ALU.max).then_inc(s_mx, 1)

            def max_row(j, i, part):
                n, a = j * n_seg + i, aux_row(i)
                dve.wait_ge(s_mt, 2 * n + part + 1)
                V.tensor_scalar(ab.q2[i % 2][a:a + 1, (1 - part) * HALF:(2 - part) * HALF], spare[0:1, :], -1.0,
                                None, ALU.mult).then_inc(s_row, 1)

            def weights(j, i, part):
                n = j * n_seg + i
                dve.wait_ge(s_sum, 2 * n + part + 1)
                w = ab.weight[:, part, :]
                V.reciprocal(w, o_bank(part)[:, 0:4]).then_inc(s_rec, 1)
                dve.wait_ge(s_rec, 2 * n + part + 3)
                hooks["gate"](dve, j, i, part, w, s_fin)
                V.tensor_tensor(ab.diag[:, part], ident[:, :].unsqueeze(1).broadcast_to([P, 4, P]),
                                w.unsqueeze(2).broadcast_to([P, 4, P]), ALU.mult).then_inc(s_w, 1)

            def scale(j, i, part):
                n = j * n_seg + i
                dve.wait_ge(s_osb, 2 * n + part + 3)
                dve.wait_ge(s_bc, 2 * n + part + 1)
                hooks["finish"](dve, j, i, part, ab.o_sb[0:HD, part, :], spare[0:HD, :], s_fin, s_mul)

            def step(j, i, nxt, prev):
                if prev:
                    weights(*prev, 1)
                if nxt:
                    low_parts(*nxt, 0)
                max_row(j, i, 1)
                if prev:
                    scale(*prev, 1)
                if nxt:
                    low_parts(*nxt, 1)
                for x in range(5, NU + 2):
                    if x == 12:
                        weights(j, i, 0)
                    if nxt:
                        for a in CHUNKS_AT.get(x, ()):
                            maxima(*nxt, a)
                    if nxt and x == 11:
                        max_row(*nxt, 0)
                scale(j, i, 0)

            low_parts(0, 0, 0)
            low_parts(0, 0, 1)
            for a in range(NU):
                maxima(0, 0, a)
            max_row(0, 0, 0)
            loop(dve, step)
            weights(n_iter - 1, n_seg - 1, 1)
            scale(n_iter - 1, n_seg - 1, 1)

        @block.tensor
        def _(pe):
            M = nc.tensor.matmul
            pe.sem_inc(s_st, 2 * NU)
            pe.sem_inc(s_pv, 2 * NU)
            pe.sem_inc(s_exp, 3)
            pe.sem_inc(s_osb, 2)
            pe.sem_inc(s_vt, 1)

            def transpose_values(j, i):
                n = j * n_seg + i
                pe.wait_ge(s_hi, hooks["act_step"] * (n + 1))
                pe.wait_ge(s_row, 2 * n + 1)
                pe.wait_ge(s_mul, 2 * n + 2)
                hooks["transposes"](i, spare).then_inc(s_vt, 1)

            def row_scores(j, i, a):
                n, s = j * n_seg + i, i % 2
                qb, kt0, m, here, bank, _ = chunks[i][a]
                if a == 0:
                    pe.wait_ge(s_hi, hooks["act_step"] * (n + 1))
                    pe.wait_ge(s_lo, 3 * (n + 1))
                    pe.wait_ge(s_pool, hooks["pool_step"] * (n + 1))
                    pe.wait_ge(s_rows[s], 16 * hooks["row_step"] * ((n_seg // 2) * j + i // 2 + 1))
                before = a // 2 - 1 if a < 10 else a - 6
                pe.wait_ge(s_mx, NT * n + before + 2)
                out, q, k = ps[:, bank, 0:m * P], slice(qb * P, (qb + 1) * P), slice(kt0 * P, (kt0 + m) * P)
                M(out, ab.q1[s][:, q], ab.k1[s][:, k], start=True, stop=False)
                mm = M(out, ab.q2[s][:, q], ab.k2[s][:, k], start=False, stop=not here)
                for c, (t, which) in enumerate(here.items()):
                    mm = M(ps[:, bank, t * P:(t + 1) * P], ident_b[:, :], masks[:, which, :], start=False,
                           stop=c == len(here) - 1)
                mm.then_inc(s_sc, 1)

            def transpose_maxima(j, i, part):
                n = j * n_seg + i
                pe.wait_ge(s_mx, NT * n + 4 * part + 5)
                if part == 0:
                    pe.wait_ge(s_v, n + 1)
                else:
                    pe.wait_ge(s_row, 2 * n + 2)
                    pe.wait_ge(s_mul, 2 * n + 3)
                for t in range(4):
                    qb = 4 - 4 * part + t
                    mm = nc.tensor.transpose(spare[0:1, t * P:(t + 1) * P], ab.mx[:, qb:qb + 1], ident[:, :])
                mm.then_inc(s_mt, 1)

            def scores(j, i, u):
                n, s = j * n_seg + i, i % 2
                part, kt, q0, nq, here, _, _ = units[i][u]
                if u in (0, FIRST):
                    pe.wait_ge(s_row, 2 * n + 2 + part)
                pe.wait_ge(s_exp, n * NU + u + 1)
                out = st_bank(u)
                k = slice(kt * P, (kt + 1) * P)
                q = slice((1 - part) * HALF + q0 * P, (1 - part) * HALF + (q0 + nq) * P)
                M(out[:, 0:nq * P], ab.k1[s][:, k], ab.q1[s][:, q], start=True, stop=False)
                mm = M(out[:, 0:nq * P], ab.k2[s][:, k], ab.q2[s][:, q], start=False, stop=not here)
                for c, (t, which) in enumerate(here.items()):
                    mm = M(out[:, t * P:(t + 1) * P], masks[:, which, :], ident_b[:, :], start=False,
                           stop=c == len(here) - 1)
                mm.then_inc(s_st, 1)

            def product(j, i, u):
                n, s = j * n_seg + i, i % 2
                part, kt, q0, nq, _, first, last = units[i][u]
                if u == 0:
                    pe.wait_ge(s_v, n + 1)
                if first:
                    pe.wait_ge(s_osb, 2 * n + part + 1)
                    pe.wait_ge(s_rec, 2 * n + part + 1)
                pe.wait_ge(s_exp, n * NU + u + 4)
                M(o_bank(part)[0:HD + 1, q0 * P:(q0 + nq) * P], ab.v[:, s, kt, :], ab.pt[:, u % 3, 0:nq * P],
                  start=first, stop=last, skip_group_check=True).then_inc(s_pv, 1)

            def turn_sums(j, i, part):
                pe.wait_ge(s_osb, 2 * (j * n_seg + i) + part + 3)
                for t in range(4):
                    mm = M(o_bank(part)[:, t:t + 1], ab.o_sb[HD:HD + 1, part, t * P:(t + 1) * P],
                           ab.one[HD:HD + 1, 0:1], start=True, stop=True)
                mm.then_inc(s_sum, 1)

            def spread(j, i, part, more):
                n = j * n_seg + i
                pe.wait_ge(s_w, 2 * n + part + 1)
                if part == 0 and more:
                    pe.wait_ge(s_row, 2 * n + 4)
                elif part == 0:
                    pe.wait_ge(s_mul, 2 * n + 4)
                elif more:
                    pe.wait_ge(s_row, 2 * n + 5)
                else:
                    pe.wait_ge(s_mul, 2 * n + 5)
                M(spare[0:HD, :], ab.one[:, :], ab.diag[:, part].rearrange("p a n -> p (a n)"), start=True,
                  stop=True).then_inc(s_bc, 1)

            def step(j, i, nxt, prev):
                for x in range(NU + 2):
                    if x < NU:
                        scores(j, i, x)
                    if prev and x == 1:
                        turn_sums(*prev, 1)
                    if x == 2:
                        transpose_maxima(j, i, 1)
                    if prev and x == 4:
                        spread(*prev, 1, True)
                    if x >= 2:
                        product(j, i, x - 2)
                    if nxt and x == 6:
                        transpose_values(*nxt)
                    if nxt:
                        for a in CHUNKS_AT.get(x, ()):
                            row_scores(*nxt, a)
                    if nxt and x == 11:
                        transpose_maxima(*nxt, 0)
                    if x == 11:
                        turn_sums(j, i, 0)
                    if x == 13:
                        spread(j, i, 0, nxt)

            transpose_values(0, 0)
            for a in range(NU):
                row_scores(0, 0, a)
            transpose_maxima(0, 0, 0)
            loop(pe, step)
            turn_sums(n_iter - 1, n_seg - 1, 1)
            spread(n_iter - 1, n_seg - 1, 1, False)


def fox_decay(nc, mem, tag, proj, tile, bias_dram, c_dram):
    H = 16
    buf = [mem.at(f"{tag}_b{i}", [H, T], 4 * KB * i) for i in range(5)]
    z, e, u, lf, c = buf
    ones = mem.at(f"{tag}_ones", [H, T], 24 * KB)
    parts = [mem.at(f"{tag}_part{i}", [H, T], (30 + 4 * i) * KB, F32R) for i in range(4)]
    b_f = mem.at(f"{tag}_bf", [H, 1], 28 * KB)
    s_in = mem.sem(f"{tag}_bias_loaded")
    s_dve = mem.sem(f"{tag}_dve_chain")
    s_act = mem.sem(f"{tag}_act_steps")
    s_out = mem.sem(f"{tag}_stored")
    with nc.Block() as block:
        @block.sync
        def _(sp):
            sp.dma_start(b_f[:, :], bias_dram).then_inc(s_in, 16)
            sp.wait_ge(s_dve, 12)
            for i in range(4):
                sp.dma_start(c_dram[i], parts[i][:, :].bitcast(F32)).then_inc(s_out, 16)
            sp.wait_ge(s_out, 64)

        @block.vector
        def _(dve):
            chain = Chain(dve, s_dve)
            V = nc.vector
            chain.link(V.memset(ones[:, :], 1.0))
            dve.wait_ge(s_in, 16)
            chain.link(V.tensor_scalar(z[:, :], proj[0:H, tile, :], b_f[:, 0:1], None, ALU.add))
            dve.wait_ge(s_act, 2)
            chain.link(V.tensor_scalar(u[:, :], e[:, :], 1.0, None, ALU.add))
            chain.link(V.scalar_tensor_tensor(out=e[:, :], in0=u[:, :], scalar=-1.0, in1=e[:, :],
                                              op0=ALU.add, op1=ALU.subtract))
            dve.wait_ge(s_act, 3)
            chain.link(V.tensor_tensor(lf[:, :], lf[:, :], e[:, :], ALU.subtract))
            chain.link(V.tensor_scalar(z[:, :], z[:, :], 0.0, None, ALU.min))
            chain.link(V.tensor_tensor(lf[:, :], z[:, :], lf[:, :], ALU.subtract))
            chain.link(V.tensor_tensor_scan(c[:, :], ones[:, :], lf[:, :], 0.0, ALU.mult, ALU.add))
            hi, lo, neg_hi, neg_lo = (part[:, :] for part in parts)
            chain.link(V.tensor_copy(hi, c[:, :]))
            chain.link(V.tensor_tensor(lo, c[:, :], hi.bitcast(F32), ALU.subtract))
            chain.link(V.tensor_scalar(neg_hi, hi.bitcast(F32), -1.0, None, ALU.mult))
            chain.link(V.tensor_scalar(neg_lo, lo.bitcast(F32), -1.0, None, ALU.mult))

        @block.scalar
        def _(act):
            act.wait_ge(s_dve, 2)
            nc.scalar.activation(e[:, :], z[:, :], ACT.Abs).then_inc(s_act, 1)
            act.wait_ge(s_act, 1)
            nc.scalar.activation(e[:, :], e[:, :], ACT.Exp, scale=-1.0).then_inc(s_act, 1)
            act.wait_ge(s_dve, 3)
            nc.scalar.activation(lf[:, :], u[:, :], ACT.Ln).then_inc(s_act, 1)


def fox_attention(nc, mem, tag, proj, c_dram, one_dram, consts, att):
    ident = consts[0]
    ab = AttentionBuffers(nc, mem, tag, 0)
    own_row = [0, HD]
    fixed = []
    for s in range(2):
        a = HD - own_row[s]
        fixed += [(ab.k2[s][a:a + 3, :], one_dram), (ab.q2[s][a + 3:a + 5, :], one_dram[0:2])]
    attention_setup(nc, mem, f"{tag}_setup", ab, fixed)

    def rows(eng, j, i, sem):
        a, head = HD - own_row[i], bass.ds(2 * j + i, 1)
        eng.dma_start(ab.q2[i][a + 1:a + 3, :], c_dram[0:2, head, :].rearrange("p h t -> p (h t)"))\
            .then_inc(sem, 16)
        eng.dma_start(ab.k2[i][a + 3:a + 5, :], c_dram[2:4, head, :].rearrange("p h t -> p (h t)"))\
            .then_inc(sem, 16)

    def own(i):
        return slice(own_row[i], own_row[i] + HD)

    def act(eng, j, i, sem):
        nc.scalar.activation(ab.v_in[own(i), :], proj[own(i), 16 + j, :], ACT.Copy).then_inc(sem, 1)

    def transposes(i, bank):
        for t in range(NT):
            tr = nc.tensor.matmul(bank[:, t * HD:(t + 1) * HD], ab.v_in[own(i), t * P:(t + 1) * P],
                                  ident[own(i), own(i)], start=True, stop=True)
        return tr

    def values_out(j, i, bank):
        return nc.scalar.activation(ab.v[:, i, :, 0:HD], bank.rearrange("p (t d) -> p t d", d=HD), ACT.Copy)

    def finish(dve, j, i, part, o, weights, s_fin, s_mul):
        nc.vector.tensor_tensor(att[own(i), j, (1 - part) * HALF:(2 - part) * HALF], o, weights, ALU.mult)\
            .then_inc(s_mul, 1)

    hooks = dict(q=lambda j, i: proj[own(i), j, :], scale=HD ** -0.5, k=lambda j, i: proj[own(i), 8 + j, :],
                 rows=rows, row_step=2, gate=lambda *a: None, pool=lambda *a: None, pool_step=1, act=act,
                 act_step=4, transposes=transposes, values_out=values_out, finish=finish)
    attention(nc, mem, tag, KT, 2, ab, [score_units(False)] * 2, [row_chunks(False)] * 2, own_row, hooks, consts)


NB = 63
NH = 8
SB = 16
TOPN = 8
FORCE = 1e30
GELU_C = 0.044715
GELU_S = 0.7978845608028654


def gelu_steps(nc, chain, act_step, x, t):
    V = nc.vector
    chain.link(V.tensor_tensor(t, x, x, ALU.mult))
    chain.link(V.tensor_scalar(t, t, GELU_C, 1.0, ALU.mult, ALU.add))
    chain.link(V.tensor_tensor(t, t, x, ALU.mult))
    act_step()
    chain.link(V.scalar_tensor_tensor(out=t, in0=t, scalar=1.0, in1=x, op0=ALU.add, op1=ALU.mult))
    chain.link(V.tensor_scalar(x, t, 0.5, None, ALU.mult))


class NsaBuffers:

    def __init__(self, mem):
        self.keys = [mem.at(f"nsa_keys{b}", [HD, 2, T], (124 + 8 * b) * KB) for b in range(2)]
        self.values = mem.at("nsa_values", [P, 2, NT, 2 * HD], 140 * KB)
        self.o_cmp = mem.at("nsa_o_cmp", [P, NT, NH, HD], 148 * KB)
        self.sel_t = mem.at("nsa_sel_t", [HD + SB, 2, T], 164 * KB)
        self.gates = mem.at("nsa_gates", [P, NT, 3 * NH], 205 * KB + 512)
        self.q_cmp = mem.at("nsa_q_cmp", [HD + 2, NH, T], 30 * KB)
        self.k_cmp = mem.at("nsa_k_cmp", [HD + 2, 2, HD], 62 * KB)
        self.v_cmp = mem.at("nsa_v_cmp", [P, 2, P], 62 * KB + 512)


def nsa_prepare(nc, mem, tag, proj, d, consts, nb):
    ident, ident_b, _ = consts
    w1 = [mem.at(f"{tag}_w1_{kv}", [P, 16, P], 8 * kv * KB) for kv in range(2)]
    pairs = [mem.at(f"{tag}_pairs{kv}", [P, 2, T], (188 + 8 * kv) * KB) for kv in range(2)]
    w2 = mem.at(f"{tag}_w2", [P, 2, HD], 16 * KB)
    pos = mem.at(f"{tag}_pos", [P, 2, 16], 17 * KB)
    bias = mem.at(f"{tag}_bias", [P, 2], 18 * KB)
    hid = mem.at(f"{tag}_hid", [P, 2, 2, HD], 19 * KB)
    tmp = mem.at(f"{tag}_tmp", [P, 2, 2, HD], 20 * KB)
    ps = mem.psum
    s_w1 = mem.sem(f"{tag}_w1_loaded")
    s_w2 = mem.sem(f"{tag}_small_loaded")
    s_aug = mem.sem(f"{tag}_rows_loaded")
    s_gt = mem.sem(f"{tag}_gates_transposed")
    s_vt = mem.sem(f"{tag}_values_transposed")
    s_hid = mem.sem(f"{tag}_hidden_summed")
    s_bias = mem.sem(f"{tag}_bias_summed")
    s_dve = mem.sem(f"{tag}_dve_chain")
    s_pre = mem.sem(f"{tag}_tanh_arg")
    s_tanh = mem.sem(f"{tag}_tanh_ready")
    s_hr = mem.sem(f"{tag}_hidden_ready")
    s_kv = mem.sem(f"{tag}_compressed")
    s_z = mem.sem(f"{tag}_zeroed")
    s_a = mem.sem(f"{tag}_act_steps")
    s_g = mem.sem(f"{tag}_pool_steps")
    s_pair = mem.sem(f"{tag}_pairs_ready")

    with nc.Block() as block:
        @block.sync
        def _(sp):
            for kv in range(2):
                sp.dma_start(w1[kv][:, :, :], d["nsa_w1"][kv]).then_inc(s_w1, 16)
            sp.dma_start(w2[:, :, :], d["nsa_w2"]).then_inc(s_w2, 16)
            sp.dma_start(pos[:, :, :], d["nsa_pos"]).then_inc(s_w2, 16)
            sp.dma_start(nb.k_cmp[HD:HD + 2, :, :], d["nsa_cmp_rows"]).then_inc(s_aug, 16)
            sp.dma_start(nb.q_cmp[HD:HD + 2, :, :], d["nsa_query_rows"]).then_inc(s_aug, 16)
            sp.wait_ge(s_aug, 32)

        @block.gpsimd
        def _(pool):
            nc.gpsimd.memset(nb.k_cmp[0:HD, :, :], 0.0).then_inc(s_z, 1)
            nc.gpsimd.memset(nb.v_cmp[:, :, :], 0.0).then_inc(s_z, 1)
            for b in range(2):
                nc.gpsimd.tensor_copy(nb.keys[b][0:HD, 0, :], proj[0:HD, 10 + 2 * b, :]).then_inc(s_g, 1)
            pool.wait_ge(s_g, 2)

        @block.scalar
        def _(act):
            for g in range(2):
                rows = slice(g * HD, (g + 1) * HD)
                nc.scalar.activation(pairs[1][0:HD, g, :], proj[rows, 9, :], ACT.Copy).then_inc(s_pair, 1)
                nc.scalar.activation(pairs[1][HD:P, g, 0:T - 1], proj[rows, 9, 1:T], ACT.Copy).then_inc(s_pair, 1)
            act.wait_ge(s_gt, 1)
            nc.scalar.activation(nb.gates[:, :, :], ps[:, 0, 0:3 * NH * NT].rearrange("p (a b) -> p a b", a=NT),
                                 ACT.Sigmoid).then_inc(s_a, 1)
            for b in range(2):
                act.wait_ge(s_vt, b + 1)
                nc.scalar.activation(nb.values[:, b], ps[:, 1 + 2 * b:3 + 2 * b, :].rearrange(
                    "p a (b n) -> p (a b) n", n=P), ACT.Copy).then_inc(s_a, 1)
            for h in range(NH):
                row = (h % 2) * HD
                nc.scalar.activation(nb.q_cmp[0:HD, h, :], proj[row:row + HD, 4 + h // 2, :], ACT.Copy,
                                     scale=HD ** -0.5).then_inc(s_a, 1)
            act.wait_ge(s_pre, 1)
            nc.scalar.activation(tmp[:, :, :, 0:NB], tmp[:, :, :, 0:NB], ACT.Tanh, scale=GELU_S)\
                .then_inc(s_tanh, 1)
            act.wait_ge(s_a, 3 + NH)

        @block.vector
        def _(dve):
            V = nc.vector
            chain = Chain(dve, s_dve)
            for g in range(2):
                rows = slice(g * HD, (g + 1) * HD)
                V.tensor_copy(pairs[0][0:HD, g, :], proj[rows, 8, :]).then_inc(s_pair, 1)
                V.tensor_copy(pairs[0][HD:P, g, 0:T - 1], proj[rows, 8, 1:T]).then_inc(s_pair, 1)
            for b in range(2):
                V.tensor_copy(nb.keys[b][0:HD, 1, :], proj[HD:P, 10 + 2 * b, :]).then_inc(s_dve, 1)
                chain.n += 1
            dve.wait_ge(s_bias, 1)
            chain.link(V.tensor_copy(bias[:, :], ps[:, 6, 0:2]))
            dve.wait_ge(s_hid, 1)
            for kv in range(2):
                chain.link(V.tensor_scalar(hid[:, kv, :, 0:NB], ps[:, 5, kv * P:kv * P + 2 * NB].rearrange(
                    "p (g n) -> p g n", g=2), bias[:, kv:kv + 1], None, ALU.add))

            def tanh():
                dve.sem_inc(s_pre, 1)
                dve.wait_ge(s_tanh, 1)

            gelu_steps(nc, chain, tanh, hid[:, :, :, 0:NB], tmp[:, :, :, 0:NB])
            dve.sem_inc(s_hr, 1)
            dve.wait_ge(s_kv, 1)
            dve.wait_ge(s_z, 2)
            chain.link(V.tensor_copy(nb.k_cmp[0:HD, :, 0:NB], ps[0:HD, 6, P:2 * P].rearrange(
                "p (a n) -> p a n", a=2)[:, :, 0:NB]))
            for hh in range(2):
                chain.link(V.tensor_copy(nb.v_cmp[hh * HD:hh * HD + NB, :, hh * HD:(hh + 1) * HD],
                                         ps[0:NB, 0, 256:256 + 2 * HD].rearrange("p (a n) -> p a n", a=2)))

        @block.tensor
        def _(pe):
            for t in range(NT):
                tr = nc.tensor.transpose(ps[:, 0, t * 3 * NH:(t + 1) * 3 * NH],
                                         proj[0:3 * NH, 14, t * P:(t + 1) * P], ident[0:3 * NH, 0:3 * NH])
            tr.then_inc(s_gt, 1)
            for b in range(2):
                for t in range(NT):
                    tr = nc.tensor.transpose(ps[:, 1 + 2 * b + t // 4, (t % 4) * P:(t % 4 + 1) * P],
                                             proj[:, 11 + 2 * b, t * P:(t + 1) * P], ident[:, :])
                tr.then_inc(s_vt, 1)
            pe.wait_ge(s_w1, 32)
            pe.wait_ge(s_w2, 32)
            for kv in range(2):
                for r in range(16):
                    mm = nc.tensor.matmul(ps[:, 6, kv:kv + 1], w1[kv][:, r, :], pos[:, kv, r:r + 1],
                                          start=r == 0, stop=r == 15)
            mm.then_inc(s_bias, 1)
            pe.wait_ge(s_pair, 8)
            for kv in range(2):
                for r in range(16):
                    mm = nc.tensor.matmul(ps[:, 5, kv * P:kv * P + 2 * NB], w1[kv][:, r, :],
                                          pairs[kv][:, :, 2 * r:2 * r + 16 * (NB - 1) + 1:16],
                                          start=r == 0, stop=r == 15)
            mm.then_inc(s_hid, 1)
            pe.wait_ge(s_hr, 1)
            pe.wait_ge(s_a, 1)
            for g in range(2):
                nc.tensor.matmul(ps[0:HD, 6, P + g * HD:P + g * HD + NB], w2[:, 0, :], hid[:, 0, g, 0:NB],
                                 start=True, stop=True)
            for g in range(2):
                mm = nc.tensor.matmul(ps[0:NB, 0, 256 + g * HD:256 + (g + 1) * HD], hid[:, 1, g, 0:NB],
                                      w2[:, 1, :], start=True, stop=True)
            mm.then_inc(s_kv, 1)


def nsa_compressed(nc, mem, tag, d, consts, nb):
    ident, ident_b, _ = consts
    maskw = mem.at(f"{tag}_maskw", [P, NT, HD], 0)
    keep = mem.at(f"{tag}_keep", [P, NT, HD], 2 * KB)
    maskb = mem.at(f"{tag}_maskb", [P, NT, HD], 4 * KB, BF16)
    selm = mem.at(f"{tag}_selm", [P, 2, NT, SB], 5 * KB)
    lower = mem.at(f"{tag}_lower", [P, SB, SB], 6 * KB)
    over = mem.at(f"{tag}_overlap", [P, SB], 7 * KB)
    e = mem.at(f"{tag}_e", [P, 2, NH, HD], 8 * KB)
    p_t = mem.at(f"{tag}_pt", [P, 2, 4, P], 12 * KB)
    gt = mem.at(f"{tag}_gt", [P, 2, SB, SB], 16 * KB)
    eq = mem.at(f"{tag}_eq", [P, 2, SB, SB], 18 * KB)
    imp = mem.at(f"{tag}_imp", [P, 2, SB], 20 * KB)
    rank = mem.at(f"{tag}_rank", [P, 2, SB], 20 * KB + 128)
    selb = mem.at(f"{tag}_selb", [P, 2, SB], 20 * KB + 256)
    mx = mem.at(f"{tag}_mx", [P, NH], 20 * KB + 384)
    sm = mem.at(f"{tag}_sm", [P, NH], 20 * KB + 416)
    ps = mem.psum
    s_in = mem.sem(f"{tag}_constants_loaded")
    s_dve = mem.sem(f"{tag}_dve_chain")
    s_mask = mem.sem(f"{tag}_mask_ready")
    s_sc = mem.sem(f"{tag}_scores_ready")
    s_sub = mem.sem(f"{tag}_shifted")
    s_exp = mem.sem(f"{tag}_exp_ready")
    s_pr = mem.sem(f"{tag}_probs_ready")
    s_tr = mem.sem(f"{tag}_transposed")
    s_pt = mem.sem(f"{tag}_transposes_out")
    s_imp = mem.sem(f"{tag}_importance_ready")
    s_o = mem.sem(f"{tag}_products_ready")
    s_sb = mem.sem(f"{tag}_choice_ready")
    s_st = mem.sem(f"{tag}_choice_transposed")
    s_end = mem.sem(f"{tag}_block_done")

    with nc.Block() as block:
        @block.sync
        def _(sp):
            for dst, name in ((maskw, "cmp_mask"), (keep, "cmp_keep"), (selm, "sel_mul_add"),
                              (lower, "lower"), (over, "overlap")):
                src = d[name]
                sp.dma_start(dst[:], src).then_inc(s_in, 16)

        @block.scalar
        def _(act):
            def exponentials(q):
                act.wait_ge(s_sub, q + 1)
                nc.scalar.activation(e[:, q % 2], e[:, q % 2], ACT.Exp).then_inc(s_exp, 1)

            exponentials(0)
            for q in range(NT):
                b = q % 2
                act.wait_ge(s_tr, q + 1)
                nc.scalar.activation(p_t[:, b], ps[:, 2 + b, :].rearrange("p (a n) -> p a n", a=4),
                                     ACT.Copy).then_inc(s_pt, 1)
                if q + 1 < NT:
                    exponentials(q + 1)

        @block.vector
        def _(dve):
            V = nc.vector
            chain = Chain(dve, s_dve)
            dve.wait_ge(s_in, 80)
            V.tensor_copy(maskb[:, :, :], maskw[:, :, :]).then_inc(s_mask, 1)

            def shift(q):
                scores = ps[:, q % 2, :].rearrange("p (h n) -> p h n", h=NH)
                dve.wait_ge(s_sc, q + 1)
                chain.link(V.tensor_reduce(mx[:, :], scores, AX.X, ALU.max))
                V.tensor_tensor(e[:, q % 2], scores, mx[:, :].unsqueeze(2).broadcast_to([P, NH, HD]),
                                ALU.subtract).then_inc(s_sub, 1)

            def probabilities(q):
                b = q % 2
                dve.wait_ge(s_exp, q + 1)
                chain.link(V.tensor_reduce(sm[:, :], e[:, b], AX.X, ALU.add))
                chain.link(V.reciprocal(sm[:, :], sm[:, :]))
                chain.link(V.tensor_tensor(e[:, b], e[:, b], sm[:, :].unsqueeze(2).broadcast_to([P, NH, HD]),
                                           ALU.mult))
                V.tensor_tensor(e[:, b], e[:, b], keep[:, q, :].unsqueeze(1).broadcast_to([P, NH, HD]),
                                ALU.mult).then_inc(s_pr, 1)

            shift(0)
            probabilities(0)
            for q in range(NT):
                b = q % 2
                if q + 1 < NT:
                    shift(q + 1)
                dve.wait_ge(s_imp, q + 1)
                chain.link(V.tensor_tensor(
                    imp[:, :, :], ps[:, 6 + b, 0:2 * SB].rearrange("p (g s) -> p g s", g=2),
                    selm[:, 0, q, :].unsqueeze(1).broadcast_to([P, 2, SB]), ALU.mult))
                chain.link(V.tensor_tensor(imp[:, :, :], imp[:, :, :],
                                           selm[:, 1, q, :].unsqueeze(1).broadcast_to([P, 2, SB]), ALU.add))
                for g in range(2):
                    other = imp[:, g, :].unsqueeze(1).broadcast_to([P, SB, SB])
                    own = imp[:, g, :].unsqueeze(2).broadcast_to([P, SB, SB])
                    V.tensor_tensor(gt[:, g], other, own, ALU.is_gt).then_inc(s_dve, 1)
                    V.tensor_tensor(eq[:, g], other, own, ALU.is_equal).then_inc(s_dve, 1)
                    chain.n += 2
                dve.wait_ge(s_dve, chain.n)
                chain.link(V.tensor_tensor(eq[:, :, :, :], eq[:, :, :, :],
                                           lower[:, :, :].unsqueeze(1).broadcast_to([P, 2, SB, SB]), ALU.mult))
                chain.link(V.tensor_tensor(gt[:, :, :, :], gt[:, :, :, :], eq[:, :, :, :], ALU.add))
                chain.link(V.tensor_reduce(rank[:, :, :], gt[:, :, :, :], AX.X, ALU.add))
                V.tensor_scalar(selb[:, :, :], rank[:, :, :], float(TOPN), NEG, ALU.is_ge, ALU.mult)\
                    .then_inc(s_sb, 1)
                if q + 1 < NT:
                    probabilities(q + 1)
                dve.wait_ge(s_o, q + 1)
                V.tensor_tensor(nb.o_cmp[:, q], ps[:, 4 + b, :].rearrange("p (h n) -> p h n", h=NH),
                                nb.gates[:, q, 0:3 * NH:3].unsqueeze(2).broadcast_to([P, NH, HD]),
                                ALU.mult).then_inc(s_dve, 1)
                chain.n += 1
                dve.wait_ge(s_st, q + 1)
                V.tensor_copy(nb.sel_t[HD:HD + SB, :, q * P:(q + 1) * P],
                              ps[0:SB, 6 + b, P:3 * P].rearrange("p (g n) -> p g n", g=2)).then_inc(s_end, 1)

        @block.tensor
        def _(pe):
            def scores(q):
                b = q % 2
                bank = ps[:, b, :].rearrange("p (h n) -> p h n", h=NH)
                if q >= 2:
                    pe.wait_ge(s_sub, q - 1)
                nc.tensor.matmul(bank, ident_b[:, :], maskb[:, q, :].unsqueeze(1).broadcast_to([P, NH, HD]),
                                 start=True, stop=True)
                for h in range(NH):
                    mm = nc.tensor.matmul(bank[:, h, :], nb.q_cmp[:, h, q * P:(q + 1) * P],
                                          nb.k_cmp[:, h // 4, :], start=False, stop=True,
                                          skip_group_check=True)
                mm.then_inc(s_sc, 1)

            pe.wait_ge(s_mask, 1)
            scores(0)
            scores(1)
            for q in range(NT):
                b = q % 2
                pe.wait_ge(s_pr, q + 1)
                if q >= 2:
                    pe.wait_ge(s_pt, q - 1)
                for k in range(4):
                    tr = nc.tensor.transpose(ps[:, 2 + b, k * P:(k + 1) * P],
                                             e[:, b, 2 * k:2 * k + 2, :].rearrange("p h n -> p (h n)"),
                                             ident[:, :])
                tr.then_inc(s_tr, 1)
                pe.wait_ge(s_pt, q + 1)
                if q >= 2:
                    pe.wait_ge(s_end, q - 1)
                for k in range(4):
                    mm = nc.tensor.matmul(ps[:, 6 + b, (k // 2) * SB:(k // 2 + 1) * SB], p_t[:, b, k, :],
                                          over[:, :], start=k % 2 == 0, stop=k % 2 == 1)
                mm.then_inc(s_imp, 1)
                for k in range(4):
                    mm = nc.tensor.matmul(ps[:, 4 + b, k * P:(k + 1) * P], p_t[:, b, k, :], nb.v_cmp[:, k // 2, :],
                                          start=True, stop=True)
                mm.then_inc(s_o, 1)
                if q + 2 < NT:
                    scores(q + 2)
                pe.wait_ge(s_sb, q + 1)
                for g in range(2):
                    tr = nc.tensor.transpose(ps[0:SB, 6 + b, (1 + g) * P:(2 + g) * P], selb[:, g, :],
                                             ident[:, :])
                tr.then_inc(s_st, 1)


def nsa_attention(nc, mem, tag, d, consts, nb, att):
    ident = consts[0]
    ab = AttentionBuffers(nc, mem, tag, 64 * KB)
    cmp_t = mem.at(f"{tag}_cmp_t", [HD, 2, T], 0)
    acc = mem.at(f"{tag}_acc", [HD, T], 8 * KB)
    sum_ = mem.at(f"{tag}_sum", [HD, HALF], 12 * KB)
    o_in = mem.at(f"{tag}_o_in", [P, 4, HD], 14 * KB)
    s_gate = mem.sem(f"{tag}_gated")
    a = HD
    fixed = [(ab.k2[b][a:a + 3, :], d["nsa_key_rows"]) for b in range(2)]
    fixed += [(ab.k2[0][a + 32:a + 32 + SB, :], d["nsa_block_rows"])]
    attention_setup(nc, mem, f"{tag}_setup", ab, fixed)

    def rows(eng, j, i, sem):
        eng.dma_start(ab.q2[i % 2][a + 1:a + 3, :], d["nsa_query_rows"][:, bass.ds(2 * j + i // 2, 1), :]
                      .rearrange("r h t -> r (h t)")).then_inc(sem, 16)

    def pool(eng, j, i, sem):
        nc.gpsimd.tensor_copy(ab.v[:, i % 2, :, 0:HD], nb.values[:, i % 2, :, bass.ds((j // 2) * HD, HD)])\
            .then_inc(sem, 1)

    def act(eng, j, i, sem):
        b = i % 2
        nc.scalar.activation(o_in[:, :, :], nb.o_cmp[:, 4 * b:4 * b + 4, 2 * j + i // 2, :], ACT.Copy)\
            .then_inc(sem, 1)
        if b == 0:
            nc.scalar.activation(ab.q2[0][a + 32:a + 32 + SB, :], nb.sel_t[HD:HD + SB, j // 2, :], ACT.Copy)\
                .then_inc(sem, 1)
        else:
            eng.sem_inc(sem, 1)

    def transposes(i, bank):
        for t in range(4):
            tr = nc.tensor.matmul(bank[0:HD, t * P:(t + 1) * P], o_in[:, t, :], ident[:, :], start=True,
                                  stop=True)
        return tr

    def values_out(j, i, bank):
        half = i % 2
        return nc.scalar.activation(cmp_t[:, i // 2, half * HALF:(half + 1) * HALF], bank[0:HD, :], ACT.Copy)

    def gate(dve, j, i, part, w, s_fin):
        g = nb.gates[:, 4 - 4 * part:8 - 4 * part, 6 * j + 3 * (i // 2) + 1 + i % 2]
        nc.vector.tensor_tensor(w, w, g, ALU.mult).then_inc(s_gate, 1)
        dve.wait_ge(s_gate, 8 * j + 2 * i + part + 1)

    def finish(dve, j, i, part, o, weights, s_fin, s_mul):
        cols = slice((1 - part) * HALF, (2 - part) * HALF)
        TT = nc.vector.tensor_tensor
        if i % 2 == 0:
            TT(acc[:, cols], o, weights, ALU.mult).then_inc(s_mul, 1)
            return
        step = 8 * j + 4 * (i // 2) + 2 * part
        TT(sum_[:, :], o, weights, ALU.mult).then_inc(s_fin, 1)
        dve.wait_ge(s_fin, step + 1)
        dve.wait_ge(s_mul, 8 * j + 2 * i + part + 3)
        TT(sum_[:, :], sum_[:, :], acc[:, cols], ALU.add).then_inc(s_fin, 1)
        dve.wait_ge(s_fin, step + 2)
        row = (i // 2) * HD
        TT(att[row:row + HD, 4 + j, cols], sum_[:, :], cmp_t[:, i // 2, cols], ALU.add).then_inc(s_mul, 1)

    hooks = dict(q=lambda j, i: nb.q_cmp[0:HD, 2 * j + i // 2, :], scale=1.0,
                 k=lambda j, i: nb.keys[i % 2][:, j // 2, :], rows=rows, row_step=1, gate=gate, pool=pool,
                 pool_step=2, act=act, act_step=5, transposes=transposes, values_out=values_out, finish=finish)
    attention(nc, mem, tag, NH // 2, 4, ab, [score_units(False), score_units(True)] * 2,
              [row_chunks(False), row_chunks(True)] * 2, [0] * 4, hooks, consts)


def shape_constants(np):
    q = np.arange(P)
    t = np.arange(T, dtype=np.float32)
    masks = np.stack([np.where(q[None] <= q[:, None], 0, NEG), np.where(q[None] > q[:, None], 0, NEG)], 1)
    slopes = np.float32(2.0) ** (-8.0 * np.arange(1, NH + 1, dtype=np.float32) / NH)
    query_rows = np.stack([-slopes[:, None] * t[None], np.repeat(slopes[:, None], T, 1)])
    one = np.ones((3, T))
    block = np.arange(T)[None] // HD == np.arange(SB)[:, None]
    key_rows = np.stack([one[0], one[0], t])
    end = np.arange(NB) * 16 + 31
    cmp_rows = np.zeros((2, 2, HD))
    cmp_rows[0, :, 0:NB] = 1
    cmp_rows[1, :, 0:NB] = end
    tok = (np.arange(NT)[None, :] * P + q[:, None])[:, :, None]
    keep = np.zeros((P, NT, HD))
    keep[:, :, 0:NB] = end[None, None] <= tok
    blk = np.arange(SB)[None, None]
    cur = tok // HD
    forced = (blk == 0) | (blk == cur) | (blk == cur - 1)
    valid = blk * HD <= tok
    sel_mul = (~forced & valid)
    sel_add = np.where(forced, FORCE, np.where(valid, 0, NEG))
    lower = np.broadcast_to(q[None, None, 0:SB] < q[None, 0:SB, None], (P, SB, SB))
    c0, s0 = (np.arange(NB) * 16)[:, None], (np.arange(SB) * HD)[None]
    ov = np.zeros((2, HD, SB))
    ov[:, 0:NB] = np.clip(np.minimum(c0 + 32, s0 + HD) - np.maximum(c0, s0), 0, None) / 32
    out = dict(ident=np.eye(P), masks=masks, nsa_query_rows=query_rows, one=one, nsa_key_rows=key_rows, nsa_block_rows=block,
               nsa_cmp_rows=cmp_rows, cmp_mask=np.where(keep > 0, 0, NEG), cmp_keep=keep,
               sel_mul_add=np.stack([sel_mul, sel_add], 1), lower=lower, overlap=ov.reshape(P, SB))
    return {k: np.ascontiguousarray(v, dtype=np.float32) for k, v in out.items()}


CL = 4
NCH = T // CL
NP = 16
CH = 32
INV_2PI = 0.15915494309189535
PI2_HI, PI2_MID, PI2_LO = 6.28125, 1.93500518798828125e-3, 3.0199159819567e-7
ROUND = 12582912.0
PI_F = 3.1415925
HALF_PI = 1.5707963267948966


class S5Buffers:
    def __init__(self, mem):
        self.rot = mem.at("s5_rot", [P, 2, NP, NCH], 0)
        self.ca = mem.at("s5_ca", [P, 2, NP, CL + 1, CH], 32 * KB)
        self.m4 = mem.at("s5_m4", [P, NP], 52 * KB)
        self.wb = mem.at("s5_wb", [P, 2, NP, P], 124 * KB)
        self.wt = mem.at("s5_wt", [P, NP, P], 140 * KB)
        self.u = mem.at("s5_u", [P, NP, NCH], 164 * KB + 256)


def s5_weights(nc, mem, tag, proj, d, consts, sb):
    ident = consts[0]
    small = mem.at(f"{tag}_small", [P, 30, NP], 52 * KB + 64)
    names = iter(range(30))

    def reg():
        i = next(names)
        return small[:, i, :]

    lr, li, step, mag, th, r0, r1, cos, sin, a_re, a_im, den, nr, z_re, z_im, t0, t1, t2 = (
        reg() for _ in range(18))
    w_re, w_im = [reg(), reg()], [reg(), reg()]
    braw = mem.at(f"{tag}_braw", [P, 2, NP, CH], 56 * KB)
    tmp = mem.at(f"{tag}_tmp", [P, 2, NP, CH], 60 * KB)
    ba = mem.at(f"{tag}_ba", [P, 2, NP, CL, CH], 148 * KB)
    u_sh = mem.at(f"{tag}_ush", [P, 4, CL, NCH], 181 * KB)
    ptmp = mem.at(f"{tag}_ptmp", [P, 8, NCH // 2], 197 * KB)
    ps = mem.psum
    s_par = mem.sem(f"{tag}_parameters_loaded")
    s_b = mem.sem(f"{tag}_bc_loaded")
    s_v = mem.sem(f"{tag}_dve_chain")
    s_a = mem.sem(f"{tag}_act_steps")
    s_ph = mem.sem(f"{tag}_angles_ready")
    s_w = mem.sem(f"{tag}_rotation_ready")
    s_g = mem.sem(f"{tag}_pool_chain")
    s_sh = mem.sem(f"{tag}_u_reordered")
    s_u = mem.sem(f"{tag}_u_laid_out")
    s_ba = mem.sem(f"{tag}_ba_ready")
    s_ca = mem.sem(f"{tag}_ca_ready")
    s_tb = mem.sem(f"{tag}_b_transposed")
    s_wb = mem.sem(f"{tag}_wb_out")
    s_tt = mem.sem(f"{tag}_toeplitz_summed")
    s_wt = mem.sem(f"{tag}_wt_out")
    s_z = mem.sem(f"{tag}_wt_cleared")

    def rotations(E, chain, h, scratch):
        pr = slice(8 * h, 8 * h + 8)
        rr, ri = sb.rot[:, 0, pr, :], sb.rot[:, 1, pr, :]
        n, cur = 1, 0
        while n < NCH:
            wr = w_re[cur][:, pr].unsqueeze(2).broadcast_to([P, 8, n])
            wi = w_im[cur][:, pr].unsqueeze(2).broadcast_to([P, 8, n])
            old_r, old_i, new_r, new_i = rr[:, :, 0:n], ri[:, :, 0:n], rr[:, :, n:2 * n], ri[:, :, n:2 * n]
            t = scratch[:, :, 0:n]
            chain.link(E.tensor_tensor(new_r, old_r, wr, ALU.mult))
            chain.link(E.tensor_tensor(t, old_i, wi, ALU.mult))
            chain.link(E.tensor_tensor(new_r, new_r, t, ALU.subtract))
            chain.link(E.tensor_tensor(new_i, old_r, wi, ALU.mult))
            chain.link(E.tensor_tensor(t, old_i, wr, ALU.mult))
            chain.link(E.tensor_tensor(new_i, new_i, t, ALU.add))
            n *= 2
            c_re, c_im, n_re, n_im = (w[k][:, pr] for k in (cur, 1 - cur) for w in (w_re, w_im))
            t = scratch[:, :, 0]
            chain.link(E.tensor_tensor(n_re, c_re, c_re, ALU.mult))
            chain.link(E.tensor_tensor(t, c_im, c_im, ALU.mult))
            chain.link(E.tensor_tensor(n_re, n_re, t, ALU.subtract))
            chain.link(E.tensor_tensor(n_im, c_re, c_im, ALU.mult))
            chain.link(E.tensor_tensor(n_im, n_im, n_im, ALU.add))
            cur = 1 - cur

    with nc.Block() as block:
        @block.sync
        def _(sp):
            sp.dma_start(lr, d["s5_lr"]).then_inc(s_par, 16)
            sp.dma_start(li, d["s5_li"]).then_inc(s_par, 16)
            for g in range(2):
                sp.dma_start(step[g * HD:(g + 1) * HD, :], d["s5_ls"][g].partition_broadcast(HD))\
                    .then_inc(s_par, 16)
            sp.dma_start(braw[:, 0], d["s5_b"][0]).then_inc(s_b, 16)
            sp.dma_start(braw[:, 1], d["s5_b"][1]).then_inc(s_b, 16)
            for ri in range(2):
                sp.dma_start(sb.ca[:, ri, :, 0, :], d["s5_c"][ri]).then_inc(s_b, 16)
            sp.wait_ge(s_sh, 4)
            for i in range(CL):
                for q in range(4):
                    sp.dma_start(sb.u[i * CH:(i + 1) * CH, q:NP:4, :],
                                 u_sh[q * CH:(q + 1) * CH, :, i, :]).then_inc(s_u, 16)
            sp.wait_ge(s_u, 16 * CL * 4)

        @block.scalar
        def _(act):
            act.wait_ge(s_par, 64)
            A = nc.scalar.activation

            def one(out, in_, func, **kw):
                A(out, in_, func, **kw).then_inc(s_a, 1)

            one(step, step, ACT.Exp)
            act.wait_ge(s_v, 1)
            one(mag, t0, ACT.Exp)
            act.wait_ge(s_ph, 1)
            one(sin, r0, ACT.Sin)
            one(cos, r1, ACT.Sin)
            for o in range(4):
                nc.scalar.activation(u_sh[:, o], proj[:, o, :].rearrange("p (c i) -> p i c", i=CL), ACT.Copy)\
                    .then_inc(s_sh, 1)
            for n in range(8):
                act.wait_ge(s_tb, n + 1)
                nc.scalar.activation(sb.wb[:, n // 4, 4 * (n % 4):4 * (n % 4) + 4, :],
                                     ps[:, n % 4, :].rearrange("p (a n) -> p a n", a=4), ACT.Copy)\
                    .then_inc(s_wb, 1)
            act.wait_ge(s_z, 1)
            for b in range(4):
                act.wait_ge(s_tt, b + 1)
                for i in range(CL):
                    rows = slice(i * CH, (i + 1) * CH)
                    nc.scalar.activation(sb.wt[rows, 4 * b:4 * b + 4, i * CH:P],
                                         ps[rows, 4 + b, :].rearrange("p (a n) -> p a n", a=4)[:, :, i * CH:P],
                                         ACT.Copy).then_inc(s_wt, 1)
            act.wait_ge(s_wt, 16)

        @block.gpsimd
        def _(pool):
            G = nc.gpsimd
            chain = Chain(pool, s_g)
            G.memset(sb.wt[:, :, :], 0.0).then_inc(s_z, 1)
            rr, ri = sb.rot[:, 0], sb.rot[:, 1]
            chain.link(G.memset(rr[:, :, 0:1], 1.0))
            chain.link(G.memset(ri[:, :, 0:1], 0.0))
            pool.wait_ge(s_w, 1)
            rotations(G, chain, 0, ptmp[:, :, :])

        @block.vector
        def _(dve):
            V = nc.vector
            chain = Chain(dve, s_v)
            TT, TS = V.tensor_tensor, V.tensor_scalar
            dve.wait_ge(s_par, 64)
            dve.wait_ge(s_a, 1)
            chain.link(TT(t0, lr, step, ALU.mult))
            chain.link(TT(th, li, step, ALU.mult))
            chain.link(TS(t1, th, INV_2PI, ROUND, ALU.mult, ALU.add))
            chain.link(TS(t1, t1, -ROUND, None, ALU.add))
            chain.link(V.scalar_tensor_tensor(out=r0, in0=t1, scalar=-PI2_HI, in1=th, op0=ALU.mult, op1=ALU.add))
            chain.link(V.scalar_tensor_tensor(out=r0, in0=t1, scalar=-PI2_MID, in1=r0, op0=ALU.mult, op1=ALU.add))
            chain.link(V.scalar_tensor_tensor(out=r0, in0=t1, scalar=-PI2_LO, in1=r0, op0=ALU.mult, op1=ALU.add))
            chain.link(TS(r0, r0, PI_F, -PI_F, ALU.min, ALU.max))
            chain.link(TS(r1, r0, -1.0, None, ALU.mult))
            chain.link(TT(r1, r1, r0, ALU.max))
            TS(r1, r1, -1.0, HALF_PI, ALU.mult, ALU.add).then_inc(s_ph, 1)
            dve.wait_ge(s_a, 4)
            chain.link(TT(a_re, mag, cos, ALU.mult))
            chain.link(TT(a_im, mag, sin, ALU.mult))
            chain.link(TT(t0, cos, cos, ALU.mult))
            chain.link(TT(t1, sin, sin, ALU.mult))
            chain.link(TT(t2, cos, sin, ALU.mult))
            chain.link(TT(t0, t0, t1, ALU.subtract))
            chain.link(TT(t2, t2, t2, ALU.add))
            chain.link(TT(t1, t2, t2, ALU.mult))
            chain.link(TT(w_re[0], t0, t0, ALU.mult))
            chain.link(TT(w_re[0], w_re[0], t1, ALU.subtract))
            chain.link(TT(w_im[0], t0, t2, ALU.mult))
            TT(w_im[0], w_im[0], w_im[0], ALU.add).then_inc(s_w, 1)
            chain.link(TT(t0, mag, mag, ALU.mult))
            chain.link(TT(sb.m4[:, :], t0, t0, ALU.mult))
            chain.link(TT(den, lr, lr, ALU.mult))
            chain.link(TT(t0, li, li, ALU.mult))
            chain.link(TT(den, den, t0, ALU.add))
            chain.link(V.reciprocal(den, den))
            chain.link(TS(nr, a_re, -1.0, None, ALU.add))
            chain.link(TT(t0, nr, lr, ALU.mult))
            chain.link(TT(t1, a_im, li, ALU.mult))
            chain.link(TT(t0, t0, t1, ALU.add))
            chain.link(TT(z_re, t0, den, ALU.mult))
            chain.link(TT(t0, a_im, lr, ALU.mult))
            chain.link(TT(t1, nr, li, ALU.mult))
            chain.link(TT(t0, t0, t1, ALU.subtract))
            chain.link(TT(z_im, t0, den, ALU.mult))

            def wide(x):
                return x.unsqueeze(2).broadcast_to([P, NP, CH])

            def times(out_r, out_i, in_r, in_i, m_r, m_i, sign):
                chain.link(TT(tmp[:, 0], in_i, wide(m_i), ALU.mult))
                chain.link(TT(tmp[:, 1], in_r, wide(m_i), ALU.mult))
                chain.link(TT(out_r, in_r, wide(m_r), ALU.mult))
                chain.link(TT(out_i, in_i, wide(m_r), ALU.mult))
                chain.link(TT(out_r, out_r, tmp[:, 0], ALU.subtract if sign > 0 else ALU.add))
                chain.link(TT(out_i, out_i, tmp[:, 1], ALU.add if sign > 0 else ALU.subtract))

            dve.wait_ge(s_b, 64)
            times(ba[:, 0, :, CL - 1], ba[:, 1, :, CL - 1], braw[:, 0], braw[:, 1], z_re, z_im, 1)
            for i in range(CL - 2, -1, -1):
                times(ba[:, 0, :, i], ba[:, 1, :, i], ba[:, 0, :, i + 1], ba[:, 1, :, i + 1], a_re, a_im, 1)
            dve.sem_inc(s_ba, 1)
            chain.link(TS(sb.ca[:, 1, :, 0, :], sb.ca[:, 1, :, 0, :], -1.0, None, ALU.mult))
            for j in range(1, CL + 1):
                times(sb.ca[:, 0, :, j], sb.ca[:, 1, :, j], sb.ca[:, 0, :, j - 1], sb.ca[:, 1, :, j - 1],
                      a_re, a_im, -1)
            dve.sem_inc(s_ca, 1)
            dve.wait_ge(s_g, 2)
            rotations(V, chain, 1, tmp[:, :, :, :].rearrange("p a b c -> p (a b c)").rearrange(
                "p (a n) -> p a n", a=8))

        @block.tensor
        def _(pe):
            pe.wait_ge(s_ba, 1)
            for n in range(8):
                if n >= 4:
                    pe.wait_ge(s_wb, n - 3)
                for k in range(4):
                    tr = nc.tensor.transpose(ps[:, n % 4, k * P:(k + 1) * P],
                                             ba[:, n // 4, 4 * (n % 4) + k].rearrange("p i c -> p (i c)"),
                                             ident[:, :])
                tr.then_inc(s_tb, 1)
            pe.wait_ge(s_ca, 1)
            for b in range(4):
                for k in range(4):
                    pair = 4 * b + k
                    for i in range(CL):
                        for ri in range(2):
                            mm = nc.tensor.matmul(
                                ps[i * CH:(i + 1) * CH, 4 + b, k * P + i * CH:(k + 1) * P],
                                ba[:, ri, pair, CL - 1, :],
                                sb.ca[:, ri, pair, 0:CL - i, :].rearrange("p j c -> p (j c)"),
                                start=ri == 0, stop=ri == 1)
                mm.then_inc(s_tt, 1)


def s5_run(nc, mem, tag, proj, d, consts, sb, att):
    v = mem.at(f"{tag}_v", [P, 2, 4, NCH + 1], 181 * KB)
    tmp = mem.at(f"{tag}_tmp", [P, 2, 4, NCH], 56 * KB)
    mb = mem.at(f"{tag}_mb", [P, 4, NCH + 1], 190 * KB)
    ysb = mem.at(f"{tag}_ysb", [P, 2, 4, NCH], 195 * KB)
    yt = mem.at(f"{tag}_yt", [P, 4, CL, NCH], 148 * KB)
    gl = mem.at(f"{tag}_gelu_tmp", [P, 4, T], 0)
    wg = mem.at(f"{tag}_wg", [P, 4, 512], 16 * KB)
    sg = mem.at(f"{tag}_sg", [P, 4, T], 24 * KB)
    dd = mem.at(f"{tag}_d", [P, 4], 52 * KB + 2560)
    ps = mem.psum
    s_in = mem.sem(f"{tag}_weights_loaded")
    s_v = mem.sem(f"{tag}_dve_chain")
    s_s = mem.sem(f"{tag}_inputs_summed")
    s_rd = mem.sem(f"{tag}_inputs_read")
    s_h = mem.sem(f"{tag}_states_ready")
    s_y = mem.sem(f"{tag}_outputs_summed")
    s_ys = mem.sem(f"{tag}_outputs_out")
    s_yt = [mem.sem(f"{tag}_outputs_laid_out{b}") for b in range(4)]
    s_pre = mem.sem(f"{tag}_tanh_arg")
    s_th = mem.sem(f"{tag}_tanh_ready")
    s_ge = mem.sem(f"{tag}_gelu_ready")
    s_z = mem.sem(f"{tag}_gate_summed")
    s_sg = mem.sem(f"{tag}_gate_ready")

    with nc.Block() as block:
        @block.sync
        def _(sp):
            sp.dma_start(dd[:, :], d["s5_d"]).then_inc(s_in, 16)
            for b in range(4):
                sp.wait_ge(s_ys, b + 1)
                for i in range(CL):
                    for q in range(4):
                        sp.dma_start(yt[q * CH:(q + 1) * CH, b, i, :],
                                     ysb[i * CH:(i + 1) * CH, b % 2, q, :]).then_inc(s_yt[b], 16)
            sp.wait_ge(s_h, 4)
            sp.dma_start(wg[:, :, :], d["s5_wg"]).then_inc(s_in, 16)

        @block.scalar
        def _(act):
            for b in range(4):
                act.wait_ge(s_y, b + 1)
                if b >= 2:
                    act.wait_ge(s_yt[b - 2], 16 * 16)
                nc.scalar.activation(ysb[:, b % 2], ps[:, 4 + 2 * (b % 2):6 + 2 * (b % 2), :].rearrange(
                    "p a (b n) -> p (a b) n", b=2), ACT.Copy).then_inc(s_ys, 1)
            act.wait_ge(s_pre, 1)
            nc.scalar.activation(gl[:, :, :], gl[:, :, :], ACT.Tanh, scale=GELU_S).then_inc(s_th, 1)
            for f in range(4):
                act.wait_ge(s_z, f + 1)
                nc.scalar.activation(sg[:, f, :], ps[:, 2 * f:2 * f + 2, :].rearrange("p a n -> p (a n)"),
                                     ACT.Sigmoid).then_inc(s_sg, 1)

        @block.vector
        def _(dve):
            V = nc.vector
            chain = Chain(dve, s_v)
            TT = V.tensor_tensor
            chain.link(V.memset(v[:, :, :, 0:1], 0.0))
            for b in range(4):
                prs = slice(4 * b, 4 * b + 4)
                rr, ri = sb.rot[:, 0, prs, :], sb.rot[:, 1, prs, :]
                s_re = ps[:, 0:2, :].rearrange("p a (b n) -> p (a b) n", b=2)
                s_im = ps[:, 2:4, :].rearrange("p a (b n) -> p (a b) n", b=2)
                v_re, v_im = v[:, 0, :, 1:NCH + 1], v[:, 1, :, 1:NCH + 1]
                chain.link(V.tensor_copy(mb[:, :, :], sb.m4[:, prs].unsqueeze(2).broadcast_to([P, 4, NCH + 1])))
                chain.link(V.memset(mb[:, :, 0:1], 0.0))
                dve.wait_ge(s_s, b + 1)
                if b:
                    dve.wait_ge(s_y, b)
                chain.link(TT(tmp[:, 0], s_im, ri, ALU.mult))
                chain.link(TT(tmp[:, 1], s_re, ri, ALU.mult))
                chain.link(TT(v_re, s_re, rr, ALU.mult))
                TT(v_im, s_im, rr, ALU.mult).then_inc(s_rd, 1)
                dve.wait_ge(s_rd, b + 1)
                chain.link(TT(v_re, v_re, tmp[:, 0], ALU.add))
                chain.link(TT(v_im, v_im, tmp[:, 1], ALU.subtract))
                for part in range(2):
                    flat = v[:, part].rearrange("p a n -> p (a n)")
                    chain.link(V.tensor_tensor_scan(flat, mb[:, :, :].rearrange("p a n -> p (a n)"), flat,
                                                    0.0, ALU.mult, ALU.add))
                chain.link(TT(tmp[:, 0], v_im, ri, ALU.mult))
                chain.link(TT(tmp[:, 1], v_re, ri, ALU.mult))
                chain.link(TT(v_re, v_re, rr, ALU.mult))
                chain.link(TT(v_im, v_im, rr, ALU.mult))
                chain.link(TT(v_re, v_re, tmp[:, 0], ALU.subtract))
                TT(v_im, v_im, tmp[:, 1], ALU.add).then_inc(s_h, 1)
            dve.wait_ge(s_in, 16)
            for b in range(4):
                dve.wait_ge(s_yt[b], 16 * 16)
                V.scalar_tensor_tensor(out=yt[:, b], in0=proj[:, b, :].rearrange("p (c i) -> p i c", i=CL),
                                       scalar=dd[:, b:b + 1], in1=yt[:, b], op0=ALU.mult, op1=ALU.add)\
                    .then_inc(s_v, 1)
                chain.n += 1
            dve.wait_ge(s_v, chain.n)

            def tanh():
                dve.sem_inc(s_pre, 1)
                dve.wait_ge(s_th, 1)

            dve.wait_ge(s_h, 4)
            gelu_steps(nc, chain, tanh, yt[:, :, :, :].rearrange("p a i c -> p a (i c)"), gl[:, :, :])
            dve.sem_inc(s_ge, 1)
            for f in range(4):
                dve.wait_ge(s_sg, f + 1)
                TT(att[:, f, :].rearrange("p (c i) -> p i c", i=CL), yt[:, f],
                   sg[:, f, :].rearrange("p (i c) -> p i c", i=CL), ALU.mult).then_inc(s_v, 1)
                chain.n += 1
            dve.wait_ge(s_v, chain.n)

        @block.tensor
        def _(pe):
            def inputs(b):
                if b:
                    pe.wait_ge(s_rd, b)
                for part in range(2):
                    for k in range(4):
                        mm = nc.tensor.matmul(ps[:, 2 * part + k // 2, (k % 2) * NCH:(k % 2 + 1) * NCH],
                                              sb.wb[:, part, 4 * b + k, :], sb.u[:, 4 * b + k, :],
                                              start=True, stop=True)
                mm.then_inc(s_s, 1)

            inputs(0)
            for b in range(4):
                if b + 1 < 4:
                    inputs(b + 1)
                pe.wait_ge(s_h, b + 1)
                if b >= 2:
                    pe.wait_ge(s_ys, b - 1)
                for k in range(4):
                    out = ps[:, 4 + 2 * (b % 2) + k // 2, (k % 2) * NCH:(k % 2 + 1) * NCH]
                    pair = 4 * b + k
                    nc.tensor.matmul(out, sb.wt[:, pair, :], sb.u[:, pair, :], start=True, stop=False)
                    for part in range(2):
                        mm = nc.tensor.matmul(out, sb.ca[:, part, pair, 1:CL + 1, :].rearrange(
                            "p j c -> p (j c)"), v[:, part, k, 0:NCH], start=False, stop=part == 1)
                mm.then_inc(s_y, 1)
            pe.wait_ge(s_in, 32)
            pe.wait_ge(s_ge, 1)
            pe.wait_ge(s_ys, 4)
            for f in range(4):
                for h in range(2):
                    for k in range(4):
                        mm = nc.tensor.matmul(ps[:, 2 * f + h, :], wg[:, k, f * P:(f + 1) * P],
                                              yt[:, k, 2 * h:2 * h + 2, :].rearrange("p i c -> p (i c)"),
                                              start=k == 0, stop=k == 3)
                mm.then_inc(s_z, 1)


def trunk(nc, d, out):
    with ExitStack() as ctx:
        mem = Mem(nc, ctx)
        consts = load_constants(nc, mem, d["ident"], d["masks"])
        ident = consts[0]
        x_hi = mem.at("x_hi", [P, KT, T], 0, F32R)
        x_lo = mem.at("x_lo", [P, KT, T], 32 * KB, F32R)
        att = mem.at("att", [P, KT, T], 172 * KB)
        hidden = mem.at("hidden", [P, FT, T], 64 * KB)
        kept = [nc.dram_tensor(f"x_kept{i}", (T, D), F32, kind="Internal").ap() for i in range(3)]
        c_kept = nc.dram_tensor("fox_c", (4, 16, T), F32, kind="Internal").ap()
        load_x(nc, mem, "load", d["x_t"], x_hi, x_lo)

        proj = mem.at("proj0", [P, 15, T], 64 * KB)
        project(nc, mem, "in0", x_hi, x_lo, d["l0_w_in"], 15, proj, 164 * KB)
        sb = S5Buffers(mem)
        s5_weights(nc, mem, "s5w", proj, d, consts, sb)
        s5_run(nc, mem, "s5r", proj, d, consts, sb, att)
        nb = NsaBuffers(mem)
        nsa_prepare(nc, mem, "nsap", proj, d, consts, nb)
        nsa_compressed(nc, mem, "nsac", d, consts, nb)
        nsa_attention(nc, mem, "nsaa", d, consts, nb, att)
        project_norm(nc, mem, "out0", att, KT, d["l0_w_out"], d["x"], d["l0_ln1"], ident, kept[0], x_hi, x_lo,
                     64 * KB, False)
        gate_up(nc, mem, "gu0", x_hi, x_lo, d["l0_gate_up"], hidden, 152 * KB)
        project_norm(nc, mem, "dn0", hidden, FT, d["l0_w_down"], kept[0], d["l0_ln2"], ident, kept[1], x_hi,
                     x_lo, 152 * KB, False)

        mem.recycle_semaphores()
        proj = mem.at("proj1", [P, 25, T], 64 * KB)
        project(nc, mem, "in1", x_hi, x_lo, d["l1_w_in"], 25, proj, 164 * KB)
        fox_decay(nc, mem, "foxd", proj, 24, d["l1_b_f"], c_kept)
        fox_attention(nc, mem, "foxa", proj, c_kept, d["one"], consts, att)
        project_norm(nc, mem, "out1", att, KT, d["l1_w_out"], kept[1], d["l1_ln1"], ident, kept[2], x_hi, x_lo,
                     64 * KB, False)
        gate_up(nc, mem, "gu1", x_hi, x_lo, d["l1_gate_up"], hidden, 152 * KB)
        project_norm(nc, mem, "dn1", hidden, FT, d["l1_w_down"], kept[2], d["l1_ln2"], ident, out, x_hi, x_lo,
                     152 * KB, True)


def layouts(np, i):
    def tiles(w):
        return np.ascontiguousarray(w.reshape(KT, P, w.shape[1] // P, P).transpose(2, 1, 0, 3))

    def to_full_tile(w):
        n = w.shape[1] % P
        return np.concatenate([w, w[:, 0:P - n]], 1)

    def pairs(a):
        return np.ascontiguousarray(a.reshape(NP, 2, HD).transpose(1, 2, 0).reshape(P, NP))

    def block(a):
        o = np.zeros((2, HD, NP, 2, CH // 2), np.float32)
        a = a.reshape(NP, 2, HD, CH // 2)
        for g in range(2):
            o[g, :, :, g, :] = a[:, g].transpose(1, 0, 2)
        return o.reshape(P, NP, CH)

    x = i["x"][0]
    w1 = np.stack([i["l0_nsa_phi_k1"], i["l0_nsa_phi_v1"]]).reshape(2, 16, P, P).transpose(0, 2, 1, 3)
    pos = np.stack([i["l0_nsa_pos_k"], i["l0_nsa_pos_v"]]).reshape(2, 16, P).transpose(2, 0, 1)
    out = dict(
        x=x, x_t=x.T.reshape(KT, P, T).transpose(1, 0, 2),
        l0_w_in=tiles(to_full_tile(i["l0_w_in"])), l1_w_in=tiles(to_full_tile(i["l1_w_in"])),
        l1_b_f=i["l1_fox_b_f"].reshape(16, 1),
        nsa_w1=w1, nsa_w2=np.stack([i["l0_nsa_phi_k2"], i["l0_nsa_phi_v2"]], 1),
        nsa_pos=pos,
        s5_lr=pairs(i["l0_s5_lambda_re"]), s5_li=pairs(i["l0_s5_lambda_im"]),
        s5_ls=i["l0_s5_log_step"].reshape(NP, 2).T,
        s5_b=np.stack([block(i["l0_s5_b_re"]), block(i["l0_s5_b_im"])]),
        s5_c=np.stack([block(i["l0_s5_c_re"].transpose(0, 2, 1)), block(i["l0_s5_c_im"].transpose(0, 2, 1))]),
        s5_d=i["l0_s5_d"].reshape(4, P).T, s5_wg=i["l0_s5_w_glu"].reshape(4, P, 512).transpose(1, 0, 2))
    for n in range(DEPTH):
        out[f"l{n}_w_out"] = i[f"l{n}_w_out"].reshape(KT, P, D)
        out[f"l{n}_gate_up"] = np.stack([tiles(i[f"l{n}_ffn_w_gate"]), tiles(i[f"l{n}_ffn_w_up"])], 1)
        out[f"l{n}_w_down"] = i[f"l{n}_ffn_w_down"].reshape(FT, P, D)
        for k in (1, 2):
            out[f"l{n}_ln{k}"] = np.stack([i[f"l{n}_ln{k}_g"], i[f"l{n}_ln{k}_b"]])
    return {k: np.ascontiguousarray(v) for k, v in {**shape_constants(np), **out}.items()}


def kernel(**inputs):
    import numpy as np
    import concourse.bacc as bacc
    from concourse.bass_utils import run_bass_kernel_spmd as run

    arrays = layouts(np, {k: np.asarray(v) for k, v in inputs.items()})
    nc = bacc.Bacc("TRN2", target_bir_lowering=False, num_devices=1)
    d = {k: nc.dram_tensor(f"in_{k}", v.shape, F32, kind="ExternalInput").ap() for k, v in arrays.items()}
    out = nc.dram_tensor("out_x", (T, D), F32, kind="ExternalOutput").ap()
    trunk(nc, d, out)
    r = run(nc, [{f"in_{k}": v for k, v in arrays.items()}], core_ids=[0])
    return r.results[0]["out_x"].reshape(1, T, D)
```
